# Optimizing a Trainium2 kernel written in Bass

```python
import math
import jax, jax.numpy as jnp
from jax import lax
import numpy as np

D_MODEL = 1024
BATCH = 1
SEQ = 1024
DEPTH = 1

CHUNK = 64
Q_BLOCK = 128
EPS = 1e-6
N_HEADS = 8
QK_NOPE = 64
QK_ROPE = 32
QK_HEAD = QK_NOPE + QK_ROPE
V_HEAD = 64
Q_LORA = 256
KV_LORA = 128
ROPE_THETA = 10000.0
ATTN_WIDTH = N_HEADS * V_HEAD
SSM_WIDTH = 256
SSM_GROUP = 16
SSM_GROUPS = SSM_WIDTH // SSM_GROUP
SSM_STATE = 64
DT_MIN = 1e-3
DT_MAX = 1e-1
CONV_WIDTH = 256
CONV_K = 31
MIX_WIDTH = ATTN_WIDTH + SSM_WIDTH + CONV_WIDTH
IN_SIZES = [Q_LORA, KV_LORA, QK_ROPE, SSM_WIDTH, CONV_WIDTH, CONV_WIDTH]
IN_PROJ = sum(IN_SIZES)
IN_SPLITS = [int(v) for v in np.cumsum(IN_SIZES)[:-1]]
N_EGROUPS = 4
EXP_PER_GROUP = 8
N_EXPERTS = N_EGROUPS * EXP_PER_GROUP
TOP_K = 2
D_FF_E = 512
MOE_BLOCK = 128

kernel_name = "hybrid_mla_s5_conformer_hmoe"

def rms_norm(x, w, eps=EPS):
    xf = x.astype(jnp.float32)
    y = xf * lax.rsqrt(jnp.mean(xf * xf, -1, keepdims=True) + eps)
    return (y * w.astype(jnp.float32)).astype(x.dtype)

def layer_norm(x, w, b, eps=1e-5):
    xf = x.astype(jnp.float32)
    mu = jnp.mean(xf, -1, keepdims=True)
    var = jnp.mean(jnp.square(xf - mu), -1, keepdims=True)
    y = (xf - mu) * lax.rsqrt(var + eps) * w.astype(jnp.float32) + b.astype(jnp.float32)
    return y.astype(x.dtype)

def rotary(x, cos, sin):
    x1, x2 = jnp.split(x, 2, axis=-1)
    return jnp.concatenate([x1 * cos - x2 * sin, x1 * sin + x2 * cos], axis=-1)

def mla_mixer(c_q, c_kv, k_pe, cos, sin, q_a_norm, w_uq, kv_a_norm, w_ukv, q_norm, k_norm):
    B, L, _ = c_q.shape
    q = (rms_norm(c_q, q_a_norm) @ w_uq).reshape(B, L, N_HEADS, QK_HEAD)
    kv = (rms_norm(c_kv, kv_a_norm) @ w_ukv).reshape(B, L, N_HEADS, QK_NOPE + V_HEAD)
    k_nope, v = kv[..., :QK_NOPE], kv[..., QK_NOPE:]
    k = jnp.concatenate([k_nope, jnp.broadcast_to(k_pe[:, :, None, :], (B, L, N_HEADS, QK_ROPE))], -1)
    q = rms_norm(q, q_norm)
    k = rms_norm(k, k_norm)
    cos = cos.astype(q.dtype)
    sin = sin.astype(q.dtype)
    q = jnp.concatenate([q[..., :QK_NOPE], rotary(q[..., QK_NOPE:], cos, sin)], -1)
    k = jnp.concatenate([k[..., :QK_NOPE], rotary(k[..., QK_NOPE:], cos, sin)], -1)
    q = q.transpose(0, 2, 1, 3)
    k = k.transpose(0, 2, 1, 3)
    v = v.transpose(0, 2, 1, 3)
    scale = QK_HEAD ** -0.5
    chunk_id = jnp.arange(L) // CHUNK
    neg = jnp.finfo(jnp.float32).min
    outs = []
    for i in range(L // Q_BLOCK):
        q0 = i * Q_BLOCK
        kv_len = q0 + Q_BLOCK
        s = jnp.einsum('bhqd,bhkd->bhqk', q[:, :, q0:kv_len], k[:, :, :kv_len]).astype(jnp.float32) * scale
        mask = chunk_id[None, :kv_len] <= chunk_id[q0:kv_len, None]
        s = jnp.where(mask, s, neg)
        p = jax.nn.softmax(s, axis=-1).astype(v.dtype)
        outs.append(jnp.einsum('bhqk,bhkd->bqhd', p, v[:, :, :kv_len]))
    o = jnp.concatenate(outs, axis=1)
    return o.reshape(B, L, ATTN_WIDTH)

def s5_mixer(u, lam_re, lam_im, b_re, b_im, c_re, c_im, d_skip, log_dt, w_glu):
    B, L, _ = u.shape
    f32 = jnp.float32
    lam = lax.complex(lam_re.astype(f32), lam_im.astype(f32))
    dt = jnp.exp(log_dt.astype(f32))[:, None]
    lam_bar = jnp.exp(lam * dt)
    b_mat = lax.complex(b_re.astype(f32), b_im.astype(f32))
    b_bar = ((lam_bar - 1.0) / lam)[..., None] * b_mat
    c_mat = lax.complex(c_re.astype(f32), c_im.astype(f32))
    ug = u.astype(f32).reshape(B, L, SSM_GROUPS, SSM_GROUP)
    bu = jnp.einsum('blgc,gpc->blgp', ug.astype(jnp.complex64), b_bar)
    a = jnp.broadcast_to(lam_bar, bu.shape)

    def combine(e1, e2):
        a1, b1 = e1
        a2, b2 = e2
        return a1 * a2, a2 * b1 + b2

    _, xs = lax.associative_scan(combine, (a, bu), axis=1)
    y = jnp.einsum('blgp,gcp->blgc', xs, c_mat).real + d_skip.astype(f32) * ug
    y = y.reshape(B, L, SSM_WIDTH)
    z = jax.nn.gelu(y)
    out = z * jax.nn.sigmoid(z @ w_glu.astype(f32))
    return out.astype(u.dtype)

def conv_mixer(a, g, dw_w, dw_b, ln_w, ln_b):
    u = a * jax.nn.sigmoid(g)
    u = jnp.pad(u, ((0, 0), (CONV_K - 1, 0), (0, 0)))
    y = lax.conv_general_dilated(u, dw_w[:, None, :].astype(u.dtype), window_strides=(1,),
                                 padding='VALID', dimension_numbers=('NWC', 'WIO', 'NWC'),
                                 feature_group_count=CONV_WIDTH)
    y = layer_norm(y + dw_b.astype(y.dtype), ln_w, ln_b)
    return jax.nn.silu(y)

def grouped_experts(xf, expert_id, gates, w1, w3, w2):
    N, D = xf.shape
    A = N * TOP_K
    flat_e = expert_id.reshape(A)
    flat_tok = jnp.repeat(jnp.arange(N, dtype=jnp.int32), TOP_K)
    flat_gate = gates.reshape(A)
    order = jnp.argsort(flat_e)
    e_sorted = flat_e[order]
    counts = jnp.bincount(flat_e, length=N_EXPERTS)
    padded = (counts + MOE_BLOCK - 1) // MOE_BLOCK * MOE_BLOCK
    pad_end = jnp.cumsum(padded)
    pad_start = pad_end - padded
    start = jnp.cumsum(counts) - counts
    dest = pad_start[e_sorted] + jnp.arange(A, dtype=jnp.int32) - start[e_sorted]
    n_rows = (A + MOE_BLOCK - 1) // MOE_BLOCK * MOE_BLOCK + N_EXPERTS * MOE_BLOCK
    n_blocks = n_rows // MOE_BLOCK
    row_tok = jnp.full((n_rows,), N, jnp.int32).at[dest].set(flat_tok[order])
    row_gate = jnp.zeros((n_rows,), flat_gate.dtype).at[dest].set(flat_gate[order])
    block_e = jnp.minimum(jnp.searchsorted(pad_end, jnp.arange(n_blocks, dtype=pad_end.dtype) * MOE_BLOCK,
                                           side='right'), N_EXPERTS - 1)
    x_pad = jnp.concatenate([xf, jnp.zeros((1, D), xf.dtype)], axis=0)
    x_rows = x_pad[row_tok].reshape(n_blocks, MOE_BLOCK, D)

    def expert_block(args):
        xb, e = args
        hb = jax.nn.silu(xb @ w1[e]) * (xb @ w3[e])
        return hb @ w2[e]

    y_rows = lax.map(expert_block, (x_rows, block_e)).reshape(n_rows, D)
    y_rows = y_rows * row_gate[:, None].astype(y_rows.dtype)
    return jax.ops.segment_sum(y_rows, row_tok, num_segments=N + 1)[:N]

def hier_moe(h, w_grp, b_grp, w_exp, b_exp, w1, w3, w2):
    B, L, D = h.shape
    xf = h.reshape(B * L, D)
    N = xf.shape[0]
    rows = jnp.arange(N)
    grp_logits = (xf @ w_grp).astype(jnp.float32) + b_grp.astype(jnp.float32)
    p_grp = jax.nn.softmax(grp_logits, axis=-1)
    g_sel = jnp.argmax(grp_logits, axis=-1)
    exp_logits = ((xf @ w_exp).astype(jnp.float32) + b_exp.astype(jnp.float32)).reshape(N, N_EGROUPS, EXP_PER_GROUP)
    p_in = jax.nn.softmax(exp_logits[rows, g_sel], axis=-1)
    top_p, top_i = lax.top_k(p_in, TOP_K)
    top_p = top_p / jnp.sum(top_p, axis=-1, keepdims=True)
    gates = p_grp[rows, g_sel][:, None] * top_p
    expert_id = (g_sel[:, None] * EXP_PER_GROUP + top_i).astype(jnp.int32)
    y = grouped_experts(xf, expert_id, gates, w1, w3, w2)
    return y.reshape(B, L, D)

def setup_inputs(seed: int = 0) -> dict:
    key = jax.random.key(seed)
    ks = iter(jax.random.split(key, 40))
    f32 = jnp.float32

    def nrm(shape, scale):
        return jax.random.normal(next(ks), shape, f32) * scale

    def gain(shape):
        return 1.0 + 0.01 * jax.random.normal(next(ks), shape, f32)

    Lr = DEPTH
    x = jax.random.normal(next(ks), (BATCH, SEQ, D_MODEL), f32)
    offsets = jax.random.randint(next(ks), (BATCH, 1), 0, 8192, jnp.int32)
    positions = offsets + jnp.arange(SEQ, dtype=jnp.int32)[None, :]
    n_idx = jnp.arange(SSM_STATE, dtype=f32)
    lam_re = -0.5 + 0.01 * jax.random.normal(next(ks), (Lr, SSM_GROUPS, SSM_STATE), f32)
    lam_im = math.pi * n_idx + 0.01 * jax.random.normal(next(ks), (Lr, SSM_GROUPS, SSM_STATE), f32)
    log_dt = jax.random.uniform(next(ks), (Lr, SSM_GROUPS), f32, math.log(DT_MIN), math.log(DT_MAX))
    return {
        "x": x,
        "positions": positions,
        "mix_norm": gain((Lr, D_MODEL)),
        "w_in": nrm((Lr, D_MODEL, IN_PROJ), D_MODEL ** -0.5),
        "q_a_norm": gain((Lr, Q_LORA)),
        "w_uq": nrm((Lr, Q_LORA, N_HEADS * QK_HEAD), Q_LORA ** -0.5),
        "kv_a_norm": gain((Lr, KV_LORA)),
        "w_ukv": nrm((Lr, KV_LORA, N_HEADS * (QK_NOPE + V_HEAD)), KV_LORA ** -0.5),
        "q_norm": gain((Lr, QK_HEAD)),
        "k_norm": gain((Lr, QK_HEAD)),
        "ssm_lam_re": lam_re,
        "ssm_lam_im": lam_im,
        "ssm_b_re": nrm((Lr, SSM_GROUPS, SSM_STATE, SSM_GROUP), (2 * SSM_GROUP) ** -0.5),
        "ssm_b_im": nrm((Lr, SSM_GROUPS, SSM_STATE, SSM_GROUP), (2 * SSM_GROUP) ** -0.5),
        "ssm_c_re": nrm((Lr, SSM_GROUPS, SSM_GROUP, SSM_STATE), (2 * SSM_STATE) ** -0.5),
        "ssm_c_im": nrm((Lr, SSM_GROUPS, SSM_GROUP, SSM_STATE), (2 * SSM_STATE) ** -0.5),
        "ssm_d": nrm((Lr, SSM_GROUPS, SSM_GROUP), 0.5),
        "ssm_log_dt": log_dt,
        "ssm_w_glu": nrm((Lr, SSM_WIDTH, SSM_WIDTH), SSM_WIDTH ** -0.5),
        "conv_dw_w": nrm((Lr, CONV_K, CONV_WIDTH), CONV_K ** -0.5),
        "conv_dw_b": nrm((Lr, CONV_WIDTH), 0.01),
        "conv_ln_w": gain((Lr, CONV_WIDTH)),
        "conv_ln_b": nrm((Lr, CONV_WIDTH), 0.01),
        "out_norm": gain((Lr, MIX_WIDTH)),
        "w_out": nrm((Lr, MIX_WIDTH, D_MODEL), MIX_WIDTH ** -0.5),
        "ffn_norm": gain((Lr, D_MODEL)),
        "w_grp": nrm((Lr, D_MODEL, N_EGROUPS), D_MODEL ** -0.5),
        "b_grp": nrm((Lr, N_EGROUPS), 0.01),
        "w_exp": nrm((Lr, D_MODEL, N_EXPERTS), D_MODEL ** -0.5),
        "b_exp": nrm((Lr, N_EXPERTS), 0.01),
        "w1": nrm((Lr, N_EXPERTS, D_MODEL, D_FF_E), D_MODEL ** -0.5),
        "w3": nrm((Lr, N_EXPERTS, D_MODEL, D_FF_E), D_MODEL ** -0.5),
        "w2": nrm((Lr, N_EXPERTS, D_FF_E, D_MODEL), D_FF_E ** -0.5),
    }

def reference(x, positions, mix_norm, w_in, q_a_norm, w_uq, kv_a_norm, w_ukv, q_norm, k_norm,
              ssm_lam_re, ssm_lam_im, ssm_b_re, ssm_b_im, ssm_c_re, ssm_c_im, ssm_d, ssm_log_dt, ssm_w_glu,
              conv_dw_w, conv_dw_b, conv_ln_w, conv_ln_b, out_norm, w_out,
              ffn_norm, w_grp, b_grp, w_exp, b_exp, w1, w3, w2):
    inv_freq = ROPE_THETA ** (-jnp.arange(0, QK_ROPE, 2, dtype=jnp.float32) / QK_ROPE)
    ang = positions.astype(jnp.float32)[..., None] * inv_freq
    cos = jnp.cos(ang)[:, :, None, :]
    sin = jnp.sin(ang)[:, :, None, :]
    for l in range(DEPTH):
        h = rms_norm(x, mix_norm[l])
        proj = h @ w_in[l]
        c_q, c_kv, k_pe, u_ssm, conv_a, conv_g = jnp.split(proj, IN_SPLITS, axis=-1)
        y_attn = mla_mixer(c_q, c_kv, k_pe, cos, sin, q_a_norm[l], w_uq[l], kv_a_norm[l], w_ukv[l],
                           q_norm[l], k_norm[l])
        y_ssm = s5_mixer(u_ssm, ssm_lam_re[l], ssm_lam_im[l], ssm_b_re[l], ssm_b_im[l], ssm_c_re[l],
                         ssm_c_im[l], ssm_d[l], ssm_log_dt[l], ssm_w_glu[l])
        y_conv = conv_mixer(conv_a, conv_g, conv_dw_w[l], conv_dw_b[l], conv_ln_w[l], conv_ln_b[l])
        g = out_norm[l]
        y = jnp.concatenate([
            rms_norm(y_attn, g[:ATTN_WIDTH]),
            rms_norm(y_ssm, g[ATTN_WIDTH:ATTN_WIDTH + SSM_WIDTH]),
            rms_norm(y_conv, g[ATTN_WIDTH + SSM_WIDTH:]),
        ], axis=-1)
        x = x + y @ w_out[l]
        x = x + hier_moe(rms_norm(x, ffn_norm[l]), w_grp[l], b_grp[l], w_exp[l], b_exp[l],
                         w1[l], w3[l], w2[l])
    return x


_drawn_inputs = setup_inputs


def setup_inputs(seed=0):
    import zlib

    import numpy as np

    out = dict(_drawn_inputs(seed))
    spreads = {}
    factors = {'mix_norm': 3.291,
     'q_a_norm': 4.456,
     'kv_a_norm': 3.151,
     'q_norm': 4.241,
     'k_norm': 5.335,
     'ssm_lam_re': 8.0,
     'conv_dw_b': 4.287,
     'conv_ln_w': 4.404,
     'conv_ln_b': 8.0,
     'out_norm': 3.437,
     'ffn_norm': 3.24,
     'b_grp': 5.56,
     'b_exp': 4.213}
    for name, (base, spread) in spreads.items():
        noise = np.random.default_rng([zlib.crc32(name.encode()), seed]).standard_normal(out[name].shape)
        drawn = base * np.exp(spread * noise) if base else spread * noise
        out[name] = __import__('jax').numpy.asarray(drawn.astype(out[name].dtype))
    for name, factor in factors.items():
        out[name] = (out[name] * factor).astype(out[name].dtype)
    return out
```

```python
from contextlib import ExitStack

import numpy as np

import concourse.bass as bass
from concourse import mybir

ALU = mybir.AluOpType
ACT = mybir.ActivationFunctionType
F32 = mybir.dt.float32
I32 = mybir.dt.int32
U32 = mybir.dt.uint32
AX = mybir.AxisListType.X

P = 128
EPS = 1e-6
LN_EPS = 1e-5
LINKS = 13
PI = float(np.pi)
TWO_PI_SAFE = 6.2831850
TWO_PI_HI = 6.28125
TWO_PI_LO = 2.0 * PI - TWO_PI_HI
ROUND = 1.5 * 2.0 ** 23
ROUND16 = 1.5 * 2.0 ** 7
NEG = -3.0e38
SKIP_ROW = 1 << 20


def build(nc, x, positions, mix_norm, w_in, q_a_norm, w_uq, kv_a_norm, w_ukv, q_norm, k_norm,
          lam_re, lam_im, b_re, b_im, c_re, c_im, d_skip, log_dt, w_glu,
          dw_w, dw_b, ln_w, ln_b, out_norm, w_out,
          ffn_norm, w_grp, b_grp, w_exp, b_exp, w1, w3, w2, out):
    T, D = x.shape[1], x.shape[2]
    NT, KC = T // P, D // P
    QL, KL = q_a_norm.shape[1], kv_a_norm.shape[1]
    QH = q_norm.shape[1]
    H = w_uq.shape[2] // QH
    RD, ND = QH - QH // 3 * 2, QH // 3 * 2
    HR = RD // 2
    VD = w_ukv.shape[2] // H - ND
    G, S = lam_re.shape[1], lam_re.shape[2]
    C = b_re.shape[3]
    SW, CW, TAPS = G * C, dw_w.shape[2], dw_w.shape[1]
    NPAIR = G // 2
    STEP = P // C
    NJ = T // STEP
    EG, NE = w_grp.shape[2], w_exp.shape[2]
    EPG = NE // EG
    FF = w1.shape[3]
    FC = FF // P
    OVF = 2 * T // P - 1
    NBLK = NE + OVF
    assert (T, D, NT, KC, QH, RD, ND, VD) == (1024, 1024, 8, 8, 96, 32, 64, 64)
    assert STEP == NT and NJ == P and SW == CW == 256 and S == 64 and 2 * C == 32
    CQ0, CKV0, KPE0, U0, A0, G0 = 0, QL, QL + KL, QL + KL + RD, QL + KL + RD + SW, QL + KL + RD + SW + CW
    NIN = G0 + CW
    SCALE = float(QH) ** -0.5
    AW = H * VD

    with ExitStack() as ctx:
        def sb(name, shape, dt=F32):
            return ctx.enter_context(nc.sbuf_tensor(name, shape, dt))[tuple(slice(0, n) for n in shape)]

        def sem(name):
            return ctx.enter_context(nc.semaphore(name))

        WORDS = 50300
        arena = sb("arena", [P, WORDS])

        def at(off, *dims, parts=P):
            n = int(np.prod(dims))
            assert off + n <= WORDS
            v = arena[0:parts, off:off + n]
            if len(dims) == 2:
                return v.rearrange("p (a b) -> p a b", b=dims[1])
            if len(dims) == 3:
                return v.rearrange("p (a b c) -> p a b c", b=dims[1], c=dims[2])
            if len(dims) == 4:
                return v.rearrange("p (a b c d) -> p a b c d", b=dims[1], c=dims[2], d=dims[3])
            return v

        hT = at(0, KC, NT, P)
        win = at(8192, KC, NIN)
        PADW = T + TAPS - 1
        upad = at(17664, 2, PADW)
        cqT = at(19772, 2, T)
        ckvT = at(21820, T)
        kpe = at(22844, NT, RD)
        S0 = 23100
        xin = at(S0, 2, D)
        wuq = at(S0 + 2048, 2, H * QH)
        wglu = at(S0 + 3584, 2, SW)
        utok = at(S0 + 4096, G, STEP, C)
        U = at(S0 + 6144, G, NJ)
        toep = at(S0 + 8192, G, P)
        WT = at(S0 + 10240, 2, NPAIR, P)
        CL = at(S0 + 12288, 2, NPAIR, STEP + 1, C)
        W = at(S0 + 14592, 2, NPAIR, STEP, C)
        cosj = at(S0 + 16640, NPAIR, NJ)
        sinj = at(S0 + 17664, NPAIR, NJ)
        decay = at(S0 + 18688, NPAIR, NJ)
        Bz = at(S0 + 19712, 2, NPAIR, 2, C)
        CTt = at(S0 + 20224, 2, NPAIR, C)
        C2 = at(S0 + 20480, 2, P)
        Bb = at(S0 + 20736, 2, NPAIR, C)
        YT0 = 44092
        Hk = at(YT0, NPAIR, STEP, C, parts=2 * C)
        Braw = at(YT0 + 1024, 2, NPAIR, C)
        kst = at(YT0 + 1280, NT, RD)
        sigT = at(19772, 2, T)
        sqc = at(14336, 3, T)
        cacc = at(YT0 + 2048, 2, T)
        wukv = at(48188, H * (ND + VD))
        tmp = at(49212, 1024)
        Vrot = at(S0 + 4096, 2, NPAIR, NJ)
        Zs = at(S0 + 10240, 2, NPAIR, NJ)
        Xp = at(S0 + 4096, 2, NPAIR, NJ)
        yssm = at(S0 + 16640, NT, SW)
        zT = at(S0 + 6144, 2, T)
        sout = at(S0 + 8192, NT, SW)
        cperm = at(S0 + 14592, 2, NT, P)
        ctok = at(S0, NT, CW)
        yT = at(YT0, 4, NT, P)
        qraw = at(0, NT, H * QH)
        kraw = at(6144, NT, H * ND)
        vtok = at(10240, NT, H * VD)
        qn = [at(14336 + 768 * b, NT, QH) for b in range(2)]
        kn = [at(14336 + 1536, NT, QH), at(S0 + 12032, NT, QH)]
        sqq = at(S0 + 19712, H, QH)
        sqk = at(S0 + 20480, H, ND)
        rot = at(14336 + 2304, 2, NT, RD)
        qT = [at(S0 + 1024 * b, T) for b in range(2)]
        kT = [at(S0 + 2048 + 1024 * b, T) for b in range(2)]
        prob = [at(S0 + 4096 + 1024 * b, T) for b in range(2)]
        probT = [at(S0 + 6144 + 512 * b, 4, P) for b in range(3)]
        otok = at(S0 + 7936, NT, AW)
        wout = at(35900, KC, D)
        oT = at(0, 4, NT, P)
        x2 = at(4096, NT, D)
        h2 = [at(32768, D), at(49212, D)]
        junk = at(48188, D)
        h2T = at(33792, KC, P)
        fnorm = at(34816, D)
        EW = KC * FF
        w13 = [[at(12288 + 12288 * b + EW * k, KC, FF) for k in range(2)] for b in range(2)]
        w2s = [at(12288 + 12288 * b + 2 * EW, FC, D) for b in range(2)]
        M0 = 36864
        xg = [at(M0 + 1024 * b, D) for b in range(2)]
        xgT = at(M0 + 2048, KC, P)
        ye = [at(M0 + 4096 + 1024 * b, D) for b in range(2)]
        he = at(M0 + 6144, FF)
        heT = at(M0 + 7168, FC, P)
        yb = [at(12288 + 2 * D * b, 2, D) for b in range(4)]
        sil = at(M0 + 8192, FF)
        R0 = M0 + 8704
        ohg, expg = at(R0, NT, EG), at(R0 + 32, NT, EG)
        gm, rt, m1, m2, expe = (at(R0 + 64 + 8 * k, NT) for k in range(5))
        es, es2 = at(R0 + 128, NT, EPG), at(R0 + 192, NT, EPG)
        oh = [at(R0 + 256 + 64 * k, NT, EPG) for k in range(2)]
        sel = at(R0 + 384, NT, EG, EPG)
        rank, blk = at(R0 + 384, NT, NE), at(R0 + 640, NT, NE)
        pick = [at(R0 + 896 + 256 * k, NT, NE) for k in range(2)]
        both = at(R0 + 1408, NT, NE)
        prior = at(R0 + 1664, NT + 1, NE)
        nov, novend, novb, one32 = (at(R0 + 1952 + NE * k, NE) for k in range(4))
        ovf = at(R0 + 2080, OVF + 1, parts=1)
        ovt = at(R0 + 2096, OVF, NE, parts=1)

        ident = sb("ident", [P, P])
        ones = sb("ones", [P, P])
        minus_half = sb("minus_half", [P, NT * H])
        before = sb("before", [P, P])
        iota_j = sb("iota_j", [P, P])
        lnwb = sb("lnwb", [P, 2, CW])
        qkw = sb("qkw", [P, 2, QH])
        wrank = sb("wrank", [P, 8])
        eiota = sb("eiota", [P, NE])
        freq = sb("freq", [P, HR])
        rope = sb("rope", [P, 2, NT, RD])
        dwc = sb("dwc", [P, 2, TAPS + 1])
        normc = sb("normc", [P, 2 * KC + 4])
        wr = sb("wr", [P, KC, EG + NE])
        brow = sb("brow", [P, EG + NE])
        lg = rope.rearrange("p a i d -> p (a i d)")[:, 0:NT * (EG + NE)].rearrange("p (i e) -> p i e", i=NT)
        st = sb("st", [P, 128])
        qks = sb("qks", [P, 2, NT, H])
        halfpi = sb("halfpi", [P, 1])
        lamc, sc = at(YT0 + 1536, 3, NPAIR), at(YT0 + 1560, 20, NPAIR)
        Lp, Lv = at(YT0 + 1720, 2, STEP + 1, NPAIR), at(YT0 + 1864, 2, STEP, NPAIR)
        dch = sb("dch", [2 * C, NPAIR])
        posi = sb("posi", [P, NT], I32)
        posf = sb("posf", [P, NT])
        gate = sb("gate", [P, 2, NT])
        am = sb("am", [P, 4, 3])
        tabi = sb("tabi", [P, NBLK, 2], I32)
        idx = sb("idx", [P, 4, 2], I32)
        pay = sb("pay", [P, NT, 2, 2], I32)
        slot = sb("slot", [P, NT, 2], I32)
        ovi = sb("ovi", [1, 16], I32)
        dmask = sb("dmask", [2 * C, C])
        bns = sb("bns", [P, NT, 8])
        psum = ctx.enter_context(nc.psum_tensor("psum", [P, 8, 512], F32))

        kpe_d = nc.dram_tensor("kpe_scratch", [T, RD], F32).ap()
        h2_d = nc.dram_tensor("h2_scratch", [T, D], F32).ap()
        tab_d = nc.dram_tensor("slot_table", [NBLK * P, 2], I32).ap()
        y_d = nc.dram_tensor("y_scratch", [2 * T, D], F32).ap()

        x_s = x.rearrange("a (p i) d -> (a p) i d", i=NT)
        out_s = out.rearrange("a (p i) d -> (a p) i d", i=NT)
        h2_s = h2_d.rearrange("(p i) d -> p i d", i=NT)
        y_s = y_d.rearrange("(p i k) d -> p i k d", i=NT, k=2)
        w1_e = w1[0].rearrange("e (c p) f -> e p c f", p=P)
        w3_e = w3[0].rearrange("e (c p) f -> e p c f", p=P)
        w2_e = w2[0].rearrange("e (c p) d -> e p c d", p=P)

        def sems(text):
            return [sem(n) for n in text.split()]

        consts_made, ssm_par_in, small_par_in, row_par_in = sems("consts_made ssm_par_in small_par_in row_par_in")
        win_ag_in, win_rest_in, x_even_in, x_odd_in = sems("win_ag_in win_rest_in x_even_in x_odd_in")
        x_squared, x_rms, x_normed, win_scaled, wproj_in = sems("x_squared x_rms x_normed win_scaled wproj_in")
        wproj_scaled, lo_filled, lo_drained, hi_filled = sems("wproj_scaled lo_filled lo_drained hi_filled")
        hi_drained, trig_ready, trig_done, phase_ready = sems("hi_drained trig_ready trig_done phase_ready")
        tables_made, ssm_w_ready, ssm_c_ready, hk_saved = sems("tables_made ssm_w_ready ssm_c_ready hk_saved")
        toep_in, kst_out, kpe_in, upad_ready, ssm_x_ready = sems("toep_in kst_out kpe_in upad_ready ssm_x_ready")
        lat_squared, lat_rms, qk_saved, qk_squared = sems("lat_squared lat_rms qk_saved qk_squared")
        qk_summed, rope_ang, rope_made, ln_stats, ln_rstd = sems("qk_summed rope_ang rope_made ln_stats ln_rstd")
        ln_done, z_ready, sigm_done, glu_done, mid_squared = sems("ln_done z_ready sigm_done glu_done mid_squared")
        mid_rms, mid_scaled, mid_done, wout_in = sems("mid_rms mid_scaled mid_done wout_in")
        wout_scaled, qkT_made, qT_saved, kT_saved = sems("wout_scaled qkT_made qT_saved kT_saved")
        s_filled, s_masked, s_max, p_ready, pT_filled = sems("s_filled s_masked s_max p_ready pT_filled")
        pT_saved_a, pT_saved_v, pv_done, sum_inv, o_saved = sems("pT_saved_a pT_saved_v pv_done sum_inv o_saved")
        o_squared, o_rms, o_scaled, oT_filled, oT_saved = sems("o_squared o_rms o_scaled oT_filled oT_saved")
        x_again, out_filled, x2_ready, x2_squared, x2_rms = sems("x_again out_filled x2_ready x2_squared x2_rms")
        h2_ready, h2_a_stored, h2_b_stored, h2T_filled = sems("h2_ready h2_a_stored h2_b_stored h2T_filled")
        h2T_saved, lg_filled, lg_saved, expg_in, expg_done = sems("h2T_saved lg_filled lg_saved expg_in expg_done")
        expe_in, expe_done, picks_ready, ranks_filled = sems("expe_in expe_done picks_ready ranks_filled")
        slots_ready, tab_cleared, tab_rows_out, tab_in = sems("slots_ready tab_cleared tab_rows_out tab_in")
        ov_table, w13_a_in, w13_b_in, w2_a_in, w2_b_in = sems("ov_table w13_a_in w13_b_in w2_a_in w2_b_in")
        idxg_copied, idxs_copied, rows_a_in, rows_b_in = sems("idxg_copied idxs_copied rows_a_in rows_b_in")
        xgT_filled, xgT_saved, a_filled, silu_e, b_filled = sems("xgT_filled xgT_saved a_filled silu_e b_filled")
        he_ready, heT_filled, heT_saved, y_filled = sems("he_ready heT_filled heT_saved y_filled")
        y_saved_a, y_saved_v, y_a_out, y_b_out, ov_w_in = sems("y_saved_a y_saved_v y_a_out y_b_out ov_w_in")
        y_in0, y_in1, y_in2, y_in3, combined, out_stored = sems("y_in0 y_in1 y_in2 y_in3 combined out_stored")
        pool_seq, act_seq, dve_seq, pool_steps, head_seq = sems("pool_seq act_seq dve_seq pool_steps head_seq")
        conv_done = sem("conv_done")
        W13_IN, W2_IN = (w13_a_in, w13_b_in), (w2_a_in, w2_b_in)
        ROWS_IN, Y_OUT = (rows_a_in, rows_b_in), (y_a_out, y_b_out)
        H2_OUT = (h2_a_stored, h2_b_stored)
        Y_IN = (y_in0, y_in1, y_in2, y_in3)

        F_XT = lambda i, k: 2 * i + k
        F_AG = lambda half, m: 2 * NT + 4 * half + m
        F_U = lambda i: 2 * NT + 8 + i
        F_LAT = lambda half, m: 3 * NT + 8 + 3 * half + m
        F_SSQ = 3 * NT + 14
        F_QKV = lambda i, k: F_SSQ + 1 + 4 * i + k
        R_C, R_W, R_H, R_U, R_V, R_Y, R_CONV, R_Z, R_GLU, R_SOUT, R_COUT = range(11)
        STEPS = 2 * NT
        fills_of = [(n % NT) // 4 + 1 for n in range(STEPS)]
        first_fill = [sum(fills_of[:n]) for n in range(STEPS + 1)]
        FILLS = first_fill[STEPS]
        by_dve = [f % 3 == 2 for f in range(FILLS)]
        saved_a = [sum(not v for v in by_dve[:f]) for f in range(FILLS + 1)]
        saved_v = [sum(by_dve[:f]) for f in range(FILLS + 1)]

        block = ctx.enter_context(nc.Block())

        def natural(view, half):
            return view.rearrange("p (j i) -> p i j", i=NT)[:, half * 4:half * 4 + 4, :]

        @block.sync
        def _(sp):
            sp.dma_start(xin[:, 0, :], x_s[:, 0, :]).then_inc(x_even_in, 16)
            sp.dma_start(xin[:, 1, :], x_s[:, 1, :]).then_inc(x_odd_in, 16)
            w_in_c = w_in[0].rearrange("(c p) n -> p c n", p=P)
            sp.dma_start(win[:, :, A0:NIN], w_in_c[:, :, A0:NIN]).then_inc(win_ag_in, 16)
            for i in range(2, NT):
                sp.wait_ge(lo_filled, F_XT(i - 2, 1) + 1)
                sp.dma_start(xin[:, i % 2, :], x_s[:, i, :]).then_inc((x_even_in, x_odd_in)[i % 2], 16)
                if i == 2:
                    sp.dma_start(win[:, :, 0:A0], w_in_c[:, :, 0:A0]).then_inc(win_rest_in, 16)
            sp.dma_start(wuq, w_uq[0].rearrange("(c p) n -> p c n", p=P)).then_inc(wproj_in, 16)
            sp.dma_start(wukv, w_ukv[0]).then_inc(wproj_in, 16)
            sp.dma_start(wglu, w_glu[0].rearrange("(c p) n -> p c n", p=P)).then_inc(wproj_in, 16)
            sp.wait_ge(hk_saved, 1)
            for t in range(STEP):
                for h in range(2):
                    sp.dma_start(toep.rearrange("p (r h) n -> p r h n", h=2)[t * C:(t + 1) * C, :, h, t * C:P],
                                 Hk[h * C:(h + 1) * C, :, 0:STEP - t, :].rearrange("p r t c -> p r (t c)")
                                 ).then_inc(toep_in, 16)
            sp.wait_ge(lo_drained, F_U(NT - 1) + 1)
            sp.dma_start(kpe_d.rearrange("(p i) d -> p i d", i=NT), kst).then_inc(kst_out, 16)
            sp.wait_ge(kst_out, 16)
            sp.dma_start(kpe, kpe_d.rearrange("(i p) d -> p i d", p=P)).then_inc(kpe_in, 16)
            sp.wait_ge(mid_done, 1)
            sp.dma_start(wout, w_out[0].rearrange("(c p) n -> p c n", p=P)).then_inc(wout_in, 16)
            sp.wait_ge(o_saved, H * NT)
            sp.dma_start(x2, x_s).then_inc(x_again, 16)
            sp.wait_ge(oT_filled, NT)
            sp.dma_start(fnorm, ffn_norm[0].partition_broadcast(P)).then_inc(x_again, 16)
            for b in range(2):
                sp.dma_start(w13[b][0], w1_e[b]).then_inc(W13_IN[b], 16)
                sp.dma_start(w13[b][1], w3_e[b]).then_inc(W13_IN[b], 16)
            sp.dma_start(w2s[0], w2_e[0]).then_inc(w2_a_in, 16)
            for i in range(NT):
                sp.wait_ge(h2_ready, i + 1)
                sp.dma_start(h2_s[:, i, :], h2[i % 2]).then_inc(H2_OUT[i % 2], 16)
            for b in range(2):
                sp.wait_ge(H2_OUT[b], 8 * NT)
            sp.wait_ge(lg_filled, NT)
            sp.dma_start(w2s[1], w2_e[1]).then_inc(w2_b_in, 16)
            sp.wait_ge(tab_rows_out, 16 * 2 * NT)
            sp.dma_start(tabi, tab_d.rearrange("(p b) k -> p b k", p=P)).then_inc(tab_in, 16)

            with sp.Fori(0, NE // 2 - 1) as it:
                for b in range(2):
                    sp.wait_ge(a_filled, 2 * it + (b + 1))
                    sp.dma_start(w13[b][0], w1_e[2 * it + (b + 2)]).then_inc(W13_IN[b], 16)
                    sp.wait_ge(b_filled, 2 * it + (b + 1))
                    sp.dma_start(w13[b][1], w3_e[2 * it + (b + 2)]).then_inc(W13_IN[b], 16)
                    sp.wait_ge(y_filled, 2 * it + (b + 1))
                    sp.dma_start(w2s[b], w2_e[2 * it + (b + 2)]).then_inc(W2_IN[b], 16)

            sp.wait_ge(ov_table, 1)
            n_ov = sp.value_load(ovi[0:1, OVF:OVF + 1], min_val=0, max_val=OVF)
            with sp.Fori(0, OVF) as it:
                with sp.If(n_ov > it):
                    sp.wait_ge(y_filled, it + NE)
                    e = sp.value_load(ovi[0:1, bass.ds(it, 1)], min_val=0, max_val=NE - 1)
                    sp.dma_start(w13[0][0], w1_e[e]).then_inc(ov_w_in, 16)
                    sp.dma_start(w13[0][1], w3_e[e]).then_inc(ov_w_in, 16)
                    sp.dma_start(w2s[0], w2_e[e]).then_inc(ov_w_in, 16)

            sp.wait_ge(y_a_out, 16 * (n_ov + NE // 2))
            sp.wait_ge(y_b_out, 16 * (NE // 2))
            for i in range(NT + 4):
                if i < NT:
                    if i >= 4:
                        sp.wait_ge(combined, i - 3)
                    sp.dma_start(yb[i % 4], y_s[:, i, :, :]).then_inc(Y_IN[i % 4], 16)
                if i >= 4:
                    sp.wait_ge(combined, i - 3)
                    sp.dma_start(out_s[:, i - 4, :], x2[:, i - 4, :]).then_inc(out_stored, 16)
            sp.wait_ge(out_stored, 16 * NT)

        @block.gpsimd
        def _(pool):
            seq = [0]

            def link(ins):
                seq[0] += 1
                ins.then_inc(pool_seq, 1)
                pool.wait_ge(pool_seq, seq[0])

            def settle():
                pool.sem_inc(pool_steps, 1)

            def rms(col_in, col_out, n, width, eps, what):
                link(pool.tensor_scalar(st[:, col_out:col_out + width], st[:, col_in:col_in + width],
                                        1.0 / n, eps, ALU.mult, ALU.add))
                pool.tensor_tensor(st[:, col_out:col_out + width], st[:, col_out:col_out + width],
                                   minus_half[:, 0:width], ALU.pow).then_inc(what, 1)

            with nc.allow_non_contiguous_dma(reason="parameters of a few KiB"):
                for k, lam in enumerate((lam_re, lam_im)):
                    pool.dma_start(lamc[:, k, :], lam[0].rearrange("(r h) s -> (h s) r", h=2)).then_inc(ssm_par_in, 16)
                for h in range(2):
                    pool.dma_start(lamc[h * S:(h + 1) * S, 2, :],
                                   log_dt[0, h:G:2].partition_broadcast(S)).then_inc(ssm_par_in, 16)
                    for k, c_ in enumerate((c_re, c_im)):
                        pool.dma_start(C2[:, k, h * S:(h + 1) * S],
                                       c_[0].rearrange("(r h) c s -> r h c s", h=2)[:, h, :, :]).then_inc(ssm_par_in, 16)
                for k, b_ in enumerate((b_re, b_im)):
                    pool.dma_start(Braw[:, k, :, :], b_[0].rearrange("(r h) s c -> (h s) r c", h=2)).then_inc(ssm_par_in, 16)
                pool.dma_start(dch[:, :], d_skip[0].rearrange("(r h) c -> (h c) r", h=2)).then_inc(ssm_par_in, 16)
                for k, (v, n) in enumerate(((mix_norm, KC), (out_norm, KC), (q_a_norm, 2), (kv_a_norm, 1))):
                    o = (0, KC, 2 * KC, 2 * KC + 2)[k]
                    pool.dma_start(normc[:, o:o + n], v[0].rearrange("(c p) -> p c", p=P)).then_inc(small_par_in, 16)
                for m in range(2):
                    pool.dma_start(dwc[:, m, 0:TAPS], dw_w[0].rearrange("k (m p) -> m p k", m=2)[m]).then_inc(small_par_in, 16)
                pool.dma_start(dwc[:, :, TAPS], dw_b[0].rearrange("(m p) -> p m", m=2)).then_inc(small_par_in, 16)
                pool.dma_start(posi[:, :], positions[0].rearrange("(i p) -> p i", p=P)).then_inc(small_par_in, 16)
                for k, v in enumerate((ln_w, ln_b)):
                    pool.dma_start(lnwb[:, k, :], v[0].partition_broadcast(P)).then_inc(row_par_in, 16)
                for k, v in enumerate((q_norm, k_norm)):
                    pool.dma_start(qkw[:, k, :], v[0].partition_broadcast(P)).then_inc(row_par_in, 16)
                pool.dma_start(wr[:, :, 0:EG], w_grp[0].rearrange("(c p) n -> p c n", p=P)).then_inc(row_par_in, 16)
                pool.dma_start(wr[:, :, EG:EG + NE], w_exp[0].rearrange("(c p) n -> p c n", p=P)).then_inc(row_par_in, 16)
                pool.dma_start(brow[:, 0:EG], b_grp[0].partition_broadcast(P)).then_inc(row_par_in, 16)
                pool.dma_start(brow[:, EG:EG + NE], b_exp[0].partition_broadcast(P)).then_inc(row_par_in, 16)

            pool.memset(minus_half[:, :], -0.5)
            pool.memset(halfpi[:, :], PI / 2)
            for k in range(HR):
                pool.memset(freq[:, k:k + 1], float(np.float32(10000.0 ** (-2.0 * k / RD))))
            for k in range(8):
                pool.memset(wrank[:, k:k + 1], 8.0 - k)
            pool.memset(ones[:, :], 1.0)
            pool.memset(before[:, :], 1.0)
            pool.memset(upad[:, :, 0:TAPS - 1], 0.0)
            pool.iota(iota_j[:, :], [[1, P]], base=0, channel_multiplier=0, allow_small_or_imprecise_dtypes=True)
            pool.iota(eiota[:, :], [[1, NE]], base=0, channel_multiplier=0, allow_small_or_imprecise_dtypes=True)
            for k in range(2):
                pool.iota(pay[:, :, k, 0], [[1, NT]], base=0, channel_multiplier=NT)
                pool.iota(pay[:, :, k, 1], [[2, NT]], base=k, channel_multiplier=2 * NT)
            pool.memset(tabi[:, :, :], SKIP_ROW)
            link(pool.memset(ident[:, :], 0.0))
            pool.affine_select(out=ident[:, :], in_=ident[:, :], compare_op=ALU.not_equal, fill=1.0,
                               base=0, pattern=[[-1, P]], channel_multiplier=1)
            link(pool.affine_select(out=before[:, :], in_=before[:, :], compare_op=ALU.is_gt, fill=0.0,
                                    base=0, pattern=[[1, P]], channel_multiplier=-1))
            pool.tensor_tensor(dmask[:, :], ident[0:2 * C, 0:C], ident[0:2 * C, C:2 * C], ALU.add).then_inc(consts_made, 1)
            pool.memset(toep, 0.0).then_inc(consts_made, 1)
            pool.wait_ge(consts_made, 2)
            pool.dma_start(tab_d.rearrange("(p b) k -> p b k", p=P), tabi[:, :, :]).then_inc(tab_cleared, 16)

            pool.wait_ge(small_par_in, 16 * 8)
            for i in range(NT):
                pool.wait_ge(x_squared, i + 1)
                rms(i, 8 + i, D, 1, EPS, x_rms)
                if i == 3:
                    pool.wait_ge(win_ag_in, 16)
                    for c in range(KC):
                        last = pool.tensor_scalar(win[:, c, A0:NIN], win[:, c, A0:NIN], normc[:, c:c + 1], None, ALU.mult)
                    last.then_inc(win_scaled, 1)
            pool.wait_ge(win_rest_in, 16)
            for c in range(KC):
                last = pool.tensor_scalar(win[:, c, 0:A0], win[:, c, 0:A0], normc[:, c:c + 1], None, ALU.mult)
            last.then_inc(win_scaled, 1)
            for half in range(2):
                for m in range(2):
                    pool.wait_ge(lo_drained, F_AG(half, 2 * m + 1) + 1)
                    v = natural(upad[:, m, TAPS - 1:PADW], half)
                    pool.tensor_tensor(v, v, natural(sigT[:, m, :], half), ALU.mult).then_inc(upad_ready, 1)
            pool.wait_ge(wproj_in, 16 * 3)
            for c in range(2):
                pool.tensor_scalar(wuq[:, c, :], wuq[:, c, :], normc[:, 2 * KC + c:2 * KC + c + 1], None, ALU.mult)
            pool.tensor_scalar(wukv, wukv, normc[:, 2 * KC + 2:2 * KC + 3], None, ALU.mult).then_inc(wproj_scaled, 1)
            pool.wait_ge(lo_drained, F_SSQ + 1)
            rms(16, 32, QL, NT, EPS, lat_rms)
            rms(24, 40, KL, NT, EPS, lat_rms)
            pool.wait_ge(hk_saved, 1)
            for i in range(NT):
                pool.wait_ge(qk_saved, i + 1)
                if i >= 1:
                    pool.wait_ge(qk_summed, i)
                qv = qraw[:, i, :].rearrange("p (h d) -> p h d", d=QH)
                kv = kraw[:, i, :].rearrange("p (h d) -> p h d", d=ND)
                pool.tensor_tensor(sqq, qv, qv, ALU.mult)
                pool.tensor_tensor(sqk, kv, kv, ALU.mult).then_inc(qk_squared, 1)
            pool.wait_ge(qk_summed, NT + 1)
            qks_f = qks.rearrange("p a i h -> p (a i h)")
            for a in range(2):
                v = qks_f[:, a * NT * H:(a + 1) * NT * H]
                link(pool.tensor_scalar(v, v, 1.0 / QH, EPS, ALU.mult, ALU.add))
                link(pool.tensor_tensor(v, v, minus_half[:, :], ALU.pow))
            pool.wait_ge(kpe_in, 16)
            pool.wait_ge(rope_made, 3)
            pool.wait_ge(row_par_in, 16 * 8)
            link(pool.tensor_scalar(qkw[:, 0, :], qkw[:, 0, :], SCALE, None, ALU.mult))

            pool.wait_ge(ln_stats, 1)
            link(pool.tensor_scalar(st[:, 112:112 + NT], bns[:, :, 7], 1.0, LN_EPS, ALU.mult, ALU.add))
            pool.tensor_tensor(st[:, 112:112 + NT], st[:, 112:112 + NT], minus_half[:, 0:NT], ALU.pow).then_inc(ln_rstd, 1)
            pool.wait_ge(mid_squared, 1)
            rms(64, 72, CW, NT, EPS, mid_rms)
            pool.wait_ge(mid_squared, 2)
            rms(48, 56, SW, NT, EPS, mid_rms)

            with pool.Fori(0, H // 2) as it:
                for b in range(2):
                    base, n = b * LINKS, [0]

                    def hlink(ins):
                        n[0] += 1
                        ins.then_inc(head_seq, 1)
                        pool.wait_ge(head_seq, it * (2 * LINKS) + (base + n[0]))

                    hd = 2 * it + b
                    for a, buf in enumerate((qn[b], kn[b])):
                        settle()
                        r = qks[:, a, :, bass.ds(hd, 1)]
                        if a == 0:
                            hlink(pool.tensor_tensor(buf, qraw[:, :, bass.ds(hd * QH, QH)],
                                                     r.to_broadcast([P, NT, QH]), ALU.mult))
                        else:
                            hlink(pool.tensor_tensor(buf[:, :, 0:ND], kraw[:, :, bass.ds(hd * ND, ND)],
                                                     r.to_broadcast([P, NT, ND]), ALU.mult))
                            settle()
                            hlink(pool.tensor_tensor(buf[:, :, ND:QH], kpe, r.to_broadcast([P, NT, RD]), ALU.mult))
                        hlink(pool.tensor_tensor(buf, buf, qkw[:, a, :].unsqueeze(1).to_broadcast([P, NT, QH]), ALU.mult))
                        hlink(pool.tensor_tensor(rot[:, 0], buf[:, :, ND:QH], rope[:, 0], ALU.mult))
                        hlink(pool.tensor_tensor(rot[:, 1, :, 0:HR], buf[:, :, ND + HR:QH], rope[:, 1, :, 0:HR], ALU.mult))
                        hlink(pool.tensor_tensor(rot[:, 1, :, HR:RD], buf[:, :, ND:ND + HR], rope[:, 1, :, HR:RD], ALU.mult))
                        hlink(pool.tensor_tensor(buf[:, :, ND:QH], rot[:, 0], rot[:, 1], ALU.add))
                    assert n[0] == LINKS
                pool.wait_ge(qkT_made, 2 * it + 2)

            pool.wait_ge(wout_in, 16)
            for c in range(KC):
                last = pool.tensor_scalar(wout[:, c, :], wout[:, c, :], normc[:, KC + c:KC + c + 1], None, ALU.mult)
            last.then_inc(wout_scaled, 1)
            pool.wait_ge(o_squared, NT)
            rms(80, 88, AW, NT, EPS, o_rms)
            for i in range(NT):
                pool.wait_ge(x2_squared, i + 1)
                rms(96 + i, 104 + i, D, 1, EPS, x2_rms)

            pool.wait_ge(tab_cleared, 16)
            pool.wait_ge(slots_ready, 1)
            for i in range(NT):
                for k in range(2):
                    pool.indirect_dma_start(out=tab_d, out_offset=bass.IndirectOffsetOnAxis(ap=slot[:, i, k:k + 1], axis=0),
                                            in_=pay[:, i, k, :], in_offset=None).then_inc(tab_rows_out, 16)
            for b in range(2):
                link(pool.memset(xg[b], 0.0))
            pool.wait_ge(tab_in, 16)
            for b in range(2):
                pool.wait_ge(H2_OUT[b], 8 * NT)

            def gather(b, e):
                pool.tensor_copy(idx[:, b, :], tabi[:, bass.ds(e, 1), :].rearrange("p a k -> p (a k)")).then_inc(idxg_copied, 1)
                pool.wait_ge(idxg_copied, e + 1)
                settle()
                pool.indirect_dma_start(out=xg[b], out_offset=None, in_=h2_d,
                                        in_offset=bass.IndirectOffsetOnAxis(ap=idx[:, b, 0:1], axis=0),
                                        bounds_check=T - 1, oob_is_err=False).then_inc(ROWS_IN[b], 16)

            def scatter(b, e):
                pool.wait_ge(y_saved_a, e + 2)
                pool.wait_ge(y_saved_v, e + 2)
                settle()
                pool.tensor_copy(idx[:, 2 + b, :], tabi[:, bass.ds(e, 1), :].rearrange("p a k -> p (a k)")).then_inc(idxs_copied, 1)
                pool.wait_ge(idxs_copied, e + 1)
                settle()
                pool.indirect_dma_start(out=y_d, out_offset=bass.IndirectOffsetOnAxis(ap=idx[:, 2 + b, 1:2], axis=0),
                                        in_=ye[b], in_offset=None,
                                        bounds_check=2 * T - 1, oob_is_err=False).then_inc(Y_OUT[b], 16)

            gather(0, 0)
            gather(1, 1)
            with pool.Fori(0, NE // 2 - 1) as it:
                for b in range(2):
                    pool.wait_ge(xgT_filled, 2 * it + (b + 1))
                    pool.wait_ge(ROWS_IN[b], 16 * it + 16)
                    settle()
                    gather(b, 2 * it + (b + 2))
                    scatter(b, 2 * it + b)
            for b in range(2):
                scatter(b, NE - 2 + b)
            n_ov = pool.value_load(ovi[0:1, OVF:OVF + 1], min_val=0, max_val=OVF)
            with pool.Fori(0, OVF) as it:
                with pool.If(n_ov > it):
                    pool.wait_ge(xgT_filled, it + NE)
                    pool.wait_ge(ROWS_IN[0], 16 * it + 16 * (NE // 2))
                    settle()
                    gather(0, it + NE)
                    scatter(0, it + NE)

        @block.scalar
        def _(act):
            seq = [0]

            def link(ins):
                seq[0] += 1
                ins.then_inc(act_seq, 1)
                act.wait_ge(act_seq, seq[0])

            def lo(n):
                return psum[:, n % 4, :]

            def save_xT(i):
                for k in range(2):
                    act.wait_ge(lo_filled, F_XT(i, k) + 1)
                    act.activation(hT[:, 4 * k:4 * k + 4, i, :], lo(F_XT(i, k)).rearrange("p (c j) -> p c j", c=4),
                                   ACT.Copy).then_inc(lo_drained, 1)

            for i in range(NT + 1):
                if i < NT:
                    act.wait_ge((x_even_in, x_odd_in)[i % 2], 16 * (i // 2 + 1))
                    link(act.activation(tmp, xin[:, i % 2, :], ACT.Square, accum_out=st[:, i:i + 1]))
                    act.sem_inc(x_squared, 1)
                    act.wait_ge(x_rms, i + 1)
                    act.activation(xin[:, i % 2, :], xin[:, i % 2, :], ACT.Copy, scale=st[:, 8 + i:9 + i]).then_inc(x_normed, 1)
                if i >= 1:
                    save_xT(i - 1)
            act.wait_ge(trig_ready, 1)
            act.activation(sc[:, 7, :], sc[:, 5, :], ACT.Sin, scale=0.5)
            act.activation(sc[:, 8, :], sc[:, 5, :], ACT.Sin).then_inc(trig_done, 1)
            act.wait_ge(consts_made, 1)
            act.wait_ge(phase_ready, 1)
            act.activation(sinj, sinj, ACT.Sin, scale=TWO_PI_SAFE)
            act.activation(cosj, cosj, ACT.Sin, scale=-TWO_PI_SAFE, bias=halfpi[:, 0:1]).then_inc(tables_made, 1)
            act.wait_ge(rope_ang, 1)
            for k in range(2):
                act.activation(rope[:, k, :, HR:RD], rope[:, k, :, 0:HR], ACT.Sin,
                               **(dict(scale=-1.0, bias=halfpi[:, 0:1]) if k == 0 else {})).then_inc(rope_made, 1)
            for half in range(2):
                for m in range(2):
                    n = F_AG(half, 2 * m)
                    act.wait_ge(lo_filled, n + 1)
                    act.activation(natural(sigT[:, m, :], half), lo(n).rearrange("p (i j) -> p i j", i=4),
                                   ACT.Sigmoid).then_inc(lo_drained, 1)
                    act.wait_ge(lo_filled, n + 2)
                    act.activation(natural(upad[:, m, TAPS - 1:PADW], half), lo(n + 1).rearrange("p (i j) -> p i j", i=4),
                                   ACT.Copy).then_inc(lo_drained, 1)
            act.wait_ge(hi_filled, R_W + 1)
            for k in range(4):
                last = act.activation(WT[:, k // 2, 4 * (k % 2):4 * (k % 2) + 4, :],
                                      psum[:, 4 + k, :].rearrange("p (r n) -> p r n", r=4), ACT.Copy)
            last.then_inc(hi_drained, 1)
            act.wait_ge(ssm_w_ready, 1)
            for i in range(NT):
                n = F_U(i)
                act.wait_ge(lo_filled, n + 1)
                act.activation(kst[:, i, :], lo(n)[:, 0:RD], ACT.Copy)
                act.activation(utok[:, :, i, :], lo(n)[:, RD:RD + SW].rearrange("p (g c) -> p g c", c=C),
                               ACT.Copy).then_inc(lo_drained, 1)
            act.wait_ge(hi_filled, R_H + 1)
            for k in range(2):
                last = act.activation(Hk[:, 4 * k:4 * k + 4, :, :].rearrange("p r t c -> p r (t c)"),
                                      psum[0:2 * C, 4 + k, :].rearrange("p (r n) -> p r n", r=4), ACT.Copy)
            last.then_inc(hi_drained, 1)
            act.wait_ge(hi_filled, R_U + 1)
            act.wait_ge(hk_saved, 1)
            for k in range(4):
                last = act.activation(U[:, 4 * k:4 * k + 4, :], psum[:, 4 + k, :].rearrange("p (g j) -> p g j", g=4), ACT.Copy)
            last.then_inc(hi_drained, 1)
            act.wait_ge(upad_ready, 4)
            for half in range(2):
                for m in range(3):
                    n = F_LAT(half, m)
                    act.wait_ge(lo_filled, n + 1)
                    dst = cqT[:, m, :] if m < 2 else ckvT
                    act.activation(natural(dst, half), lo(n).rearrange("p (i j) -> p i j", i=4), ACT.Copy).then_inc(lo_drained, 1)
            act.wait_ge(lo_drained, F_LAT(1, 2) + 1)
            for m in range(3):
                last = act.activation(sqc[:, m, :], cqT[:, m, :] if m < 2 else ckvT, ACT.Square)
            last.then_inc(lat_squared, 1)
            act.wait_ge(lo_filled, F_SSQ + 1)
            act.activation(st[:, 16:16 + 2 * NT], lo(F_SSQ)[:, 0:2 * NT], ACT.Copy).then_inc(lo_drained, 1)
            act.wait_ge(lat_rms, 2)
            for i in range(NT):
                for k in range(2):
                    n = F_QKV(i, k)
                    act.wait_ge(lo_filled, n + 1)
                    act.activation(qraw[:, i, k * 384:k * 384 + 384], lo(n)[:, 0:384], ACT.Copy,
                                   scale=st[:, 32 + i:33 + i]).then_inc(lo_drained, 1)
                for k in range(2):
                    n = F_QKV(i, 2 + k)
                    act.wait_ge(lo_filled, n + 1)
                    v = lo(n).rearrange("p (h d) -> p h d", d=ND + VD)
                    for dst, d0 in ((kraw, 0), (vtok, ND)):
                        last = act.activation(dst[:, i, k * 256:k * 256 + 256].rearrange("p (h d) -> p h d", d=ND),
                                              v[:, :, d0:d0 + ND], ACT.Copy, scale=st[:, 40 + i:41 + i])
                    link(last)
                    act.sem_inc(lo_drained, 1)
                act.sem_inc(qk_saved, 1)
            act.wait_ge(ssm_x_ready, 1)
            act.wait_ge(hi_filled, R_Y + 1)
            z_v = yssm.rearrange("p t (r h c) -> p h r t c", h=2, c=C)
            for h in range(2):
                for k in range(2):
                    for t4 in range(4):
                        last = act.activation(z_v[:, h, 4 * k + t4, :, :],
                                              psum[:, 4 + 2 * h + k, t4 * P:(t4 + 1) * P].rearrange("p (t c) -> p t c", c=C),
                                              ACT.Gelu_apprx_tanh)
            link(last)
            act.sem_inc(z_ready, 1)
            act.sem_inc(hi_drained, 1)
            act.wait_ge(ln_done, 1)
            link(act.activation(ctok, ctok, ACT.Silu))
            for i in range(NT):
                link(act.activation(tmp[:, 0:CW], ctok[:, i, :], ACT.Square, accum_out=st[:, 64 + i:65 + i]))
            act.sem_inc(mid_squared, 1)
            act.wait_ge(mid_rms, 1)
            for i in range(NT):
                last = act.activation(ctok[:, i, :], ctok[:, i, :], ACT.Copy, scale=st[:, 72 + i:73 + i])
            link(last)
            act.sem_inc(mid_scaled, 1)
            act.wait_ge(hi_filled, R_Z + 1)
            for k in range(4):
                last = act.activation(zT.rearrange("p c (k i j) -> p k i c j", k=4, i=2)[:, k],
                                      psum[:, 4 + k, :].rearrange("p (i c j) -> p i c j", i=2, c=2), ACT.Copy)
            last.then_inc(hi_drained, 1)
            act.wait_ge(hi_filled, R_GLU + 1)
            for k in range(4):
                last = act.activation(sout[:, 2 * k:2 * k + 2, :], psum[:, 4 + k, :].rearrange("p (i n) -> p i n", i=2), ACT.Sigmoid)
            link(last)
            act.sem_inc(hi_drained, 1)
            act.sem_inc(sigm_done, 1)
            act.wait_ge(glu_done, 1)
            for i in range(NT):
                link(act.activation(tmp[:, 0:SW], sout[:, i, :], ACT.Square, accum_out=st[:, 48 + i:49 + i]))
            act.sem_inc(mid_squared, 1)
            act.wait_ge(mid_rms, 2)
            for i in range(NT):
                last = act.activation(sout[:, i, :], sout[:, i, :], ACT.Copy, scale=st[:, 56 + i:57 + i])
            link(last)
            act.sem_inc(mid_scaled, 1)
            for r, c0 in ((R_SOUT, 0), (R_COUT, 2)):
                act.wait_ge(hi_filled, r + 1)
                for k in range(4):
                    last = act.activation(yT[:, c0:c0 + 2].rearrange("p c (k i) j -> p k i c j", k=4)[:, k],
                                          psum[:, 4 + k, :].rearrange("p (i c j) -> p i c j", i=2, c=2), ACT.Copy)
                last.then_inc(hi_drained, 1)
            act.wait_ge(hi_drained, R_COUT + 1)
            act.sem_inc(mid_done, 1)

            with act.Fori(0, H // 2) as it:
                it16, itF = act.snap(STEPS * it), act.snap(FILLS * it)
                ita, itv = act.snap(saved_a[FILLS] * it), act.snap(saved_v[FILLS] * it)

                def save_kT(b):
                    act.wait_ge(qkT_made, 2 * it + (b + 1))
                    last = act.activation(kT[b][0:QH, :].rearrange("p (k n) -> p k n", k=2), psum[0:QH, 4 * b + 2:4 * b + 4, :], ACT.Copy)
                    last.then_inc(kT_saved, 1)

                def exponentials(n):
                    act.wait_ge(s_max, it16 + (n + 1))
                    if n >= 2:
                        act.wait_ge(pT_filled, itF + first_fill[n - 1])
                    i, a = n % NT, am[:, n % 4, :]
                    L = (i + 1) * P
                    act.activation(prob[n % 2][:, 0:L], psum[:, 2 * (n % 2):2 * (n % 2) + 2, :].rearrange("p a n -> p (a n)")[:, 0:L],
                                   ACT.Exp, bias=a[:, 0:1], accum_out=a[:, 1:2]).then_inc(p_ready, 1)

                for b in range(2):
                    save_kT(b)
                exponentials(0)
                exponentials(1)
                for n in range(STEPS):
                    for f in range(first_fill[n], first_fill[n + 1]):
                        if not by_dve[f]:
                            act.wait_ge(pT_filled, itF + (f + 1))
                            w = min(4, n % NT + 1 - 4 * (f - first_fill[n]))
                            if f >= 3:
                                act.wait_ge(pv_done, itF + (f - 2))
                            act.activation(probT[f % 3][:, 0:w, :], psum[:, 4 + f % 2, 0:w * P].rearrange("p (a n) -> p a n", n=P),
                                           ACT.Copy).then_inc(pT_saved_a, 1)
                    if n + 2 < STEPS:
                        exponentials(n + 2)

            act.wait_ge(o_saved, H * NT)
            for i in range(NT):
                link(act.activation(prob[0][:, 0:AW], otok[:, i, :], ACT.Square, accum_out=st[:, 80 + i:81 + i]))
            act.sem_inc(o_squared, NT)
            act.wait_ge(o_rms, 1)
            for i in range(NT):
                act.activation(otok[:, i, :], otok[:, i, :], ACT.Copy, scale=st[:, 88 + i:89 + i]).then_inc(o_scaled, 1)
            for i in range(NT):
                act.wait_ge(oT_filled, i + 1)
                for c in range(4):
                    last = act.activation(oT[:, c, :, 16 * i:16 * i + 16].rearrange("p i j -> p j i"),
                                          psum[:, i % 4, c * P:(c + 1) * P].rearrange("p (j i) -> p j i", i=NT), ACT.Copy)
                last.then_inc(oT_saved, 1)
            for i in range(NT + 1):
                if i < NT:
                    act.wait_ge(x2_ready, i + 1)
                    link(act.activation(junk, x2[:, i, :], ACT.Square, accum_out=st[:, 96 + i:97 + i]))
                    act.sem_inc(x2_squared, 1)
                if i >= 1:
                    act.wait_ge(h2T_filled, i)
                    act.activation(h2T.rearrange("p (k c) n -> p k (c n)", k=2), psum[:, 4:6, :], ACT.Copy).then_inc(h2T_saved, 1)
            act.wait_ge(expg_in, 1)
            act.activation(expg, expg, ACT.Exp).then_inc(expg_done, 1)
            act.wait_ge(expe_in, 1)
            act.activation(expe, expe, ACT.Exp).then_inc(expe_done, 1)

            def save_xgT(e):
                act.wait_ge(xgT_filled, e + 1)
                act.activation(xgT.rearrange("p (k c) n -> p k (c n)", k=2), psum[:, 3:5, :], ACT.Copy).then_inc(xgT_saved, 1)

            def silu(e):
                if not isinstance(e, int) or e >= 1:
                    act.wait_ge(he_ready, e)
                act.wait_ge(a_filled, e + 1)
                act.activation(sil, psum[:, 0, :], ACT.Silu).then_inc(silu_e, 1)

            def save_y(b, e, scatters):
                if not isinstance(scatters, int) or scatters >= 1:
                    act.wait_ge(Y_OUT[b], scatters)
                act.wait_ge(y_filled, e + 1)
                act.activation(ye[b][:, 0:512], psum[:, 5, :], ACT.Copy).then_inc(y_saved_a, 1)

            act.sem_inc(y_saved_a, 1)
            save_xgT(0)
            silu(0)
            save_xgT(1)

            def two_experts(it):
                for b in (1, 0):
                    e = 2 * it + (2 - b)
                    silu(e)
                    save_xgT(e + 1)
                    save_y(1 - b, e - 1, 16 * it)

            two_experts(0)
            with act.Fori(1, NE // 2 - 1) as it:
                two_experts(it)
            silu(NE - 1)
            save_y(0, NE - 2, 16 * (NE // 2 - 1))
            save_y(1, NE - 1, 16 * (NE // 2 - 1))
            n_ov = act.value_load(ovi[0:1, OVF:OVF + 1], min_val=0, max_val=OVF)
            with act.Fori(0, OVF) as it:
                with act.If(n_ov > it):
                    save_xgT(it + NE)
                    silu(it + NE)
                    save_y(0, it + NE, 16 * it + 16 * (NE // 2))

        @block.vector
        def _(dve):
            seq = [0]

            def link(ins):
                seq[0] += 1
                ins.then_inc(dve_seq, 1)
                dve.wait_ge(dve_seq, seq[0])

            def tt(out_, a, b_, op):
                link(dve.tensor_tensor(out_, a, b_, op))

            def ts(out_, a, s1, s2, op0, op1=None):
                link(dve.tensor_scalar(out_, a, s1, s2, op0, *(() if op1 is None else (op1,))))

            def stt(out_, a, s1, b_, op0, op1):
                link(dve.scalar_tensor_tensor(out_, a, s1, b_, op0, op1))

            def v(k):
                return sc[:, k, :]

            M_, A_, S_ = ALU.mult, ALU.add, ALU.subtract

            dve.wait_ge(ssm_par_in, 16 * 11)
            lr, li = lamc[:, 0, :], lamc[:, 1, :]
            ts(v(0), lamc[:, 2, :], 1.0 / 16, None, M_)
            ts(v(1), v(0), 1.0 / 9, 1.0, M_, A_)
            for k in range(8, 0, -1):
                tt(v(1), v(1), v(0), M_)
                ts(v(1), v(1), 1.0 / k, 1.0, M_, A_)
            for _ in range(4):
                tt(v(1), v(1), v(1), M_)
            tt(v(2), lr, v(1), M_)
            ts(v(3), v(2), -20.0, 1.0 / 16, ALU.max, M_)
            ts(v(4), v(3), 1.0 / 7, 1.0, M_, A_)
            for k in range(6, 1, -1):
                tt(v(4), v(4), v(3), M_)
                ts(v(4), v(4), 1.0 / k, 1.0, M_, A_)
            tt(v(4), v(4), v(3), M_)
            for _ in range(4):
                stt(v(4), v(4), 2.0, v(4), A_, M_)

            def reduce_angle(x_, turns):
                ts(turns, x_, 1.0 / (2 * PI), ROUND, M_, A_)
                ts(turns, turns, ROUND, None, S_)
                stt(x_, turns, -TWO_PI_HI, x_, M_, A_)
                stt(x_, turns, -TWO_PI_LO, x_, M_, A_)
                ts(x_, x_, 3.1415925, -3.1415925, ALU.min, ALU.max)

            tt(v(5), li, v(1), M_)
            reduce_angle(v(5), v(6))
            dve.sem_inc(trig_ready, 1)
            ts(v(10), v(5), float(STEP), None, M_)
            reduce_angle(v(10), v(11))
            ts(v(10), v(10), 1.0 / (2 * PI), None, M_)
            ts(v(11), v(10), ROUND16, None, A_)
            ts(v(11), v(11), ROUND16, None, S_)
            tt(v(12), v(10), v(11), S_)
            dve.wait_ge(consts_made, 1)
            jb = iota_j[:, :].unsqueeze(1).to_broadcast([P, NPAIR, NJ])

            def wide(col):
                return col.unsqueeze(2).to_broadcast([P, NPAIR, NJ])

            tt(sinj, wide(v(11)), jb, M_)
            ts(cosj, sinj, ROUND, None, A_)
            ts(cosj, cosj, ROUND, None, S_)
            tt(sinj, sinj, cosj, S_)
            tt(cosj, wide(v(12)), jb, M_)
            tt(sinj, sinj, cosj, A_)
            ts(cosj, sinj, ROUND, None, A_)
            ts(cosj, cosj, ROUND, None, S_)
            tt(sinj, sinj, cosj, S_)
            ts(sinj, sinj, 0.5, -0.5, ALU.min, ALU.max)
            fl = "p r j -> p (r j)"
            stt(cosj.rearrange(fl), sinj.rearrange(fl), -1.0, sinj.rearrange(fl), M_, ALU.max)
            dve.sem_inc(phase_ready, 1)
            dve.wait_ge(small_par_in, 16 * 8)
            link(dve.tensor_copy(posf[:, :], posi[:, :]))
            ang, turns = rope[:, 1, :, 0:HR], rope[:, 0, :, 0:HR]
            tt(ang, posf[:, :].unsqueeze(2).to_broadcast([P, NT, HR]),
               freq[:, :].unsqueeze(1).to_broadcast([P, NT, HR]), M_)
            reduce_angle(ang, turns)
            stt(turns, ang, -1.0, ang, M_, ALU.max)
            dve.sem_inc(rope_ang, 1)
            dve.wait_ge(trig_done, 1)
            tt(v(7), v(7), v(7), M_)
            ts(v(7), v(7), -2.0, None, M_)
            stt(v(9), v(7), 1.0, v(4), A_, M_)
            tt(v(9), v(9), v(7), A_)
            link(dve.memset(Lp[:, 0, 0, :], 1.0))
            link(dve.memset(Lp[:, 1, 0, :], 0.0))
            ts(Lp[:, 0, 1, :], v(9), 1.0, None, A_)
            stt(Lp[:, 1, 1, :], v(4), 1.0, v(8), A_, M_)

            def lpow(k, n):
                a = [Lp[:, c, 1:1 + n, :] for c in range(2)]
                m = [Lp[:, c, k:k + 1, :].to_broadcast([P, n, NPAIR]) for c in range(2)]
                o = [Lp[:, c, k + 1:k + 1 + n, :] for c in range(2)]
                t_ = sc[:, 14:14 + n, :]
                tt(o[0], a[0], m[0], M_)
                tt(t_, a[1], m[1], M_)
                tt(o[0], o[0], t_, S_)
                tt(o[1], a[0], m[1], M_)
                tt(t_, a[1], m[0], M_)
                tt(o[1], o[1], t_, A_)

            lpow(1, 1)
            lpow(2, 2)
            lpow(4, 4)
            for t in range(STEP):
                link(dve.tensor_copy(Lv[:, :, t, :], Lp[:, :, STEP - 1 - t, :]))
            ts(v(13), v(4), 1.0, None, A_)
            for _ in range(3):
                tt(v(13), v(13), v(13), M_)
            link(dve.tensor_copy(decay, wide(v(13))))
            link(dve.memset(decay[:, :, 0:1], 0.0))
            tt(v(14), lr, lr, M_)
            tt(v(15), li, li, M_)
            tt(v(14), v(14), v(15), A_)
            link(dve.reciprocal(v(14), v(14)))
            tt(v(18), v(9), lr, M_)
            tt(v(15), Lp[:, 1, 1, :], li, M_)
            tt(v(18), v(18), v(15), A_)
            tt(v(18), v(18), v(14), M_)
            tt(v(19), Lp[:, 1, 1, :], lr, M_)
            tt(v(15), v(9), li, M_)
            tt(v(19), v(19), v(15), S_)
            tt(v(19), v(19), v(14), M_)

            def cmul(out_, a, b_, t_):
                tt(out_[0], a[0], b_[0], M_)
                tt(t_, a[1], b_[1], M_)
                tt(out_[0], out_[0], t_, S_)
                tt(out_[1], a[0], b_[1], M_)
                tt(t_, a[1], b_[0], M_)
                tt(out_[1], out_[1], t_, A_)

            T4 = at(S0 + 8192 - 2048, NPAIR, STEP, C)
            cmul([Bb[:, k] for k in range(2)], [v(k).unsqueeze(2).to_broadcast([P, NPAIR, C]) for k in (18, 19)],
                 [Braw[:, k] for k in range(2)], T4[:, :, 0, :])
            cmul([W[:, k] for k in range(2)],
                 [Lv[:, k].rearrange("p t r -> p r t").unsqueeze(3).to_broadcast([P, NPAIR, STEP, C]) for k in range(2)],
                 [Bb[:, k].unsqueeze(2).to_broadcast([P, NPAIR, STEP, C]) for k in range(2)], T4)
            link(dve.memset(Bz, 0.0))
            for h in range(2):
                link(dve.tensor_copy(Bz[h * S:(h + 1) * S, :, :, h, :], Bb[h * S:(h + 1) * S]))
            dve.sem_inc(ssm_w_ready, 1)
            dve.wait_ge(hi_filled, R_C + 1)
            link(dve.tensor_copy(CTt.rearrange("p a r c -> p a (r c)"), psum[:, 4, 0:2 * P].rearrange("p (a n) -> p a n", a=2)))
            dve.sem_inc(hi_drained, 1)
            T5 = at(S0 + 6144, NPAIR, STEP + 1, C)
            Cb = [CTt[:, k].unsqueeze(2).to_broadcast([P, NPAIR, STEP + 1, C]) for k in range(2)]
            Lb = [Lp[:, k].rearrange("p t r -> p r t").unsqueeze(3).to_broadcast([P, NPAIR, STEP + 1, C]) for k in range(2)]
            tt(CL[:, 0], Cb[0], Lb[0], M_)
            tt(T5, Cb[1], Lb[1], M_)
            tt(CL[:, 0], CL[:, 0], T5, S_)
            tt(CL[:, 1], Cb[0], Lb[1], M_)
            tt(T5, Cb[1], Lb[0], M_)
            flat = "p r t c -> p (r t c)"
            stt(CL[:, 1].rearrange(flat), CL[:, 1].rearrange(flat), -1.0, T5.rearrange(flat), M_, S_)
            dve.sem_inc(ssm_c_ready, 1)
            dve.wait_ge(rope_made, 2)
            link(dve.tensor_copy(rope[:, 0, :, 0:HR], rope[:, 0, :, HR:RD]))
            ts(rope[:, 1, :, 0:HR], rope[:, 1, :, HR:RD], -1.0, None, M_)
            dve.sem_inc(rope_made, 1)
            dve.wait_ge(consts_made, 2)
            dd = at(S0 + 6144, NPAIR, C, parts=2 * C)
            tt(dd, dmask[:, :].unsqueeze(1).to_broadcast([2 * C, NPAIR, C]),
               dch[:, :].unsqueeze(2).to_broadcast([2 * C, NPAIR, C]), M_)
            dve.wait_ge(hi_drained, R_H + 1)
            tt(Hk[:, :, 0, :], Hk[:, :, 0, :], dd, A_)
            dve.sem_inc(hk_saved, 1)

            dve.wait_ge(upad_ready, 4)
            base, n = seq[0], 0
            for k in range(TAPS):
                for m in range(2):
                    if n >= 2:
                        dve.wait_ge(dve_seq, base + n - 1)
                    src = upad[:, m, k:k + T]
                    if k == 0:
                        ins = dve.tensor_scalar(cacc[:, m, :], src, dwc[:, m, 0:1], dwc[:, m, TAPS:TAPS + 1], M_, A_)
                    elif k < TAPS - 1:
                        ins = dve.scalar_tensor_tensor(cacc[:, m, :], src, dwc[:, m, k:k + 1], cacc[:, m, :], M_, A_)
                    else:
                        ins = dve.scalar_tensor_tensor(cperm[:, m].rearrange("p i j -> p j i"), src.rearrange("p (j i) -> p j i", i=NT),
                                                       dwc[:, m, k:k + 1], cacc[:, m, :].rearrange("p (j i) -> p j i", i=NT), M_, A_)
                    ins.then_inc(dve_seq, 1)
                    n += 1
            seq[0] += n
            dve.wait_ge(dve_seq, seq[0])
            dve.sem_inc(conv_done, 1)

            dve.wait_ge(hi_filled, R_V + 1)
            dve.wait_ge(tables_made, 1)
            Vp = [psum[:, 4 + 2 * k:6 + 2 * k, :].rearrange("p a (r j) -> p (a r) j", j=NJ) for k in range(2)]
            tmp3 = tmp.rearrange("p (r j) -> p r j", j=NJ)
            tt(Vrot[:, 0], Vp[0], cosj, M_)
            tt(tmp3, Vp[1], sinj, M_)
            tt(Vrot[:, 0], Vrot[:, 0], tmp3, A_)
            tt(Vrot[:, 1], Vp[1], cosj, M_)
            tt(tmp3, Vp[0], sinj, M_)
            dve.sem_inc(hi_drained, 1)
            tt(Vrot[:, 1], Vrot[:, 1], tmp3, S_)
            for k in range(2):
                link(dve.tensor_tensor_scan(Zs[:, k].rearrange("p r j -> p (r j)"), decay.rearrange("p r j -> p (r j)"),
                                            Vrot[:, k].rearrange("p r j -> p (r j)"), 0.0, M_, A_))
            z_ = [Zs[:, k, :, 0:NJ - 1] for k in range(2)]
            cs_, sn_ = cosj[:, :, 0:NJ - 1], sinj[:, :, 0:NJ - 1]
            for k in range(2):
                link(dve.memset(Xp[:, k, :, 0:1], 0.0))
            tt(Xp[:, 0, :, 1:NJ], z_[0], cs_, M_)
            tt(tmp3[:, :, 1:NJ], z_[1], sn_, M_)
            tt(Xp[:, 0, :, 1:NJ], Xp[:, 0, :, 1:NJ], tmp3[:, :, 1:NJ], S_)
            tt(Xp[:, 1, :, 1:NJ], z_[0], sn_, M_)
            tt(tmp3[:, :, 1:NJ], z_[1], cs_, M_)
            tt(Xp[:, 1, :, 1:NJ], Xp[:, 1, :, 1:NJ], tmp3[:, :, 1:NJ], A_)
            dve.sem_inc(ssm_x_ready, 1)

            for i in range(NT):
                dve.wait_ge(qk_squared, i + 1)
                link(dve.reduce_sum(qks[:, 0, i, :], sqq, AX))
                link(dve.reduce_sum(qks[:, 1, i, :], sqk, AX))
                dve.sem_inc(qk_summed, 1)
            dve.wait_ge(kpe_in, 16)
            kp2 = at(S0 + 19712, NT, RD)
            tt(kp2, kpe, kpe, M_)
            link(dve.reduce_sum(st[:, 120:120 + NT], kp2, AX))
            tt(qks[:, 1], qks[:, 1], st[:, 120:120 + NT].unsqueeze(2).to_broadcast([P, NT, H]), A_)
            dve.sem_inc(qk_summed, 1)

            dve.wait_ge(hi_filled, R_CONV + 1)
            pc = [psum[:, 4 + i // 2, (i % 2) * CW:(i % 2 + 1) * CW] for i in range(NT)]
            for i in range(NT):
                last = dve.bn_stats(bns[:, i, 0:6], pc[i])
            link(last)
            for i in range(NT):
                last = dve.bn_aggr(bns[:, i, 6:8], bns[:, i, 0:6])
            link(last)
            dve.sem_inc(ln_stats, 1)
            dve.wait_ge(ln_rstd, 1)
            for i in range(NT):
                last = dve.tensor_scalar(ctok[:, i, :], pc[i], bns[:, i, 6:7], st[:, 112 + i:113 + i], S_, M_)
            link(last)
            dve.sem_inc(hi_drained, 1)
            dve.wait_ge(row_par_in, 16 * 8)
            tt(ctok, ctok, lnwb[:, 0, :].unsqueeze(1).to_broadcast([P, NT, CW]), M_)
            tt(ctok, ctok, lnwb[:, 1, :].unsqueeze(1).to_broadcast([P, NT, CW]), A_)
            dve.sem_inc(ln_done, 1)
            dve.wait_ge(sigm_done, 1)
            tt(sout, sout, yssm, M_)
            dve.sem_inc(glu_done, 1)

            dve.wait_ge(mid_done, 1)
            with dve.Fori(0, H // 2) as it:
                it16, itF = dve.snap(STEPS * it), dve.snap(FILLS * it)

                def save_qT(b):
                    dve.wait_ge(qkT_made, 2 * it + (b + 1))
                    dve.tensor_copy(qT[b][0:QH, :].rearrange("p (k n) -> p k n", k=2),
                                    psum[0:QH, 4 * b:4 * b + 2, :]).then_inc(qT_saved, 1)

                def row_max(n):
                    i = n % NT
                    sv = psum[:, 2 * (n % 2):2 * (n % 2) + 2, :].rearrange("p a n -> p (a n)")
                    dve.wait_ge(s_filled, it16 + (n + 1))
                    dve.memset(sv[0:P // 2, (i + 1) * P - P // 2:(i + 1) * P], NEG).then_inc(s_masked, 1)
                    dve.wait_ge(s_masked, it16 + (n + 1))
                    dve.reduce_max(am[:, n % 4, 0:1], sv[:, 0:(i + 1) * P], AX, negate=True).then_inc(s_max, 1)

                for b in range(2):
                    save_qT(b)
                row_max(0)
                row_max(1)
                for n in range(STEPS):
                    for f in range(first_fill[n], first_fill[n + 1]):
                        if by_dve[f]:
                            dve.wait_ge(pT_filled, itF + (f + 1))
                            w = min(4, n % NT + 1 - 4 * (f - first_fill[n]))
                            if f >= 3:
                                dve.wait_ge(pv_done, itF + (f - 2))
                            dve.tensor_copy(probT[f % 3][:, 0:w, :], psum[:, 4 + f % 2, 0:w * P].rearrange("p (a n) -> p a n", n=P)
                                            ).then_inc(pT_saved_v, 1)
                    if n + 2 < STEPS:
                        row_max(n + 2)
                    a = am[:, n % 4, :]
                    dve.wait_ge(p_ready, it16 + (n + 1))
                    dve.reciprocal(a[:, 2:3], a[:, 1:2]).then_inc(sum_inv, 1)
                    dve.wait_ge(sum_inv, it16 + (n + 1))
                    dve.wait_ge(pv_done, itF + first_fill[n + 1])
                    dve.tensor_scalar(otok[:, n % NT, bass.ds((2 * it + n // NT) * VD, VD)],
                                      psum[:, 6 + n % 2, 0:VD], a[:, 2:3], None, M_).then_inc(o_saved, 1)

            dve.wait_ge(x_again, 16 * 2)
            for i in range(NT + 3):
                if i < NT:
                    dve.wait_ge(out_filled, i + 1)
                    xi = x2[:, i, :].rearrange("p (a n) -> p a n", a=2)
                    dve.tensor_tensor(xi, xi, psum[:, 2 * (i % 2):2 * (i % 2) + 2, :], A_).then_inc(x2_ready, 1)
                if i >= 3:
                    dve.wait_ge(lg_filled, i - 2)
                    dve.tensor_tensor(lg[:, i - 3, :], psum[:, 6 + (i - 3) % 2, 0:EG + NE], brow[:, :], A_).then_inc(lg_saved, 1)
                if 1 <= i <= NT:
                    dve.wait_ge(x2_rms, i)
                    if i >= 3:
                        dve.wait_ge(H2_OUT[(i - 1) % 2], 16 * ((i - 1) // 2))
                        dve.wait_ge(h2T_filled, i - 2)
                    dve.scalar_tensor_tensor(h2[(i - 1) % 2], x2[:, i - 1, :], st[:, 103 + i:104 + i], fnorm, M_, M_).then_inc(h2_ready, 1)
            dve.wait_ge(lg_saved, NT)

            gl, el = lg[:, :, 0:EG], lg[:, :, EG:EG + NE].rearrange("p t (g k) -> p t g k", g=EG)

            def over(a, n_):
                return a.unsqueeze(2).to_broadcast([P, NT, n_])

            def first_max(hot, top, x_, n_, t_):
                link(dve.reduce_max(top, x_, AX))
                tt(hot, x_, over(top, n_), ALU.is_equal)
                tt(hot, hot, wrank[:, 8 - n_:8].unsqueeze(1).to_broadcast([P, NT, n_]), M_)
                link(dve.reduce_max(t_, hot, AX))
                tt(hot, hot, over(t_, n_), ALU.is_equal)

            first_max(ohg, gm, gl, EG, rt)
            tt(expg, gl, over(gm, EG), S_)
            dve.sem_inc(expg_in, 1)
            tt(sel, el, ohg.unsqueeze(3).to_broadcast([P, NT, EG, EPG]), M_)
            link(dve.reduce_sum(es, sel.rearrange("p t g k -> p t k g"), AX))
            first_max(oh[0], m1, es, EPG, rt)
            stt(es2.rearrange("p t k -> p (t k)"), oh[0].rearrange("p t k -> p (t k)"), -1e30, es.rearrange("p t k -> p (t k)"), M_, A_)
            first_max(oh[1], m2, es2, EPG, rt)
            tt(expe, m2, m1, S_)
            dve.sem_inc(expe_in, 1)
            for k in range(2):
                tt(pick[k].rearrange("p t (g k) -> p t g k", g=EG), ohg.unsqueeze(3).to_broadcast([P, NT, EG, EPG]),
                   oh[k].unsqueeze(2).to_broadcast([P, NT, EG, EPG]), M_)
            tt(both, pick[0], pick[1], A_)
            link(dve.memset(prior[:, 0, :], 0.0))
            for i in range(NT):
                tt(prior[:, i + 1, :], prior[:, i, :], both[:, i, :], A_)
            dve.sem_inc(picks_ready, 1)
            dve.wait_ge(expg_done, 1)
            link(dve.reduce_sum(rt, expg, AX))
            dve.wait_ge(expe_done, 1)
            ts(m1, expe, 1.0, None, A_)
            tt(rt, rt, m1, M_)
            link(dve.reciprocal(gate[:, 0, :], rt))
            tt(gate[:, 1, :], gate[:, 0, :], expe, M_)
            dve.wait_ge(ranks_filled, 1)
            link(dve.tensor_copy(rank, psum[:, 0, 0:NT * NE].rearrange("p (t e) -> p t e", e=NE)))
            ts(nov, psum[:, 1, 0:NE], 63.5, 1.0 / P, A_, M_)
            ts(nov, nov, ROUND, None, A_)
            ts(nov, nov, ROUND + 1.0, 0.0, S_, ALU.max)
            link(dve.memset(one32, 1.0))
            link(dve.tensor_tensor_scan(novend, one32, nov, 0.0, M_, A_))
            tt(novb, novend, nov, S_)
            stt(novb, novb, float(NE - 1), eiota[:, :], A_, S_)
            ts(blk, rank, 63.5, 1.0 / P, S_, M_)
            ts(blk, blk, ROUND, None, A_)
            ts(blk, blk, ROUND, None, S_)
            flat3 = "p t e -> p (t e)"
            stt(rank.rearrange(flat3), blk.rearrange(flat3), -float(P), rank.rearrange(flat3), M_, A_)
            ts(both, blk, 1.0, None, ALU.min)
            tt(both, both, novb.unsqueeze(1).to_broadcast([P, NT, NE]), M_)
            tt(blk, blk, both, A_)
            tt(blk, blk, eiota[:, :].unsqueeze(1).to_broadcast([P, NT, NE]), A_)
            stt(blk.rearrange(flat3), rank.rearrange(flat3), float(NBLK), blk.rearrange(flat3), M_, A_)
            for k in range(2):
                tt(both, pick[k], blk, M_)
                link(dve.reduce_sum(rt, both, AX))
                link(dve.tensor_copy(slot[:, :, k], rt))
            dve.sem_inc(slots_ready, 1)
            tt(ovt, novend[0:1, :].unsqueeze(1).to_broadcast([1, OVF, NE]),
               iota_j[0:1, 0:OVF].unsqueeze(2).to_broadcast([1, OVF, NE]), ALU.is_le)
            link(dve.reduce_sum(ovf[:, 0:OVF], ovt, AX))
            ts(ovf[:, 0:OVF], ovf[:, 0:OVF], float(NE - 1), None, ALU.min)
            link(dve.tensor_copy(ovf[:, OVF:OVF + 1], novend[0:1, NE - 1:NE]))
            link(dve.tensor_copy(ovi[:, :], ovf))
            dve.sem_inc(ov_table, 4)

            def save_heT(e):
                dve.wait_ge(heT_filled, e + 1)
                dve.tensor_copy(heT.rearrange("p c n -> p (c n)"), psum[:, 2, :]).then_inc(heT_saved, 1)

            def hidden(e):
                dve.wait_ge(silu_e, e + 1)
                dve.wait_ge(b_filled, e + 1)
                dve.tensor_tensor(he, sil, psum[:, 1, :], M_).then_inc(he_ready, 1)

            def save_y(b, e, scatters):
                if not isinstance(scatters, int) or scatters >= 1:
                    dve.wait_ge(Y_OUT[b], scatters)
                dve.wait_ge(y_filled, e + 1)
                dve.tensor_copy(ye[b][:, 512:D], psum[:, 6, :]).then_inc(y_saved_v, 1)

            dve.sem_inc(y_saved_v, 1)
            hidden(0)

            def two_experts(it):
                for b in (1, 0):
                    e = 2 * it + (2 - b)
                    save_heT(e - 1)
                    hidden(e)
                    save_y(1 - b, e - 1, 16 * it)

            two_experts(0)
            with dve.Fori(1, NE // 2 - 1) as it:
                two_experts(it)
            save_heT(NE - 2)
            hidden(NE - 1)
            save_y(0, NE - 2, 16 * (NE // 2 - 1))
            save_heT(NE - 1)
            save_y(1, NE - 1, 16 * (NE // 2 - 1))
            n_ov = dve.value_load(ovi[0:1, OVF:OVF + 1], min_val=0, max_val=OVF)
            with dve.Fori(0, OVF) as it:
                with dve.If(n_ov > it):
                    hidden(it + NE)
                    save_heT(it + NE)
                    save_y(0, it + NE, 16 * it + 16 * (NE // 2))

            for i in range(NT):
                dve.wait_ge(Y_IN[i % 4], 16 * (i // 4 + 1))
                stt(x2[:, i, :], yb[i % 4][:, 0, :], gate[:, 0, i:i + 1], x2[:, i, :], M_, A_)
                dve.scalar_tensor_tensor(x2[:, i, :], yb[i % 4][:, 1, :], gate[:, 1, i:i + 1], x2[:, i, :], M_, A_).then_inc(combined, 1)

        @block.tensor
        def _(pe):
            def lo(n):
                if n >= 4:
                    pe.wait_ge(lo_drained, n - 3)
                return psum[:, n % 4, :]

            def hi(r):
                if r >= 1:
                    pe.wait_ge(hi_drained, r)

            pe.wait_ge(consts_made, 1)
            pe.wait_ge(ssm_par_in, 16 * 11)
            hi(R_C)
            for k in range(2):
                last = pe.transpose(psum[:, 4, k * P:(k + 1) * P], C2[:, k, :], ident[:, :])
            last.then_inc(hi_filled, 1)
            for i in range(NT):
                pe.wait_ge(x_normed, i + 1)
                for k in range(2):
                    bank = lo(F_XT(i, k))
                    for c in range(4):
                        last = pe.transpose(bank[:, c * P:(c + 1) * P], xin[:, i % 2, (4 * k + c) * P:(4 * k + c + 1) * P], ident[:, :])
                    last.then_inc(lo_filled, 1)
            def project(n, half, c0):
                bank = lo(n)
                pe.wait_ge(lo_drained, F_XT(4 * half + 3, 1) + 1)
                for c in range(KC):
                    last = pe.matmul(bank, win[:, c, c0:c0 + P], hT[:, c, 4 * half:4 * half + 4, :].rearrange("p i j -> p (i j)"),
                                     start=(c == 0), stop=(c == KC - 1))
                last.then_inc(lo_filled, 1)

            pe.wait_ge(win_scaled, 1)
            for half in range(2):
                for m in range(2):
                    project(F_AG(half, 2 * m), half, G0 + m * P)
                    project(F_AG(half, 2 * m + 1), half, A0 + m * P)
            pe.wait_ge(ssm_w_ready, 1)
            hi(R_W)
            for k in range(2):
                for r in range(NPAIR):
                    last = pe.transpose(psum[:, 4 + 2 * k + r // 4, (r % 4) * P:(r % 4 + 1) * P],
                                        W[:, k, r].rearrange("p t c -> p (t c)"), ident[:, :])
            last.then_inc(hi_filled, 1)
            pe.wait_ge(win_scaled, 2)
            for i in range(NT):
                bank = lo(F_U(i))
                for c in range(KC):
                    last = pe.matmul(bank[:, 0:RD + SW], hT[:, c, i, :], win[:, c, KPE0:A0], start=(c == 0), stop=(c == KC - 1))
                last.then_inc(lo_filled, 1)
            pe.wait_ge(ssm_c_ready, 1)
            hi(R_H)
            for r in range(NPAIR):
                o = psum[0:2 * C, 4 + r // 4, (r % 4) * P:(r % 4 + 1) * P]
                for k in range(2):
                    last = pe.matmul(o, Bz[:, k, r].rearrange("p h c -> p (h c)"),
                                     CL[:, k, r, 0:STEP, :].rearrange("p t c -> p (t c)"), start=(k == 0), stop=(k == 1))
            last.then_inc(hi_filled, 1)
            hi(R_U)
            pe.wait_ge(lo_drained, F_U(NT - 1) + 1)
            for g in range(G):
                last = pe.transpose(psum[:, 4 + g // 4, (g % 4) * P:(g % 4 + 1) * P], utok[:, g].rearrange("p t c -> p (t c)"), ident[:, :])
            last.then_inc(hi_filled, 1)
            for half in range(2):
                for m, c0 in enumerate((CQ0, CQ0 + P, CKV0)):
                    project(F_LAT(half, m), half, c0)
            hi(R_V)
            for k in range(2):
                for r in range(NPAIR):
                    for h in range(2):
                        last = pe.matmul(psum[h * S:(h + 1) * S, 4 + 2 * k + r // 4, (r % 4) * P:(r % 4 + 1) * P],
                                         WT[:, k, r, h * S:(h + 1) * S], U[:, 2 * r + h, :], start=True, stop=True)
            last.then_inc(hi_filled, 1)
            pe.wait_ge(lat_squared, 1)
            bank = lo(F_SSQ)
            for i in range(NT):
                for m in range(2):
                    pe.matmul(bank[:, i:i + 1], sqc[:, m, i * P:(i + 1) * P], ones[:, 0:1], start=(m == 0), stop=(m == 1))
                last = pe.matmul(bank[:, NT + i:NT + i + 1], sqc[:, 2, i * P:(i + 1) * P], ones[:, 0:1], start=True, stop=True)
            last.then_inc(lo_filled, 1)
            pe.wait_ge(wproj_scaled, 1)
            for i in range(NT):
                for k in range(2):
                    bank = lo(F_QKV(i, k))
                    for m in range(2):
                        last = pe.matmul(bank[:, 0:384], cqT[:, m, i * P:(i + 1) * P], wuq[:, m, k * 384:(k + 1) * 384],
                                         start=(m == 0), stop=(m == 1))
                    last.then_inc(lo_filled, 1)
                for k in range(2):
                    pe.matmul(lo(F_QKV(i, 2 + k)), ckvT[:, i * P:(i + 1) * P], wukv[:, k * 512:(k + 1) * 512],
                              start=True, stop=True).then_inc(lo_filled, 1)
            pe.wait_ge(toep_in, 16 * 2 * STEP)
            pe.wait_ge(ssm_x_ready, 1)
            hi(R_Y)
            for h in range(2):
                for r in range(NPAIR):
                    o = psum[:, 4 + 2 * h + r // 4, (r % 4) * P:(r % 4 + 1) * P]
                    pe.matmul(o, U[:, 2 * r + h, :], toep[:, 2 * r + h, :], start=True, stop=False)
                    for k in range(2):
                        last = pe.matmul(o, Xp[h * S:(h + 1) * S, k, r, :],
                                         CL[h * S:(h + 1) * S, k, r, 1:STEP + 1, :].rearrange("p t c -> p (t c)"),
                                         start=False, stop=(k == 1))
            last.then_inc(hi_filled, 1)

            def turn(src, r):
                hi(r)
                for i in range(NT):
                    for c in range(2):
                        last = pe.transpose(psum[:, 4 + i // 2, (i % 2) * 256 + c * P:(i % 2) * 256 + (c + 1) * P], src(i, c), ident[:, :])
                last.then_inc(hi_filled, 1)

            pe.wait_ge(conv_done, 1)
            turn(lambda i, c: cperm[:, c, i, :], R_CONV)
            pe.wait_ge(z_ready, 1)
            turn(lambda i, c: yssm[:, i, c * P:(c + 1) * P], R_Z)
            hi(R_GLU)
            for i in range(NT):
                for c in range(2):
                    last = pe.matmul(psum[:, 4 + i // 2, (i % 2) * 256:(i % 2 + 1) * 256], zT[:, c, i * P:(i + 1) * P], wglu[:, c, :],
                                     start=(c == 0), stop=(c == 1))
            last.then_inc(hi_filled, 1)
            pe.wait_ge(mid_scaled, 2)
            turn(lambda i, c: sout[:, i, c * P:(c + 1) * P], R_SOUT)
            turn(lambda i, c: ctok[:, i, c * P:(c + 1) * P], R_COUT)

            pe.wait_ge(mid_done, 1)
            with pe.Fori(0, H // 2) as it:
                it16, itF = pe.snap(STEPS * it), pe.snap(FILLS * it)
                ita, itv = pe.snap(saved_a[FILLS] * it), pe.snap(saved_v[FILLS] * it)
                for b in range(2):
                    pe.wait_ge(head_seq, LINKS * 2 * it + LINKS * (b + 1))
                    for a, buf in enumerate((qn[b], kn[b])):
                        for i in range(NT):
                            last = pe.transpose(psum[0:QH, 4 * b + 2 * a + i // 4, (i % 4) * P:(i % 4 + 1) * P], buf[:, i, :], ident[:, :])
                    last.then_inc(qkT_made, 1)

                def scores(n):
                    b, i = n // NT, n % NT
                    if i == 0:
                        pe.wait_ge(qT_saved, 2 * it + (b + 1))
                        pe.wait_ge(kT_saved, 2 * it + (b + 1))
                    if n >= 2:
                        pe.wait_ge(p_ready, it16 + (n - 1))
                    L = (i + 1) * P
                    for k in range((L + 511) // 512):
                        w = min(512, L - 512 * k)
                        last = pe.matmul(psum[:, 2 * (n % 2) + k, 0:w], qT[b][0:QH, i * P:(i + 1) * P], kT[b][0:QH, 512 * k:512 * k + w],
                                         start=True, stop=True)
                    last.then_inc(s_filled, 1)

                def saved(f, n):
                    pe.wait_ge(pT_saved_a, ita + saved_a[f + 1])
                    if saved_v[f + 1]:
                        pe.wait_ge(pT_saved_v, itv + saved_v[f + 1])

                def turn_probs(n):
                    pe.wait_ge(p_ready, it16 + (n + 1))
                    for f in range(first_fill[n], first_fill[n + 1]):
                        if f < 2:
                            pe.wait_ge(qT_saved, 2 * it + 2)
                        else:
                            saved(f - 2, n)
                        j0 = 4 * (f - first_fill[n])
                        for j in range(j0, min(j0 + 4, n % NT + 1)):
                            last = pe.transpose(psum[:, 4 + f % 2, (j - j0) * P:(j - j0 + 1) * P], prob[n % 2][:, j * P:(j + 1) * P], ident[:, :])
                        last.then_inc(pT_filled, 1)

                def values(n):
                    i = n % NT
                    if n < 2:
                        pe.wait_ge(kT_saved, 2 * it + 2)
                    else:
                        pe.wait_ge(o_saved, it16 + (n - 1))
                    for f in range(first_fill[n], first_fill[n + 1]):
                        saved(f, n)
                        j0 = 4 * (f - first_fill[n])
                        for j in range(j0, min(j0 + 4, i + 1)):
                            last = pe.matmul(psum[:, 6 + n % 2, 0:VD], probT[f % 3][:, j - j0, :],
                                             vtok[:, j, bass.ds((2 * it + n // NT) * VD, VD)], start=(j == 0), stop=(j == i))
                        last.then_inc(pv_done, 1)

                scores(0)
                scores(1)
                for n in range(STEPS):
                    turn_probs(n)
                    if n + 2 < STEPS:
                        scores(n + 2)
                    values(n)
                pe.wait_ge(o_saved, it16 + STEPS)

            for i in range(NT):
                pe.wait_ge(o_scaled, i + 1)
                if i >= 4:
                    pe.wait_ge(oT_saved, i - 3)
                for c in range(4):
                    last = pe.transpose(psum[:, i % 4, c * P:(c + 1) * P], otok[:, i, c * P:(c + 1) * P], ident[:, :])
                last.then_inc(oT_filled, 1)
            pe.wait_ge(oT_saved, NT)
            pe.wait_ge(wout_scaled, 1)

            def logits(i):
                pe.wait_ge(h2T_saved, i + 1)
                if i >= 2:
                    pe.wait_ge(lg_saved, i - 1)
                for c in range(KC):
                    last = pe.matmul(psum[:, 6 + i % 2, 0:EG + NE], h2T[:, c, :], wr[:, c, :], start=(c == 0), stop=(c == KC - 1))
                last.then_inc(lg_filled, 1)

            for i in range(NT + 2):
                if i < NT:
                    if i >= 2:
                        pe.wait_ge(x2_ready, i - 1)
                    for k in range(2):
                        for c in range(KC):
                            y_ = oT[:, c, i, :] if c < 4 else yT[:, c - 4, i, :]
                            last = pe.matmul(psum[:, 2 * (i % 2) + k, :], y_, wout[:, c, 512 * k:512 * (k + 1)],
                                             start=(c == 0), stop=(c == KC - 1))
                    last.then_inc(out_filled, 1)
                if i >= 2:
                    logits(i - 2)
                if 1 <= i <= NT:
                    pe.wait_ge(h2_ready, i)
                    if i >= 2:
                        pe.wait_ge(h2T_saved, i - 1)
                    for c in range(KC):
                        last = pe.transpose(psum[:, 4 + c // 4, (c % 4) * P:(c % 4 + 1) * P], h2[(i - 1) % 2][:, c * P:(c + 1) * P], ident[:, :])
                    last.then_inc(h2T_filled, 1)
            pe.wait_ge(picks_ready, 1)
            o = psum[:, 0, 0:NT * NE]
            pe.matmul(o, before[:, :], both.rearrange("p t e -> p (t e)"), start=True, stop=False)
            pe.matmul(o, ones[:, :], prior[:, 0:NT, :].rearrange("p t e -> p (t e)"), start=False, stop=True)
            pe.matmul(psum[:, 1, 0:NE], ones[:, :], prior[:, NT, :], start=True, stop=True).then_inc(ranks_filled, 1)

            def turn_rows(b, e, gathers):
                pe.wait_ge(ROWS_IN[b], gathers)
                for c in range(KC):
                    last = pe.transpose(psum[:, 3 + c // 4, (c % 4) * P:(c % 4 + 1) * P], xg[b][:, c * P:(c + 1) * P], ident[:, :])
                last.then_inc(xgT_filled, 1)

            def up(k, b, e):
                for c in range(KC):
                    last = pe.matmul(psum[:, k, :], xgT[:, c, :], w13[b][k][:, c, :], start=(c == 0), stop=(c == KC - 1))
                last.then_inc((a_filled, b_filled)[k], 1)

            def turn_hidden(e):
                pe.wait_ge(he_ready, e + 1)
                for c in range(FC):
                    last = pe.transpose(psum[:, 2, c * P:(c + 1) * P], he[:, c * P:(c + 1) * P], ident[:, :])
                last.then_inc(heT_filled, 1)

            def down(b, e):
                pe.wait_ge(heT_saved, e + 1)
                pe.wait_ge(y_saved_a, e + 1)
                pe.wait_ge(y_saved_v, e + 1)
                for k in range(2):
                    for c in range(FC):
                        last = pe.matmul(psum[:, 5 + k, :], heT[:, c, :], w2s[b][:, c, 512 * k:512 * (k + 1)], start=(c == 0), stop=(c == FC - 1))
                last.then_inc(y_filled, 1)

            pe.wait_ge(slots_ready, 1)
            turn_rows(0, 0, 16)
            pe.wait_ge(xgT_saved, 1)
            pe.wait_ge(W13_IN[0], 32)
            up(0, 0, 0)
            up(1, 0, 0)
            turn_rows(1, 1, 16)
            with pe.Fori(0, NE // 2 - 1) as it:
                for b in (1, 0):
                    e = 2 * it + (2 - b)
                    pe.wait_ge(xgT_saved, e + 1)
                    pe.wait_ge(W13_IN[b], 32 * it + 32 * (2 - b))
                    pe.wait_ge(silu_e, e)
                    up(0, b, e)
                    turn_hidden(e - 1)
                    up(1, b, e)
                    turn_rows(1 - b, e + 1, 16 * it + 32)
                    pe.wait_ge(W2_IN[1 - b], 16 * it + 16)
                    down(1 - b, e - 1)
            pe.wait_ge(xgT_saved, NE)
            pe.wait_ge(W13_IN[1], 16 * NE)
            pe.wait_ge(silu_e, NE - 1)
            up(0, 1, NE - 1)
            turn_hidden(NE - 2)
            up(1, 1, NE - 1)
            pe.wait_ge(W2_IN[0], 8 * NE)
            down(0, NE - 2)
            turn_hidden(NE - 1)
            pe.wait_ge(W2_IN[1], 8 * NE)
            down(1, NE - 1)
            pe.wait_ge(ov_table, 1)
            n_ov = pe.value_load(ovi[0:1, OVF:OVF + 1], min_val=0, max_val=OVF)
            with pe.Fori(0, OVF) as it:
                with pe.If(n_ov > it):
                    turn_rows(0, it + NE, 16 * it + 16 * (NE // 2 + 1))
                    pe.wait_ge(xgT_saved, it + (NE + 1))
                    pe.wait_ge(ov_w_in, 48 * it + 48)
                    up(0, 0, it + NE)
                    up(1, 0, it + NE)
                    turn_hidden(it + NE)
                    down(0, it + NE)


_INS = ["x", "positions", "mix_norm", "w_in", "q_a_norm", "w_uq", "kv_a_norm", "w_ukv", "q_norm", "k_norm",
        "ssm_lam_re", "ssm_lam_im", "ssm_b_re", "ssm_b_im", "ssm_c_re", "ssm_c_im", "ssm_d", "ssm_log_dt", "ssm_w_glu",
        "conv_dw_w", "conv_dw_b", "conv_ln_w", "conv_ln_b", "out_norm", "w_out",
        "ffn_norm", "w_grp", "b_grp", "w_exp", "b_exp", "w1", "w3", "w2"]


def kernel(**inputs):
    import numpy as _np
    import concourse.bacc as _bacc
    from concourse import mybir as _mybir
    from concourse.bass_utils import run_bass_kernel_spmd as _run

    nc = _bacc.Bacc("TRN2", target_bir_lowering=False, num_devices=1)
    arrays, args = {}, []
    for name in _INS:
        a = _np.ascontiguousarray(inputs[name])
        arrays[f"in_{name}"] = a
        args.append(nc.dram_tensor(f"in_{name}", a.shape, _mybir.dt.from_np(a.dtype), kind="ExternalInput").ap())
    x = arrays["in_x"]
    out = nc.dram_tensor("out_0", x.shape, _mybir.dt.float32, kind="ExternalOutput").ap()
    build(nc, *args, out)
    r = _run(nc, [arrays], core_ids=[0])
    return r.results[0]["out_0"]
```

```python
from contextlib import ExitStack

import numpy as np

import concourse.bass as bass
from concourse import mybir

ALU = mybir.AluOpType
ACT = mybir.ActivationFunctionType
F32 = mybir.dt.float32
I32 = mybir.dt.int32
U32 = mybir.dt.uint32
AX = mybir.AxisListType.X

P = 128
EPS = 1e-6
LN_EPS = 1e-5
LINKS = 13
PI = float(np.pi)
TWO_PI_SAFE = 6.2831850
TWO_PI_HI = 6.28125
TWO_PI_LO = 2.0 * PI - TWO_PI_HI
ROUND = 1.5 * 2.0 ** 23
ROUND16 = 1.5 * 2.0 ** 7
NEG = -3.0e38
SKIP_ROW = 1 << 20


def build(nc, x, positions, mix_norm, w_in, q_a_norm, w_uq, kv_a_norm, w_ukv, q_norm, k_norm,
          lam_re, lam_im, b_re, b_im, c_re, c_im, d_skip, log_dt, w_glu,
          dw_w, dw_b, ln_w, ln_b, out_norm, w_out,
          ffn_norm, w_grp, b_grp, w_exp, b_exp, w1, w3, w2, out):
    T, D = x.shape[1], x.shape[2]
    NT, KC = T // P, D // P
    QL, KL = q_a_norm.shape[1], kv_a_norm.shape[1]
    QH = q_norm.shape[1]
    H = w_uq.shape[2] // QH
    RD, ND = QH - QH // 3 * 2, QH // 3 * 2
    HR = RD // 2
    VD = w_ukv.shape[2] // H - ND
    G, S = lam_re.shape[1], lam_re.shape[2]
    C = b_re.shape[3]
    SW, CW, TAPS = G * C, dw_w.shape[2], dw_w.shape[1]
    NPAIR = G // 2
    STEP = P // C
    NJ = T // STEP
    EG, NE = w_grp.shape[2], w_exp.shape[2]
    EPG = NE // EG
    FF = w1.shape[3]
    FC = FF // P
    OVF = 2 * T // P
    NBLK = NE + OVF + 2
    assert (T, D, NT, KC, QH, RD, ND, VD) == (1024, 1024, 8, 8, 96, 32, 64, 64)
    assert STEP == NT and NJ == P and SW == CW == 256 and S == 64 and 2 * C == 32
    CQ0, CKV0, KPE0, U0, A0, G0 = 0, QL, QL + KL, QL + KL + RD, QL + KL + RD + SW, QL + KL + RD + SW + CW
    NIN = G0 + CW
    SCALE = float(QH) ** -0.5
    AW = H * VD

    with ExitStack() as ctx:
        def sb(name, shape, dt=F32):
            return ctx.enter_context(nc.sbuf_tensor(name, shape, dt))[tuple(slice(0, n) for n in shape)]

        def sem(name):
            return ctx.enter_context(nc.semaphore(name))

        WORDS = 50300
        arena = sb("arena", [P, WORDS])

        def at(off, *dims, parts=P):
            n = int(np.prod(dims))
            assert off + n <= WORDS
            v = arena[0:parts, off:off + n]
            if len(dims) == 2:
                return v.rearrange("p (a b) -> p a b", b=dims[1])
            if len(dims) == 3:
                return v.rearrange("p (a b c) -> p a b c", b=dims[1], c=dims[2])
            if len(dims) == 4:
                return v.rearrange("p (a b c d) -> p a b c d", b=dims[1], c=dims[2], d=dims[3])
            return v

        hT = at(0, KC, NT, P)
        win = at(8192, KC, NIN)
        PADW = T + TAPS - 1
        upad = at(17664, 2, PADW)
        cqT = at(19772, 2, T)
        ckvT = at(21820, T)
        kpe = at(22844, NT, RD)
        S0 = 23100
        xin = [at((S0, S0 + 2048, S0 + 4096, 19772)[k], 2, D) for k in range(4)]
        wuq = at(S0 + 2048, 2, H * QH)
        wglu = at(S0 + 3584, 2, SW)
        utok = at(S0 + 4096, G, STEP, C)
        U = at(S0 + 6144, G, NJ)
        toep = at(S0 + 8192, G, P)
        WT = at(S0 + 10240, 2, NPAIR, P)
        CL = at(S0 + 12288, 2, NPAIR, STEP + 1, C)
        W = at(S0 + 14592, 2, NPAIR, STEP, C)
        cosj = at(S0 + 16640, NPAIR, NJ)
        sinj = at(S0 + 17664, NPAIR, NJ)
        decay = at(S0 + 18688, NPAIR, NJ)
        Bz = at(S0 + 19712, 2, NPAIR, 2, C)
        CTt = at(S0 + 20224, 2, NPAIR, C)
        C2 = at(S0 + 20480, 2, P)
        Bb = at(S0 + 20736, 2, NPAIR, C)
        YT0 = 44092
        Hk = at(YT0, NPAIR, STEP, C, parts=2 * C)
        Braw = at(YT0 + 1024, 2, NPAIR, C)
        kst = at(YT0 + 1280, NT, RD)
        sigT = at(19772, 2, T)
        sqc = at(14336, 3, T)
        cacc = at(YT0 + 2048, 2, T)
        wukv = at(48188, H * (ND + VD))
        tmp = at(49212, 1024)
        Vrot = at(S0 + 4096, 2, NPAIR, NJ)
        Zs = at(S0 + 10240, 2, NPAIR, NJ)
        Xp = at(S0 + 4096, 2, NPAIR, NJ)
        yssm = at(S0 + 16640, NT, SW)
        zT = at(S0 + 6144, 2, T)
        sout = at(S0 + 8192, NT, SW)
        cperm = at(S0 + 14592, 2, NT, P)
        ctok = at(S0, NT, CW)
        yT = at(YT0, 4, NT, P)
        qraw = at(0, NT, H * QH)
        kraw = at(6144, NT, H * ND)
        vtok = at(10240, NT, H * VD)
        qn = [at(14336 + 768 * b, NT, QH) for b in range(2)]
        kn = [at(14336 + 1536, NT, QH), at(S0 + 12032, NT, QH)]
        sqq = [at(14336 + 1280 * b, H, QH) for b in range(2)]
        sqk = [at(14336 + 1280 * b + 768, H, ND) for b in range(2)]
        rot = at(14336 + 2304, 2, NT, RD)
        rot_dve = at(14336 + 2816, 2, NT, RD)
        qT = [at(S0 + 1024 * b, T) for b in range(2)]
        kT = [at(S0 + 2048 + 1024 * b, T) for b in range(2)]
        prob = [at(S0 + 4096 + 1024 * b, T) for b in range(2)]
        probT = [at((S0 + 6144, S0 + 6656, S0 + 7168, 17664)[b], 4, P) for b in range(4)]
        otok = at(S0 + 7936, NT, AW)
        wout = at(35900, KC, D)
        oT = at(0, 4, NT, P)
        x2 = at(4096, NT, D)
        h2 = [at(32768, D), at(49212, D)]
        junk = at(48188, D)
        h2T = at(33792, KC, P)
        fnorm = at(34816, D)
        EW = KC * FF
        w13 = [[at(12288 + 12288 * b + EW * k, KC, FF) for k in range(2)] for b in range(2)]
        w2s = [at(12288 + 12288 * b + 2 * EW, FC, D) for b in range(2)]
        M0 = 36864
        xg = [at(M0 + 1024 * b, D) for b in range(2)]
        xgT = at(M0 + 2048, KC, P)
        ye = [at(M0 + 4096 + 1024 * b, D) for b in range(2)]
        he = at(M0 + 6144, FF)
        heT = at(M0 + 7168, FC, P)
        sil = at(M0 + 8192, FF)
        R0 = M0 + 8704
        ohg, expg = at(R0, NT, EG), at(R0 + 32, NT, EG)
        gm, rt, m1, m2, expe = (at(R0 + 64 + 8 * k, NT) for k in range(5))
        es, es2 = at(R0 + 128, NT, EPG), at(R0 + 192, NT, EPG)
        oh = [at(R0 + 256 + 64 * k, NT, EPG) for k in range(2)]
        sel = at(R0 + 384, NT, EG, EPG)
        rank, blk = at(R0 + 384, NT, NE), at(R0 + 640, NT, NE)
        pick = [at(R0 + 896 + 256 * k, NT, NE) for k in range(2)]
        both = at(R0 + 1408, NT, NE)
        prior = at(R0 + 1664, NT + 1, NE)
        nov, novend, novb, one32 = (at(R0 + 1952 + NE * k, NE) for k in range(4))
        ovf = at(R0 + 2080, OVF + 1, parts=1)
        ovt = at(R0 + 2096, OVF, NE, parts=1)

        ident = sb("ident", [P, P])
        ones = sb("ones", [P, P])
        minus_half = sb("minus_half", [P, NT * H])
        before = sb("before", [P, P])
        iota_j = sb("iota_j", [P, P])
        lnwb = sb("lnwb", [P, 2, CW])
        qkw = sb("qkw", [P, 2, QH])
        wrank = sb("wrank", [P, 8])
        eiota = sb("eiota", [P, NE])
        freq = sb("freq", [P, HR])
        rope = sb("rope", [P, 2, NT, RD])
        dwc = sb("dwc", [P, 2, TAPS + 1])
        normc = sb("normc", [P, 2 * KC + 4])
        wr = sb("wr", [P, KC, EG + NE])
        brow = sb("brow", [P, EG + NE])
        lg = rope.rearrange("p a i d -> p (a i d)")[:, 0:NT * (EG + NE)].rearrange("p (i e) -> p i e", i=NT)
        st = sb("st", [P, 128])
        qks = sb("qks", [P, 2, NT, H])
        halfpi = sb("halfpi", [P, 1])
        lamc, sc = at(YT0 + 1536, 3, NPAIR), at(YT0 + 1560, 20, NPAIR)
        Lp, Lv = at(YT0 + 1720, 2, STEP + 1, NPAIR), at(YT0 + 1864, 2, STEP, NPAIR)
        dch = sb("dch", [2 * C, NPAIR])
        posi = sb("posi", [P, NT], I32)
        posf = sb("posf", [P, NT])
        gate = sb("gate", [P, 2, NT])
        am = sb("am", [P, 4, 3])
        tabi = sb("tabi", [P, NBLK, 2], I32)
        idx = sb("idx", [P, 4, 2], I32)
        pay = sb("pay", [P, NT, 2, 2], I32)
        slot = sb("slot", [P, NT, 2], I32)
        ovi = sb("ovi", [1, OVF + 1], I32)
        dmask = sb("dmask", [2 * C, C])
        bns = sb("bns", [P, NT, 8])
        psum = ctx.enter_context(nc.psum_tensor("psum", [P, 8, 512], F32))

        kpe_d = nc.dram_tensor("kpe_scratch", [T, RD], F32).ap()
        h2_d = nc.dram_tensor("h2_scratch", [T, D], F32).ap()
        tab_d = nc.dram_tensor("slot_table", [NBLK * P, 2], I32).ap()

        x_s = x.rearrange("a (p i) d -> (a p) i d", i=NT)
        out_s = out.rearrange("a (p i) d -> (a p) i d", i=NT)
        h2_s = h2_d.rearrange("(p i) d -> p i d", i=NT)
        out_d = out.rearrange("a t d -> (a t) d")
        w1_e = w1[0].rearrange("e (c p) f -> e p c f", p=P)
        w3_e = w3[0].rearrange("e (c p) f -> e p c f", p=P)
        w2_e = w2[0].rearrange("e (c p) d -> e p c d", p=P)

        def sems(text):
            return [sem(n) for n in text.split()]

        consts_made, ssm_par_in, small_par_in, row_par_in = sems("consts_made ssm_par_in small_par_in row_par_in")
        win_ag_in, win_rest_in, x01_in, x23_in, x45_in, x67_in = sems("win_ag_in win_rest_in x01_in x23_in x45_in x67_in")
        x_squared, x_rms, x_normed, win_scaled, wproj_in = sems("x_squared x_rms x_normed win_scaled wproj_in")
        wproj_scaled, lo_filled, lo_drained, hi_filled = sems("wproj_scaled lo_filled lo_drained hi_filled")
        hi_drained, trig_ready, trig_done, phase_ready = sems("hi_drained trig_ready trig_done phase_ready")
        tables_made, ssm_w_ready, ssm_c_ready, hk_saved = sems("tables_made ssm_w_ready ssm_c_ready hk_saved")
        toep_in, kst_out, kpe_in, upad_ready, ssm_x_ready = sems("toep_in kst_out kpe_in upad_ready ssm_x_ready")
        lat_squared, lat_rms, qk_saved, qk_squared = sems("lat_squared lat_rms qk_saved qk_squared")
        qk_summed, rope_ang, rope_made, ln_stats, ln_rstd = sems("qk_summed rope_ang rope_made ln_stats ln_rstd")
        ln_done, z_ready, sigm_done, glu_done, mid_squared = sems("ln_done z_ready sigm_done glu_done mid_squared")
        mid_rms, mid_scaled, mid_done, wout_in = sems("mid_rms mid_scaled mid_done wout_in")
        wout_scaled, qkT_made, qT_saved, kT_saved = sems("wout_scaled qkT_made qT_saved kT_saved")
        s_filled, s_masked, s_max, p_ready, pT_filled = sems("s_filled s_masked s_max p_ready pT_filled")
        pT_saved_a, pT_saved_v, pv_done, sum_inv, o_saved = sems("pT_saved_a pT_saved_v pv_done sum_inv o_saved")
        o_squared, o_rms, o_scaled, oT_filled, oT_saved = sems("o_squared o_rms o_scaled oT_filled oT_saved")
        x_again, out_filled, x2_ready, x2_squared, x2_rms = sems("x_again out_filled x2_ready x2_squared x2_rms")
        h2_ready, h2_a_stored, h2_b_stored, h2T_filled = sems("h2_ready h2_a_stored h2_b_stored h2T_filled")
        h2T_saved, lg_filled, lg_saved, expg_in, expg_done = sems("h2T_saved lg_filled lg_saved expg_in expg_done")
        expe_in, expe_done, picks_ready, ranks_filled = sems("expe_in expe_done picks_ready ranks_filled")
        slots_ready, tab_cleared, tab_rows_out, tab_in = sems("slots_ready tab_cleared tab_rows_out tab_in")
        ov_table, w13_a_in, w13_b_in, w2_a_in, w2_b_in = sems("ov_table w13_a_in w13_b_in w2_a_in w2_b_in")
        idxg_copied, idxs_copied, rows_a_in, rows_b_in = sems("idxg_copied idxs_copied rows_a_in rows_b_in")
        xgT_filled, xgT_saved, a_filled, silu_e, b_filled = sems("xgT_filled xgT_saved a_filled silu_e b_filled")
        he_ready, heT_filled, heT_saved, y_filled = sems("he_ready heT_filled heT_saved y_filled")
        y_saved_a, y_saved_v, y_a_out, y_b_out, ov_w_a_in, ov_w_b_in = sems("y_saved_a y_saved_v y_a_out y_b_out ov_w_a_in ov_w_b_in")
        out_stored = sem("out_stored")
        pool_seq, act_seq, dve_seq, pool_steps, head_seq = sems("pool_seq act_seq dve_seq pool_steps head_seq")
        conv_done, qk_mean, qk_root, heads_made = sems("conv_done qk_mean qk_root heads_made")
        X_IN = (x01_in, x23_in, x45_in, x67_in)
        W13_IN, W2_IN = (w13_a_in, w13_b_in), (w2_a_in, w2_b_in)
        ROWS_IN, Y_OUT = (rows_a_in, rows_b_in), (y_a_out, y_b_out)
        OV_W_IN = (ov_w_a_in, ov_w_b_in)
        H2_OUT = (h2_a_stored, h2_b_stored)

        F_XT = lambda i, k: 2 * i + k
        F_AG = lambda half, m: 2 * NT + 4 * half + m
        F_U = lambda i: 2 * NT + 8 + i
        F_LAT = lambda half, m: 3 * NT + 8 + 3 * half + m
        F_SSQ = 3 * NT + 14
        F_QKV = lambda i, k: F_SSQ + 1 + 4 * i + k
        R_C, R_W, R_H, R_U, R_V, R_Y, R_CONV, R_Z, R_GLU, R_COUT, R_SOUT = range(11)
        STEPS = 2 * NT
        tile_of = [(NT - 1 - n % NT // 2) if n % 2 == 0 else n % NT // 2 for n in range(STEPS)]
        fills_of = [i // 4 + 1 for i in tile_of]
        first_fill = [sum(fills_of[:n]) for n in range(STEPS + 1)]
        FILLS = first_fill[STEPS]
        by_dve = [f % 3 == 2 for f in range(FILLS)]
        saved_a = [sum(not v for v in by_dve[:f]) for f in range(FILLS + 1)]
        saved_v = [sum(by_dve[:f]) for f in range(FILLS + 1)]

        block = ctx.enter_context(nc.Block())

        def natural(view, half):
            return view.rearrange("p (j i) -> p i j", i=NT)[:, half * 4:half * 4 + 4, :]

        def make_heads_part(eng, link, settle, hd, b, a, rot):
            mult, buf = ALU.mult, (qn, kn)[a][b]
            r = qks[:, a, :, bass.ds(hd, 1)]
            if settle:
                settle()
            if a == 0:
                link(eng.tensor_tensor(buf, qraw[:, :, bass.ds(hd * QH, QH)], r.to_broadcast([P, NT, QH]), mult))
            else:
                link(eng.tensor_tensor(buf[:, :, 0:ND], kraw[:, :, bass.ds(hd * ND, ND)], r.to_broadcast([P, NT, ND]), mult))
                if settle:
                    settle()
                link(eng.tensor_tensor(buf[:, :, ND:QH], kpe, r.to_broadcast([P, NT, RD]), mult))
            link(eng.tensor_tensor(buf, buf, qkw[:, a, :].unsqueeze(1).to_broadcast([P, NT, QH]), mult))
            link(eng.tensor_tensor(rot[:, 0], buf[:, :, ND:QH], rope[:, 0], mult))
            link(eng.tensor_tensor(rot[:, 1, :, 0:HR], buf[:, :, ND + HR:QH], rope[:, 1, :, 0:HR], mult))
            link(eng.tensor_tensor(rot[:, 1, :, HR:RD], buf[:, :, ND:ND + HR], rope[:, 1, :, HR:RD], mult))
            link(eng.tensor_tensor(buf[:, :, ND:QH], rot[:, 0], rot[:, 1], ALU.add))

        @block.sync
        def _(sp):
            def load_x(k):
                sp.dma_start(xin[k], x_s[:, 2 * k:2 * k + 2, :]).then_inc(X_IN[k], 16)

            load_x(0)
            with nc.allow_non_contiguous_dma(reason="parameters of a few KiB"):
                for k, lam in enumerate((lam_re, lam_im)):
                    sp.dma_start(lamc[:, k, :], lam[0].rearrange("(r h) s -> (h s) r", h=2)).then_inc(ssm_par_in, 16)
                for h in range(2):
                    sp.dma_start(lamc[h * S:(h + 1) * S, 2, :],
                                   log_dt[0, h:G:2].partition_broadcast(S)).then_inc(ssm_par_in, 16)
                    for k, c_ in enumerate((c_re, c_im)):
                        sp.dma_start(C2[:, k, h * S:(h + 1) * S],
                                       c_[0].rearrange("(r h) c s -> r h c s", h=2)[:, h, :, :]).then_inc(ssm_par_in, 16)
                for k, b_ in enumerate((b_re, b_im)):
                    sp.dma_start(Braw[:, k, :, :], b_[0].rearrange("(r h) s c -> (h s) r c", h=2)).then_inc(ssm_par_in, 16)
                sp.dma_start(dch[:, :], d_skip[0].rearrange("(r h) c -> (h c) r", h=2)).then_inc(ssm_par_in, 16)
            for k in range(1, 4):
                load_x(k)
            with nc.allow_non_contiguous_dma(reason="parameters of a few KiB"):
                for k, (v, n) in enumerate(((mix_norm, KC), (out_norm, KC), (q_a_norm, 2), (kv_a_norm, 1))):
                    o = (0, KC, 2 * KC, 2 * KC + 2)[k]
                    sp.dma_start(normc[:, o:o + n], v[0].rearrange("(c p) -> p c", p=P)).then_inc(small_par_in, 16)
                for m in range(2):
                    sp.dma_start(dwc[:, m, 0:TAPS], dw_w[0].rearrange("k (m p) -> m p k", m=2)[m]).then_inc(small_par_in, 16)
                sp.dma_start(dwc[:, :, TAPS], dw_b[0].rearrange("(m p) -> p m", m=2)).then_inc(small_par_in, 16)
                sp.dma_start(posi[:, :], positions[0].rearrange("(i p) -> p i", p=P)).then_inc(small_par_in, 16)
            w_in_c = w_in[0].rearrange("(c p) n -> p c n", p=P)
            sp.dma_start(win[:, :, A0:NIN], w_in_c[:, :, A0:NIN]).then_inc(win_ag_in, 16)
            sp.dma_start(win[:, :, 0:A0], w_in_c[:, :, 0:A0]).then_inc(win_rest_in, 16)
            sp.wait_ge(lo_filled, F_XT(3, 1) + 1)
            sp.dma_start(wuq, w_uq[0].rearrange("(c p) n -> p c n", p=P)).then_inc(wproj_in, 16)
            sp.dma_start(wukv, w_ukv[0]).then_inc(wproj_in, 16)
            sp.dma_start(wglu, w_glu[0].rearrange("(c p) n -> p c n", p=P)).then_inc(wproj_in, 16)
            sp.wait_ge(hk_saved, 1)
            for t in range(STEP):
                for h in range(2):
                    sp.dma_start(toep.rearrange("p (r h) n -> p r h n", h=2)[t * C:(t + 1) * C, :, h, t * C:P],
                                 Hk[h * C:(h + 1) * C, :, 0:STEP - t, :].rearrange("p r t c -> p r (t c)")
                                 ).then_inc(toep_in, 16)
            sp.wait_ge(lo_drained, F_U(NT - 1) + 1)
            sp.dma_start(kpe_d.rearrange("(p i) d -> p i d", i=NT), kst).then_inc(kst_out, 16)
            sp.wait_ge(kst_out, 16)
            sp.dma_start(kpe, kpe_d.rearrange("(i p) d -> p i d", p=P)).then_inc(kpe_in, 16)
            sp.wait_ge(mid_done, 1)
            sp.dma_start(wout, w_out[0].rearrange("(c p) n -> p c n", p=P)).then_inc(wout_in, 16)
            sp.wait_ge(o_saved, H * NT)
            sp.dma_start(x2, x_s).then_inc(x_again, 16)
            sp.wait_ge(oT_filled, NT)
            sp.dma_start(fnorm, ffn_norm[0].partition_broadcast(P)).then_inc(x_again, 16)
            for b in range(2):
                sp.dma_start(w13[b][0], w1_e[b]).then_inc(W13_IN[b], 16)
                sp.dma_start(w13[b][1], w3_e[b]).then_inc(W13_IN[b], 16)
            sp.dma_start(w2s[0], w2_e[0]).then_inc(w2_a_in, 16)
            for i in range(NT):
                sp.wait_ge(h2_ready, i + 1)
                sp.dma_start(h2_s[:, i, :], h2[i % 2]).then_inc(H2_OUT[i % 2], 16)
                sp.dma_start(out_s[:, i, :], x2[:, i, :]).then_inc(out_stored, 16)
            for b in range(2):
                sp.wait_ge(H2_OUT[b], 8 * NT)
            sp.wait_ge(lg_filled, NT)
            sp.dma_start(w2s[1], w2_e[1]).then_inc(w2_b_in, 16)
            sp.wait_ge(tab_rows_out, 16 * 2 * NT)
            sp.dma_start(tabi, tab_d.rearrange("(p b) k -> p b k", p=P)).then_inc(tab_in, 16)

            with sp.Fori(0, NE // 2 - 1) as it:
                for b in range(2):
                    sp.wait_ge(a_filled, 2 * it + (b + 1))
                    sp.dma_start(w13[b][0], w1_e[2 * it + (b + 2)]).then_inc(W13_IN[b], 16)
                    sp.wait_ge(b_filled, 2 * it + (b + 1))
                    sp.dma_start(w13[b][1], w3_e[2 * it + (b + 2)]).then_inc(W13_IN[b], 16)
                    sp.wait_ge(y_filled, 2 * it + (b + 1))
                    sp.dma_start(w2s[b], w2_e[2 * it + (b + 2)]).then_inc(W2_IN[b], 16)

            sp.wait_ge(ov_table, 1)
            n_ov = sp.value_load(ovi[0:1, OVF:OVF + 1], min_val=0, max_val=OVF)
            with sp.Fori(0, OVF // 2) as it:
                for b in range(2):
                    with sp.If(n_ov > 2 * it + b):
                        e = sp.value_load(ovi[0:1, bass.ds(2 * it + b, 1)], min_val=0, max_val=NE - 1)
                        sp.wait_ge(b_filled, 2 * it + (NE - 1 + b))
                        sp.dma_start(w13[b][0], w1_e[e]).then_inc(OV_W_IN[b], 16)
                        sp.dma_start(w13[b][1], w3_e[e]).then_inc(OV_W_IN[b], 16)
                        sp.wait_ge(y_filled, 2 * it + (NE - 1 + b))
                        sp.dma_start(w2s[b], w2_e[e]).then_inc(OV_W_IN[b], 16)

        @block.gpsimd
        def _(pool):
            seq = [0]

            def link(ins):
                seq[0] += 1
                ins.then_inc(pool_seq, 1)
                pool.wait_ge(pool_seq, seq[0])

            def settle():
                pool.sem_inc(pool_steps, 1)

            def rms(col_in, col_out, n, width, eps, what):
                link(pool.tensor_scalar(st[:, col_out:col_out + width], st[:, col_in:col_in + width],
                                        1.0 / n, eps, ALU.mult, ALU.add))
                pool.tensor_tensor(st[:, col_out:col_out + width], st[:, col_out:col_out + width],
                                   minus_half[:, 0:width], ALU.pow).then_inc(what, 1)

            pool.memset(minus_half[:, :], -0.5)
            pool.memset(halfpi[:, :], PI / 2)
            for k in range(HR):
                pool.memset(freq[:, k:k + 1], float(np.float32(10000.0 ** (-2.0 * k / RD))))
            for k in range(8):
                pool.memset(wrank[:, k:k + 1], 8.0 - k)
            pool.memset(ones[:, :], 1.0)
            pool.memset(before[:, :], 1.0)
            pool.memset(upad[:, :, 0:TAPS - 1], 0.0)
            pool.iota(iota_j[:, :], [[1, P]], base=0, channel_multiplier=0, allow_small_or_imprecise_dtypes=True)
            pool.iota(eiota[:, :], [[1, NE]], base=0, channel_multiplier=0, allow_small_or_imprecise_dtypes=True)
            for k in range(2):
                pool.iota(pay[:, :, k, 0], [[1, NT]], base=0, channel_multiplier=NT)
            pool.memset(tabi[:, :, :], SKIP_ROW)
            link(pool.memset(ident[:, :], 0.0))
            pool.affine_select(out=ident[:, :], in_=ident[:, :], compare_op=ALU.not_equal, fill=1.0,
                               base=0, pattern=[[-1, P]], channel_multiplier=1)
            link(pool.affine_select(out=before[:, :], in_=before[:, :], compare_op=ALU.is_gt, fill=0.0,
                                    base=0, pattern=[[1, P]], channel_multiplier=-1))
            pool.tensor_tensor(dmask[:, :], ident[0:2 * C, 0:C], ident[0:2 * C, C:2 * C], ALU.add).then_inc(consts_made, 1)
            pool.memset(toep, 0.0).then_inc(consts_made, 1)
            pool.wait_ge(consts_made, 2)
            pool.dma_start(tab_d.rearrange("(p b) k -> p b k", p=P), tabi[:, :, :]).then_inc(tab_cleared, 16)

            for i in range(NT):
                pool.wait_ge(x_squared, i + 1)
                rms(i, 8 + i, D, 1, EPS, x_rms)
            with nc.allow_non_contiguous_dma(reason="parameters of a few KiB"):
                for k, v in enumerate((ln_w, ln_b)):
                    pool.dma_start(lnwb[:, k, :], v[0].partition_broadcast(P)).then_inc(row_par_in, 16)
                for k, v in enumerate((q_norm, k_norm)):
                    pool.dma_start(qkw[:, k, :], v[0].partition_broadcast(P)).then_inc(row_par_in, 16)
                pool.dma_start(wr[:, :, 0:EG], w_grp[0].rearrange("(c p) n -> p c n", p=P)).then_inc(row_par_in, 16)
                pool.dma_start(wr[:, :, EG:EG + NE], w_exp[0].rearrange("(c p) n -> p c n", p=P)).then_inc(row_par_in, 16)
                pool.dma_start(brow[:, 0:EG], b_grp[0].partition_broadcast(P)).then_inc(row_par_in, 16)
                pool.dma_start(brow[:, EG:EG + NE], b_exp[0].partition_broadcast(P)).then_inc(row_par_in, 16)

            for half in range(2):
                for m in range(2):
                    pool.wait_ge(lo_drained, F_AG(half, 2 * m + 1) + 1)
                    v = natural(upad[:, m, TAPS - 1:PADW], half)
                    pool.tensor_tensor(v, v, natural(sigT[:, m, :], half), ALU.mult).then_inc(upad_ready, 1)
            pool.wait_ge(wproj_in, 16 * 3)
            for c in range(2):
                pool.tensor_scalar(wuq[:, c, :], wuq[:, c, :], normc[:, 2 * KC + c:2 * KC + c + 1], None, ALU.mult)
            pool.tensor_scalar(wukv, wukv, normc[:, 2 * KC + 2:2 * KC + 3], None, ALU.mult).then_inc(wproj_scaled, 1)
            pool.wait_ge(lo_drained, F_SSQ + 1)
            rms(16, 32, QL, NT, EPS, lat_rms)
            rms(24, 40, KL, NT, EPS, lat_rms)
            def square_qk(i):
                pool.wait_ge(qk_saved, i + 1)
                if i >= 2:
                    pool.wait_ge(qk_summed, i - 1)
                qv = qraw[:, i, :].rearrange("p (h d) -> p h d", d=QH)
                kv = kraw[:, i, :].rearrange("p (h d) -> p h d", d=ND)
                pool.tensor_tensor(sqq[i % 2], qv, qv, ALU.mult)
                pool.tensor_tensor(sqk[i % 2], kv, kv, ALU.mult).then_inc(qk_squared, 1)

            for i in range(6):
                square_qk(i)
            pool.wait_ge(ln_stats, 1)
            link(pool.tensor_scalar(st[:, 112:112 + NT], bns[:, :, 7], 1.0, LN_EPS, ALU.mult, ALU.add))
            pool.tensor_tensor(st[:, 112:112 + NT], st[:, 112:112 + NT], minus_half[:, 0:NT], ALU.pow).then_inc(ln_rstd, 1)
            for i in range(6, NT):
                square_qk(i)
            pool.wait_ge(mid_squared, 1)
            rms(64, 72, CW, NT, EPS, mid_rms)
            pool.wait_ge(mid_squared, 2)
            rms(48, 56, SW, NT, EPS, mid_rms)
            pool.wait_ge(heads_made, 2)
            with pool.Fori(1, H // 2) as it:
                pool.wait_ge(qkT_made, 2 * it)
                for b in range(2):
                    n = [b * LINKS]

                    def hlink(ins):
                        n[0] += 1
                        ins.then_inc(head_seq, 1)
                        pool.wait_ge(head_seq, (it - 1) * (2 * LINKS) + n[0])

                    for a in range(2):
                        make_heads_part(pool, hlink, settle, 2 * it + b, b, a, rot)
                    assert n[0] == (b + 1) * LINKS
                    pool.sem_inc(heads_made, 1)

            pool.wait_ge(wout_in, 16)
            for c in range(KC):
                last = pool.tensor_scalar(wout[:, c, :], wout[:, c, :], normc[:, KC + c:KC + c + 1], None, ALU.mult)
            last.then_inc(wout_scaled, 1)
            pool.wait_ge(o_squared, NT)
            rms(80, 88, AW, NT, EPS, o_rms)
            for i in range(NT):
                pool.wait_ge(x2_squared, i + 1)
                rms(96 + i, 104 + i, D, 1, EPS, x2_rms)

            pool.wait_ge(tab_cleared, 16)
            pool.wait_ge(slots_ready, 1)
            for i in range(NT):
                for k in range(2):
                    pool.indirect_dma_start(out=tab_d, out_offset=bass.IndirectOffsetOnAxis(ap=slot[:, i, k:k + 1], axis=0),
                                            in_=pay[:, i, k, :], in_offset=None).then_inc(tab_rows_out, 16)
            for b in range(2):
                link(pool.memset(xg[b], 0.0))
            pool.wait_ge(tab_in, 16)
            for b in range(2):
                pool.wait_ge(H2_OUT[b], 8 * NT)

            def gather(b, e):
                pool.tensor_copy(idx[:, b, :], tabi[:, bass.ds(e, 1), :].rearrange("p a k -> p (a k)")).then_inc(idxg_copied, 1)
                pool.wait_ge(idxg_copied, e + 1)
                settle()
                pool.indirect_dma_start(out=xg[b], out_offset=None, in_=h2_d,
                                        in_offset=bass.IndirectOffsetOnAxis(ap=idx[:, b, 0:1], axis=0),
                                        bounds_check=T - 1, oob_is_err=False).then_inc(ROWS_IN[b], 16)

            def prepare(b, e):
                pool.tensor_copy(idx[:, 2 + b, :], tabi[:, bass.ds(e, 1), :].rearrange("p a k -> p (a k)")).then_inc(idxs_copied, 1)

            def scatter(b, e):
                pool.wait_ge(y_saved_a, e + 2)
                pool.wait_ge(y_saved_v, e + 2)
                settle()
                pool.indirect_dma_start(out=out_d, out_offset=bass.IndirectOffsetOnAxis(ap=idx[:, 2 + b, 0:1], axis=0),
                                        in_=ye[b], in_offset=None, bounds_check=T - 1, oob_is_err=False,
                                        compute_op=ALU.add).then_inc(Y_OUT[b], 16)

            prepare(0, 0)
            gather(0, 0)
            gather(1, 1)
            for e in range(2):
                pool.wait_ge(xgT_filled, e + 1)
                gather(e, e + 2)
            pool.wait_ge(out_stored, 16 * NT)

            def two_blocks(it):
                for b in range(2):
                    e = 2 * it + b
                    pool.wait_ge(xgT_filled, e + 1)
                    settle()
                    gather(b, e + 2)
                    if b == 1:
                        pool.wait_ge(Y_OUT[0], 16 * it)
                    elif not isinstance(it, int):
                        pool.wait_ge(Y_OUT[1], 16 * (it - 1))
                    settle()
                    prepare(1 - b, e - 1)
                    scatter(b, e - 2)

            two_blocks(1)
            with pool.Fori(2, NE // 2 - 1) as it:
                two_blocks(it)
            n_ov = pool.value_load(ovi[0:1, OVF:OVF + 1], min_val=0, max_val=OVF)
            for e in range(NE - 2, NE + 2):
                b = e % 2
                if e < NE:
                    with pool.If(n_ov > b):
                        pool.wait_ge(xgT_filled, e + 1)
                        gather(b, e + 2)
                pool.wait_ge(Y_OUT[1 - b], 16 * ((e - 2 - b) // 2 + b))
                prepare(1 - b, e - 1)
                scatter(b, e - 2)
            pool.wait_ge(Y_OUT[1], 8 * NE)
            with pool.Fori(0, OVF // 2) as it:
                for b in range(2):
                    with pool.If(n_ov > 2 * it + b):
                        with pool.If(n_ov > 2 * it + (b + 2)):
                            pool.wait_ge(xgT_filled, 2 * it + (NE + b + 1))
                            settle()
                            gather(b, 2 * it + (NE + b + 2))
                        prepare(1 - b, 2 * it + (NE + b + 1))
                        scatter(b, 2 * it + (NE + b))
                        pool.wait_ge(Y_OUT[b], 16 * it + 16 * (NE // 2 + 1))
                        settle()

        @block.scalar
        def _(act):
            seq = [0]

            def link(ins):
                seq[0] += 1
                ins.then_inc(act_seq, 1)
                act.wait_ge(act_seq, seq[0])

            def lo(n):
                return psum[:, n % 4, :]

            def save_xT(i):
                for k in range(2):
                    act.wait_ge(lo_filled, F_XT(i, k) + 1)
                    act.activation(hT[:, 4 * k:4 * k + 4, i, :], lo(F_XT(i, k)).rearrange("p (c j) -> p c j", c=4),
                                   ACT.Copy).then_inc(lo_drained, 1)

            def square_x(i):
                if i % 2 == 0:
                    act.wait_ge(X_IN[i // 2], 16)
                if i >= 1:
                    act.wait_ge(x_squared, i)
                act.activation(tmp, xin[i // 2][:, i % 2, :], ACT.Square, accum_out=st[:, i:i + 1]).then_inc(x_squared, 1)

            square_x(0)
            for i in range(NT):
                if i + 1 < NT:
                    square_x(i + 1)
                act.wait_ge(x_rms, i + 1)
                act.activation(xin[i // 2][:, i % 2, :], xin[i // 2][:, i % 2, :], ACT.Copy, scale=st[:, 8 + i:9 + i]).then_inc(x_normed, 1)
                if i >= 1:
                    save_xT(i - 1)
            save_xT(NT - 1)
            act.wait_ge(trig_ready, 1)
            act.activation(sc[:, 7, :], sc[:, 5, :], ACT.Sin, scale=0.5)
            act.activation(sc[:, 8, :], sc[:, 5, :], ACT.Sin).then_inc(trig_done, 1)
            act.wait_ge(consts_made, 1)
            act.wait_ge(phase_ready, 1)
            act.activation(sinj, sinj, ACT.Sin, scale=TWO_PI_SAFE)
            act.activation(cosj, cosj, ACT.Sin, scale=-TWO_PI_SAFE, bias=halfpi[:, 0:1]).then_inc(tables_made, 1)
            act.wait_ge(rope_ang, 1)
            for k in range(2):
                act.activation(rope[:, k, :, HR:RD], rope[:, k, :, 0:HR], ACT.Sin,
                               **(dict(scale=-1.0, bias=halfpi[:, 0:1]) if k == 0 else {})).then_inc(rope_made, 1)
            for half in range(2):
                for m in range(2):
                    n = F_AG(half, 2 * m)
                    act.wait_ge(lo_filled, n + 1)
                    act.activation(natural(sigT[:, m, :], half), lo(n).rearrange("p (i j) -> p i j", i=4),
                                   ACT.Sigmoid).then_inc(lo_drained, 1)
                    act.wait_ge(lo_filled, n + 2)
                    act.activation(natural(upad[:, m, TAPS - 1:PADW], half), lo(n + 1).rearrange("p (i j) -> p i j", i=4),
                                   ACT.Copy).then_inc(lo_drained, 1)
            act.wait_ge(hi_filled, R_W + 1)
            for k in range(4):
                last = act.activation(WT[:, k // 2, 4 * (k % 2):4 * (k % 2) + 4, :],
                                      psum[:, 4 + k, :].rearrange("p (r n) -> p r n", r=4), ACT.Copy)
            last.then_inc(hi_drained, 1)
            act.wait_ge(ssm_w_ready, 1)
            for i in range(NT):
                n = F_U(i)
                act.wait_ge(lo_filled, n + 1)
                act.activation(kst[:, i, :], lo(n)[:, 0:RD], ACT.Copy)
                act.activation(utok[:, :, i, :], lo(n)[:, RD:RD + SW].rearrange("p (g c) -> p g c", c=C),
                               ACT.Copy).then_inc(lo_drained, 1)
            act.wait_ge(hi_filled, R_H + 1)
            for k in range(2):
                last = act.activation(Hk[:, 4 * k:4 * k + 4, :, :].rearrange("p r t c -> p r (t c)"),
                                      psum[0:2 * C, 4 + k, :].rearrange("p (r n) -> p r n", r=4), ACT.Copy)
            last.then_inc(hi_drained, 1)
            act.wait_ge(hi_filled, R_U + 1)
            for k in range(4):
                last = act.activation(U[:, 4 * k:4 * k + 4, :], psum[:, 4 + k, :].rearrange("p (g j) -> p g j", g=4), ACT.Copy)
            last.then_inc(hi_drained, 1)
            act.wait_ge(upad_ready, 4)
            for half in range(2):
                for m in range(3):
                    n = F_LAT(half, m)
                    act.wait_ge(lo_filled, n + 1)
                    dst = cqT[:, m, :] if m < 2 else ckvT
                    act.activation(natural(dst, half), lo(n).rearrange("p (i j) -> p i j", i=4), ACT.Copy).then_inc(lo_drained, 1)
            act.wait_ge(lo_drained, F_LAT(1, 2) + 1)
            for m in range(3):
                last = act.activation(sqc[:, m, :], cqT[:, m, :] if m < 2 else ckvT, ACT.Square)
            last.then_inc(lat_squared, 1)
            act.wait_ge(lo_filled, F_SSQ + 1)
            act.activation(st[:, 16:16 + 2 * NT], lo(F_SSQ)[:, 0:2 * NT], ACT.Copy).then_inc(lo_drained, 1)
            act.wait_ge(lat_rms, 2)

            def save_qkv(i):
                for k in range(2):
                    n = F_QKV(i, k)
                    act.wait_ge(lo_filled, n + 1)
                    act.activation(qraw[:, i, k * 384:k * 384 + 384], lo(n)[:, 0:384], ACT.Copy,
                                   scale=st[:, 32 + i:33 + i]).then_inc(lo_drained, 1)
                for k in range(2):
                    n = F_QKV(i, 2 + k)
                    act.wait_ge(lo_filled, n + 1)
                    v = lo(n).rearrange("p (h d) -> p h d", d=ND + VD)
                    for dst, d0 in ((kraw, 0), (vtok, ND)):
                        last = act.activation(dst[:, i, k * 256:k * 256 + 256].rearrange("p (h d) -> p h d", d=ND),
                                              v[:, :, d0:d0 + ND], ACT.Copy, scale=st[:, 40 + i:41 + i])
                    link(last)
                    act.sem_inc(lo_drained, 1)
                act.sem_inc(qk_saved, 1)

            for i in range(4):
                save_qkv(i)
            act.wait_ge(ssm_x_ready, 1)
            act.wait_ge(hi_filled, R_Y + 1)
            z_v = yssm.rearrange("p t (r h c) -> p h r t c", h=2, c=C)
            for h in range(2):
                for k in range(2):
                    for t4 in range(4):
                        last = act.activation(z_v[:, h, 4 * k + t4, :, :],
                                              psum[:, 4 + 2 * h + k, t4 * P:(t4 + 1) * P].rearrange("p (t c) -> p t c", c=C),
                                              ACT.Gelu_apprx_tanh)
            link(last)
            act.sem_inc(z_ready, 1)
            act.sem_inc(hi_drained, 1)
            for i in range(4, NT):
                save_qkv(i)
            act.wait_ge(hi_filled, R_Z + 1)
            for k in range(4):
                last = act.activation(zT.rearrange("p c (k i j) -> p k i c j", k=4, i=2)[:, k],
                                      psum[:, 4 + k, :].rearrange("p (i c j) -> p i c j", i=2, c=2), ACT.Copy)
            last.then_inc(hi_drained, 1)
            act.wait_ge(ln_done, 1)
            link(act.activation(ctok, ctok, ACT.Silu))
            for i in range(NT):
                link(act.activation(tmp[:, 0:CW], ctok[:, i, :], ACT.Square, accum_out=st[:, 64 + i:65 + i]))
            act.sem_inc(mid_squared, 1)
            act.wait_ge(qk_mean, 1)
            act.activation(at(14336 + 2816, 2 * NT * H), qks.rearrange("p a i h -> p (a i h)"), ACT.Sqrt).then_inc(qk_root, 1)
            act.wait_ge(hi_filled, R_GLU + 1)
            for k in range(4):
                last = act.activation(sout[:, 2 * k:2 * k + 2, :], psum[:, 4 + k, :].rearrange("p (i n) -> p i n", i=2), ACT.Sigmoid)
            link(last)
            act.sem_inc(hi_drained, 1)
            act.sem_inc(sigm_done, 1)
            act.wait_ge(mid_rms, 1)
            for i in range(NT):
                last = act.activation(ctok[:, i, :], ctok[:, i, :], ACT.Copy, scale=st[:, 72 + i:73 + i])
            link(last)
            act.sem_inc(mid_scaled, 1)
            act.wait_ge(glu_done, 1)
            for i in range(NT):
                link(act.activation(tmp[:, 0:SW], sout[:, i, :], ACT.Square, accum_out=st[:, 48 + i:49 + i]))
            act.sem_inc(mid_squared, 1)
            act.wait_ge(mid_rms, 2)
            for i in range(NT):
                last = act.activation(sout[:, i, :], sout[:, i, :], ACT.Copy, scale=st[:, 56 + i:57 + i])
            link(last)
            act.sem_inc(mid_scaled, 1)
            for r, c0 in ((R_COUT, 2), (R_SOUT, 0)):
                act.wait_ge(hi_filled, r + 1)
                for k in range(4):
                    last = act.activation(yT[:, c0:c0 + 2].rearrange("p c (k i) j -> p k i c j", k=4)[:, k],
                                          psum[:, 4 + k, :].rearrange("p (i c j) -> p i c j", i=2, c=2), ACT.Copy)
                last.then_inc(hi_drained, 1)
            act.wait_ge(hi_drained, R_SOUT + 1)
            act.sem_inc(mid_done, 1)

            with act.Fori(0, H // 2) as it:
                it16, itF = act.snap(STEPS * it), act.snap(FILLS * it)
                ita, itv = act.snap(saved_a[FILLS] * it), act.snap(saved_v[FILLS] * it)

                def save_kT(b):
                    act.wait_ge(qkT_made, 2 * it + (b + 1))
                    last = act.activation(kT[b][0:QH, :].rearrange("p (k n) -> p k n", k=2), psum[0:QH, 4 * b + 2:4 * b + 4, :], ACT.Copy)
                    last.then_inc(kT_saved, 1)

                def exponentials(n):
                    act.wait_ge(s_max, it16 + (n + 1))
                    if n >= 2:
                        act.wait_ge(pT_filled, itF + first_fill[n - 1])
                    i, a = tile_of[n], am[:, n % 4, :]
                    L = (i + 1) * P
                    act.activation(prob[n % 2][:, 0:L], psum[:, 2 * (n % 2):2 * (n % 2) + 2, :].rearrange("p a n -> p (a n)")[:, 0:L],
                                   ACT.Exp, bias=a[:, 0:1], accum_out=a[:, 1:2]).then_inc(p_ready, 1)

                for b in range(2):
                    save_kT(b)
                exponentials(0)
                exponentials(1)
                for n in range(STEPS):
                    for f in range(first_fill[n], first_fill[n + 1]):
                        if not by_dve[f]:
                            act.wait_ge(pT_filled, itF + (f + 1))
                            w = min(4, tile_of[n] + 1 - 4 * (f - first_fill[n]))
                            if f >= 4:
                                act.wait_ge(pv_done, itF + (f - 3))
                            act.activation(probT[f % 4][:, 0:w, :], psum[:, 4 + f % 2, 0:w * P].rearrange("p (a n) -> p a n", n=P),
                                           ACT.Copy).then_inc(pT_saved_a, 1)
                    if n + 2 < STEPS:
                        exponentials(n + 2)

            act.wait_ge(o_saved, H * NT)
            for i in range(NT):
                link(act.activation(prob[0][:, 0:AW], otok[:, i, :], ACT.Square, accum_out=st[:, 80 + i:81 + i]))
            act.sem_inc(o_squared, NT)
            act.wait_ge(o_rms, 1)
            for i in range(NT):
                act.activation(otok[:, i, :], otok[:, i, :], ACT.Copy, scale=st[:, 88 + i:89 + i]).then_inc(o_scaled, 1)
            for i in range(NT):
                act.wait_ge(oT_filled, i + 1)
                for c in range(4):
                    last = act.activation(oT[:, c, :, 16 * i:16 * i + 16].rearrange("p i j -> p j i"),
                                          psum[:, i % 4, c * P:(c + 1) * P].rearrange("p (j i) -> p j i", i=NT), ACT.Copy)
                last.then_inc(oT_saved, 1)
            for i in range(NT + 1):
                if i < NT:
                    act.wait_ge(x2_ready, i + 1)
                    link(act.activation(junk, x2[:, i, :], ACT.Square, accum_out=st[:, 96 + i:97 + i]))
                    act.sem_inc(x2_squared, 1)
                if i >= 1:
                    act.wait_ge(h2T_filled, i)
                    act.activation(h2T.rearrange("p (k c) n -> p k (c n)", k=2), psum[:, 4:6, :], ACT.Copy).then_inc(h2T_saved, 1)
            act.wait_ge(expg_in, 1)
            act.activation(expg, expg, ACT.Exp).then_inc(expg_done, 1)
            act.wait_ge(expe_in, 1)
            act.activation(expe, expe, ACT.Exp).then_inc(expe_done, 1)

            def save_xgT(e):
                act.wait_ge(xgT_filled, e + 1)
                act.activation(xgT.rearrange("p (k c) n -> p k (c n)", k=2), psum[:, 3:5, :], ACT.Copy).then_inc(xgT_saved, 1)

            def silu(e):
                if not isinstance(e, int) or e >= 1:
                    act.wait_ge(he_ready, e)
                act.wait_ge(a_filled, e + 1)
                act.activation(sil, psum[:, 0, :], ACT.Silu).then_inc(silu_e, 1)

            def save_y(b, e):
                act.wait_ge(idxs_copied, e + 1)
                act.wait_ge(y_filled, e + 1)
                act.activation(ye[b][:, 0:512], psum[:, 5, :], ACT.Copy, scale=idx[:, 2 + b, 1:2].bitcast(F32)).then_inc(y_saved_a, 1)

            act.sem_inc(y_saved_a, 1)
            save_xgT(0)
            silu(0)
            save_xgT(1)

            with act.Fori(0, NE // 2 - 1) as it:
                for b in (1, 0):
                    e = 2 * it + (2 - b)
                    silu(e)
                    save_xgT(e + 1)
                    save_y(1 - b, e - 1)
            silu(NE - 1)
            save_y(0, NE - 2)
            save_y(1, NE - 1)
            n_ov = act.value_load(ovi[0:1, OVF:OVF + 1], min_val=0, max_val=OVF)
            with act.Fori(0, OVF // 2) as it:
                for b in range(2):
                    with act.If(n_ov > 2 * it + b):
                        e = 2 * it + (NE + b)
                        save_xgT(e)
                        silu(e)
                        save_y(b, e)

        @block.vector
        def _(dve):
            seq = [0]

            def link(ins):
                seq[0] += 1
                ins.then_inc(dve_seq, 1)
                dve.wait_ge(dve_seq, seq[0])

            def tt(out_, a, b_, op):
                link(dve.tensor_tensor(out_, a, b_, op))

            def ts(out_, a, s1, s2, op0, op1=None):
                link(dve.tensor_scalar(out_, a, s1, s2, op0, *(() if op1 is None else (op1,))))

            def stt(out_, a, s1, b_, op0, op1):
                link(dve.scalar_tensor_tensor(out_, a, s1, b_, op0, op1))

            def v(k):
                return sc[:, k, :]

            M_, A_, S_ = ALU.mult, ALU.add, ALU.subtract

            dve.wait_ge(ssm_par_in, 16 * 11)
            lr, li = lamc[:, 0, :], lamc[:, 1, :]
            ts(v(0), lamc[:, 2, :], 1.0 / 16, None, M_)
            ts(v(1), v(0), 1.0 / 9, 1.0, M_, A_)
            for k in range(8, 0, -1):
                tt(v(1), v(1), v(0), M_)
                ts(v(1), v(1), 1.0 / k, 1.0, M_, A_)
            for _ in range(4):
                tt(v(1), v(1), v(1), M_)
            tt(v(2), lr, v(1), M_)
            ts(v(3), v(2), -20.0, 1.0 / 16, ALU.max, M_)
            ts(v(4), v(3), 1.0 / 7, 1.0, M_, A_)
            for k in range(6, 1, -1):
                tt(v(4), v(4), v(3), M_)
                ts(v(4), v(4), 1.0 / k, 1.0, M_, A_)
            tt(v(4), v(4), v(3), M_)
            for _ in range(4):
                stt(v(4), v(4), 2.0, v(4), A_, M_)

            def reduce_angle(x_, turns):
                ts(turns, x_, 1.0 / (2 * PI), ROUND, M_, A_)
                ts(turns, turns, ROUND, None, S_)
                stt(x_, turns, -TWO_PI_HI, x_, M_, A_)
                stt(x_, turns, -TWO_PI_LO, x_, M_, A_)
                ts(x_, x_, 3.1415925, -3.1415925, ALU.min, ALU.max)

            tt(v(5), li, v(1), M_)
            reduce_angle(v(5), v(6))
            dve.sem_inc(trig_ready, 1)
            ts(v(10), v(5), float(STEP), None, M_)
            reduce_angle(v(10), v(11))
            ts(v(10), v(10), 1.0 / (2 * PI), None, M_)
            ts(v(11), v(10), ROUND16, None, A_)
            ts(v(11), v(11), ROUND16, None, S_)
            tt(v(12), v(10), v(11), S_)
            dve.wait_ge(consts_made, 1)
            jb = iota_j[:, :].unsqueeze(1).to_broadcast([P, NPAIR, NJ])

            def wide(col):
                return col.unsqueeze(2).to_broadcast([P, NPAIR, NJ])

            tt(sinj, wide(v(11)), jb, M_)
            ts(cosj, sinj, ROUND, None, A_)
            ts(cosj, cosj, ROUND, None, S_)
            tt(sinj, sinj, cosj, S_)
            tt(cosj, wide(v(12)), jb, M_)
            tt(sinj, sinj, cosj, A_)
            ts(cosj, sinj, ROUND, None, A_)
            ts(cosj, cosj, ROUND, None, S_)
            tt(sinj, sinj, cosj, S_)
            ts(sinj, sinj, 0.5, -0.5, ALU.min, ALU.max)
            fl = "p r j -> p (r j)"
            stt(cosj.rearrange(fl), sinj.rearrange(fl), -1.0, sinj.rearrange(fl), M_, ALU.max)
            dve.sem_inc(phase_ready, 1)
            dve.wait_ge(small_par_in, 16 * 8)
            link(dve.tensor_copy(posf[:, :], posi[:, :]))
            ang, turns = rope[:, 1, :, 0:HR], rope[:, 0, :, 0:HR]
            tt(ang, posf[:, :].unsqueeze(2).to_broadcast([P, NT, HR]),
               freq[:, :].unsqueeze(1).to_broadcast([P, NT, HR]), M_)
            reduce_angle(ang, turns)
            stt(turns, ang, -1.0, ang, M_, ALU.max)
            dve.sem_inc(rope_ang, 1)
            for arrived, c0, c1 in ((win_ag_in, A0, NIN), (win_rest_in, 0, A0)):
                dve.wait_ge(arrived, 16)
                for c in range(KC):
                    last = dve.tensor_scalar(win[:, c, c0:c1], win[:, c, c0:c1], normc[:, c:c + 1], None, M_)
                last.then_inc(win_scaled, 1)
            dve.wait_ge(trig_done, 1)
            tt(v(7), v(7), v(7), M_)
            ts(v(7), v(7), -2.0, None, M_)
            stt(v(9), v(7), 1.0, v(4), A_, M_)
            tt(v(9), v(9), v(7), A_)
            link(dve.memset(Lp[:, 0, 0, :], 1.0))
            link(dve.memset(Lp[:, 1, 0, :], 0.0))
            ts(Lp[:, 0, 1, :], v(9), 1.0, None, A_)
            stt(Lp[:, 1, 1, :], v(4), 1.0, v(8), A_, M_)

            def lpow(k, n):
                a = [Lp[:, c, 1:1 + n, :] for c in range(2)]
                m = [Lp[:, c, k:k + 1, :].to_broadcast([P, n, NPAIR]) for c in range(2)]
                o = [Lp[:, c, k + 1:k + 1 + n, :] for c in range(2)]
                t_ = sc[:, 14:14 + n, :]
                tt(o[0], a[0], m[0], M_)
                tt(t_, a[1], m[1], M_)
                tt(o[0], o[0], t_, S_)
                tt(o[1], a[0], m[1], M_)
                tt(t_, a[1], m[0], M_)
                tt(o[1], o[1], t_, A_)

            lpow(1, 1)
            lpow(2, 2)
            lpow(4, 4)
            for t in range(STEP):
                link(dve.tensor_copy(Lv[:, :, t, :], Lp[:, :, STEP - 1 - t, :]))
            ts(v(13), v(4), 1.0, None, A_)
            for _ in range(3):
                tt(v(13), v(13), v(13), M_)
            link(dve.tensor_copy(decay, wide(v(13))))
            link(dve.memset(decay[:, :, 0:1], 0.0))
            tt(v(14), lr, lr, M_)
            tt(v(15), li, li, M_)
            tt(v(14), v(14), v(15), A_)
            link(dve.reciprocal(v(14), v(14)))
            tt(v(18), v(9), lr, M_)
            tt(v(15), Lp[:, 1, 1, :], li, M_)
            tt(v(18), v(18), v(15), A_)
            tt(v(18), v(18), v(14), M_)
            tt(v(19), Lp[:, 1, 1, :], lr, M_)
            tt(v(15), v(9), li, M_)
            tt(v(19), v(19), v(15), S_)
            tt(v(19), v(19), v(14), M_)

            def cmul(out_, a, b_, t_):
                tt(out_[0], a[0], b_[0], M_)
                tt(t_, a[1], b_[1], M_)
                tt(out_[0], out_[0], t_, S_)
                tt(out_[1], a[0], b_[1], M_)
                tt(t_, a[1], b_[0], M_)
                tt(out_[1], out_[1], t_, A_)

            T4 = at(S0 + 8192 - 2048, NPAIR, STEP, C)
            cmul([Bb[:, k] for k in range(2)], [v(k).unsqueeze(2).to_broadcast([P, NPAIR, C]) for k in (18, 19)],
                 [Braw[:, k] for k in range(2)], T4[:, :, 0, :])
            cmul([W[:, k] for k in range(2)],
                 [Lv[:, k].rearrange("p t r -> p r t").unsqueeze(3).to_broadcast([P, NPAIR, STEP, C]) for k in range(2)],
                 [Bb[:, k].unsqueeze(2).to_broadcast([P, NPAIR, STEP, C]) for k in range(2)], T4)
            link(dve.memset(Bz, 0.0))
            for h in range(2):
                link(dve.tensor_copy(Bz[h * S:(h + 1) * S, :, :, h, :], Bb[h * S:(h + 1) * S]))
            dve.sem_inc(ssm_w_ready, 1)
            dve.wait_ge(hi_filled, R_C + 1)
            link(dve.tensor_copy(CTt.rearrange("p a r c -> p a (r c)"), psum[:, 4, 0:2 * P].rearrange("p (a n) -> p a n", a=2)))
            dve.sem_inc(hi_drained, 1)
            T5 = at(S0 + 6144, NPAIR, STEP + 1, C)
            Cb = [CTt[:, k].unsqueeze(2).to_broadcast([P, NPAIR, STEP + 1, C]) for k in range(2)]
            Lb = [Lp[:, k].rearrange("p t r -> p r t").unsqueeze(3).to_broadcast([P, NPAIR, STEP + 1, C]) for k in range(2)]
            tt(CL[:, 0], Cb[0], Lb[0], M_)
            tt(T5, Cb[1], Lb[1], M_)
            tt(CL[:, 0], CL[:, 0], T5, S_)
            tt(CL[:, 1], Cb[0], Lb[1], M_)
            tt(T5, Cb[1], Lb[0], M_)
            flat = "p r t c -> p (r t c)"
            stt(CL[:, 1].rearrange(flat), CL[:, 1].rearrange(flat), -1.0, T5.rearrange(flat), M_, S_)
            dve.sem_inc(ssm_c_ready, 1)
            dve.wait_ge(rope_made, 2)
            link(dve.tensor_copy(rope[:, 0, :, 0:HR], rope[:, 0, :, HR:RD]))
            ts(rope[:, 1, :, 0:HR], rope[:, 1, :, HR:RD], -1.0, None, M_)
            dve.sem_inc(rope_made, 1)
            dve.wait_ge(upad_ready, 4)
            dve.wait_ge(hi_filled, R_W + 1)
            base, n = seq[0], 0
            for k in range(TAPS):
                for m in range(2):
                    if n >= 2:
                        dve.wait_ge(dve_seq, base + n - 1)
                    src = upad[:, m, k:k + T]
                    if k == 0:
                        ins = dve.tensor_scalar(cacc[:, m, :], src, dwc[:, m, 0:1], dwc[:, m, TAPS:TAPS + 1], M_, A_)
                    elif k < TAPS - 1:
                        ins = dve.scalar_tensor_tensor(cacc[:, m, :], src, dwc[:, m, k:k + 1], cacc[:, m, :], M_, A_)
                    else:
                        ins = dve.scalar_tensor_tensor(cperm[:, m].rearrange("p i j -> p j i"), src.rearrange("p (j i) -> p j i", i=NT),
                                                       dwc[:, m, k:k + 1], cacc[:, m, :].rearrange("p (j i) -> p j i", i=NT), M_, A_)
                    ins.then_inc(dve_seq, 1)
                    n += 1
            seq[0] += n
            dve.wait_ge(dve_seq, seq[0])
            dve.sem_inc(conv_done, 1)

            dve.wait_ge(consts_made, 2)
            dd = at(YT0 + 1864, NPAIR, C, parts=2 * C)
            tt(dd, dmask[:, :].unsqueeze(1).to_broadcast([2 * C, NPAIR, C]),
               dch[:, :].unsqueeze(2).to_broadcast([2 * C, NPAIR, C]), M_)
            dve.wait_ge(hi_drained, R_H + 1)
            tt(Hk[:, :, 0, :], Hk[:, :, 0, :], dd, A_)
            dve.sem_inc(hk_saved, 1)

            dve.wait_ge(hi_filled, R_V + 1)
            dve.wait_ge(tables_made, 1)
            Vp = [psum[:, 4 + 2 * k:6 + 2 * k, :].rearrange("p a (r j) -> p (a r) j", j=NJ) for k in range(2)]
            tmp3 = tmp.rearrange("p (r j) -> p r j", j=NJ)
            tt(Vrot[:, 0], Vp[0], cosj, M_)
            tt(tmp3, Vp[1], sinj, M_)
            tt(Vrot[:, 0], Vrot[:, 0], tmp3, A_)
            tt(Vrot[:, 1], Vp[1], cosj, M_)
            tt(tmp3, Vp[0], sinj, M_)
            dve.sem_inc(hi_drained, 1)
            tt(Vrot[:, 1], Vrot[:, 1], tmp3, S_)
            for k in range(2):
                link(dve.tensor_tensor_scan(Zs[:, k].rearrange("p r j -> p (r j)"), decay.rearrange("p r j -> p (r j)"),
                                            Vrot[:, k].rearrange("p r j -> p (r j)"), 0.0, M_, A_))
            z_ = [Zs[:, k, :, 0:NJ - 1] for k in range(2)]
            cs_, sn_ = cosj[:, :, 0:NJ - 1], sinj[:, :, 0:NJ - 1]
            for k in range(2):
                link(dve.memset(Xp[:, k, :, 0:1], 0.0))
            tt(Xp[:, 0, :, 1:NJ], z_[0], cs_, M_)
            tt(tmp3[:, :, 1:NJ], z_[1], sn_, M_)
            tt(Xp[:, 0, :, 1:NJ], Xp[:, 0, :, 1:NJ], tmp3[:, :, 1:NJ], S_)
            tt(Xp[:, 1, :, 1:NJ], z_[0], sn_, M_)
            tt(tmp3[:, :, 1:NJ], z_[1], cs_, M_)
            tt(Xp[:, 1, :, 1:NJ], Xp[:, 1, :, 1:NJ], tmp3[:, :, 1:NJ], A_)
            dve.sem_inc(ssm_x_ready, 1)

            def sum_qk(i):
                dve.wait_ge(qk_squared, i + 1)
                link(dve.reduce_sum(qks[:, 0, i, :], sqq[i % 2], AX))
                link(dve.reduce_sum(qks[:, 1, i, :], sqk[i % 2], AX))
                dve.sem_inc(qk_summed, 1)
            for i in range(6):
                sum_qk(i)
            dve.wait_ge(hi_filled, R_CONV + 1)
            pc = [psum[:, 4 + i // 2, (i % 2) * CW:(i % 2 + 1) * CW] for i in range(NT)]
            for i in range(NT):
                last = dve.bn_stats(bns[:, i, 0:6], pc[i])
            link(last)
            for i in range(NT):
                last = dve.bn_aggr(bns[:, i, 6:8], bns[:, i, 0:6])
            link(last)
            dve.sem_inc(ln_stats, 1)
            dve.wait_ge(ln_rstd, 1)
            for i in range(NT):
                last = dve.tensor_scalar(ctok[:, i, :], pc[i], bns[:, i, 6:7], st[:, 112 + i:113 + i], S_, M_)
            link(last)
            dve.sem_inc(hi_drained, 1)
            dve.wait_ge(row_par_in, 16 * 8)
            tt(ctok, ctok, lnwb[:, 0, :].unsqueeze(1).to_broadcast([P, NT, CW]), M_)
            tt(ctok, ctok, lnwb[:, 1, :].unsqueeze(1).to_broadcast([P, NT, CW]), A_)
            dve.sem_inc(ln_done, 1)
            for i in range(6, NT):
                sum_qk(i)
            dve.wait_ge(kpe_in, 16)
            kp2 = at(14336 + 2560, NT, RD)
            tt(kp2, kpe, kpe, M_)
            link(dve.reduce_sum(st[:, 120:120 + NT], kp2, AX))
            tt(qks[:, 1], qks[:, 1], st[:, 120:120 + NT].unsqueeze(2).to_broadcast([P, NT, H]), A_)
            dve.sem_inc(qk_summed, 1)

            qk_f, qkr = qks.rearrange("p a i h -> p (a i h)"), at(14336 + 2816, 2 * NT * H)
            ts(qk_f, qk_f, 1.0 / QH, EPS, M_, A_)
            dve.sem_inc(qk_mean, 1)
            dve.wait_ge(sigm_done, 1)
            tt(sout, sout, yssm, M_)
            dve.sem_inc(glu_done, 1)
            dve.wait_ge(qk_root, 1)
            link(dve.reciprocal(qkr, qkr))
            tt(qk_f, qk_f, qkr, M_)
            tt(qk_f, qk_f, qkr, M_)
            ts(qk_f, qk_f, -0.5, 1.5, M_, A_)
            tt(qk_f, qk_f, qkr, M_)
            ts(qkw[:, 0, :], qkw[:, 0, :], SCALE, None, M_)
            for b in range(2):
                for a in range(2):
                    make_heads_part(dve, link, None, b, b, a, rot_dve)
                dve.sem_inc(heads_made, 1)

            dve.wait_ge(mid_done, 1)
            with dve.Fori(0, H // 2) as it:
                it16, itF = dve.snap(STEPS * it), dve.snap(FILLS * it)

                def save_qT(b):
                    dve.wait_ge(qkT_made, 2 * it + (b + 1))
                    dve.tensor_copy(qT[b][0:QH, :].rearrange("p (k n) -> p k n", k=2),
                                    psum[0:QH, 4 * b:4 * b + 2, :]).then_inc(qT_saved, 1)

                def row_max(n):
                    i = tile_of[n]
                    sv = psum[:, 2 * (n % 2):2 * (n % 2) + 2, :].rearrange("p a n -> p (a n)")
                    dve.wait_ge(s_filled, it16 + (n + 1))
                    dve.memset(sv[0:P // 2, (i + 1) * P - P // 2:(i + 1) * P], NEG).then_inc(s_masked, 1)
                    dve.wait_ge(s_masked, it16 + (n + 1))
                    dve.reduce_max(am[:, n % 4, 0:1], sv[:, 0:(i + 1) * P], AX, negate=True).then_inc(s_max, 1)

                def save_o(n):
                    a = am[:, n % 4, :]
                    dve.wait_ge(p_ready, it16 + (n + 1))
                    dve.reciprocal(a[:, 2:3], a[:, 1:2]).then_inc(sum_inv, 1)
                    dve.wait_ge(sum_inv, it16 + (n + 1))
                    dve.wait_ge(pv_done, itF + first_fill[n + 1])
                    dve.tensor_scalar(otok[:, tile_of[n], bass.ds((2 * it + n // NT) * VD, VD)],
                                      psum[:, 6 + n % 2, 0:VD], a[:, 2:3], None, M_).then_inc(o_saved, 1)

                for b in range(2):
                    save_qT(b)
                row_max(0)
                row_max(1)
                for n in range(STEPS):
                    for f in range(first_fill[n], first_fill[n + 1]):
                        if by_dve[f]:
                            dve.wait_ge(pT_filled, itF + (f + 1))
                            w = min(4, tile_of[n] + 1 - 4 * (f - first_fill[n]))
                            if f >= 4:
                                dve.wait_ge(pv_done, itF + (f - 3))
                            dve.tensor_copy(probT[f % 4][:, 0:w, :], psum[:, 4 + f % 2, 0:w * P].rearrange("p (a n) -> p a n", n=P)
                                            ).then_inc(pT_saved_v, 1)
                    if n + 2 < STEPS:
                        row_max(n + 2)
                    if n >= 1:
                        save_o(n - 1)
                save_o(STEPS - 1)

            dve.wait_ge(x_again, 16 * 2)
            for i in range(NT + 3):
                if i < NT:
                    dve.wait_ge(out_filled, i + 1)
                    xi = x2[:, i, :].rearrange("p (a n) -> p a n", a=2)
                    dve.tensor_tensor(xi, xi, psum[:, 2 * (i % 2):2 * (i % 2) + 2, :], A_).then_inc(x2_ready, 1)
                if i >= 3:
                    dve.wait_ge(lg_filled, i - 2)
                    dve.tensor_tensor(lg[:, i - 3, :], psum[:, 6 + (i - 3) % 2, 0:EG + NE], brow[:, :], A_).then_inc(lg_saved, 1)
                if 1 <= i <= NT:
                    dve.wait_ge(x2_rms, i)
                    if i >= 3:
                        dve.wait_ge(H2_OUT[(i - 1) % 2], 16 * ((i - 1) // 2))
                        dve.wait_ge(h2T_filled, i - 2)
                    dve.scalar_tensor_tensor(h2[(i - 1) % 2], x2[:, i - 1, :], st[:, 103 + i:104 + i], fnorm, M_, M_).then_inc(h2_ready, 1)
            dve.wait_ge(lg_saved, NT)

            gl, el = lg[:, :, 0:EG], lg[:, :, EG:EG + NE].rearrange("p t (g k) -> p t g k", g=EG)

            def over(a, n_):
                return a.unsqueeze(2).to_broadcast([P, NT, n_])

            def first_max(hot, top, x_, n_, t_):
                link(dve.reduce_max(top, x_, AX))
                tt(hot, x_, over(top, n_), ALU.is_equal)
                tt(hot, hot, wrank[:, 8 - n_:8].unsqueeze(1).to_broadcast([P, NT, n_]), M_)
                link(dve.reduce_max(t_, hot, AX))
                tt(hot, hot, over(t_, n_), ALU.is_equal)

            first_max(ohg, gm, gl, EG, rt)
            tt(expg, gl, over(gm, EG), S_)
            dve.sem_inc(expg_in, 1)
            tt(sel, el, ohg.unsqueeze(3).to_broadcast([P, NT, EG, EPG]), M_)
            link(dve.reduce_sum(es, sel.rearrange("p t g k -> p t k g"), AX))
            first_max(oh[0], m1, es, EPG, rt)
            stt(es2.rearrange("p t k -> p (t k)"), oh[0].rearrange("p t k -> p (t k)"), -1e30, es.rearrange("p t k -> p (t k)"), M_, A_)
            first_max(oh[1], m2, es2, EPG, rt)
            tt(expe, m2, m1, S_)
            dve.sem_inc(expe_in, 1)
            for k in range(2):
                tt(pick[k].rearrange("p t (g k) -> p t g k", g=EG), ohg.unsqueeze(3).to_broadcast([P, NT, EG, EPG]),
                   oh[k].unsqueeze(2).to_broadcast([P, NT, EG, EPG]), M_)
            tt(both, pick[0], pick[1], A_)
            link(dve.memset(prior[:, 0, :], 0.0))
            for i in range(NT):
                tt(prior[:, i + 1, :], prior[:, i, :], both[:, i, :], A_)
            dve.sem_inc(picks_ready, 1)
            dve.wait_ge(expg_done, 1)
            link(dve.reduce_sum(rt, expg, AX))
            dve.wait_ge(expe_done, 1)
            ts(m1, expe, 1.0, None, A_)
            tt(rt, rt, m1, M_)
            link(dve.reciprocal(gate[:, 0, :], rt))
            tt(gate[:, 1, :], gate[:, 0, :], expe, M_)
            dve.wait_ge(ranks_filled, 1)
            link(dve.tensor_copy(rank, psum[:, 0, 0:NT * NE].rearrange("p (t e) -> p t e", e=NE)))
            ts(nov, psum[:, 1, 0:NE], 63.5, 1.0 / P, A_, M_)
            ts(nov, nov, ROUND, None, A_)
            ts(nov, nov, ROUND + 1.0, 0.0, S_, ALU.max)
            link(dve.memset(one32, 1.0))
            link(dve.tensor_tensor_scan(novend, one32, nov, 0.0, M_, A_))
            tt(novb, novend, nov, S_)
            stt(novb, novb, float(NE - 1), eiota[:, :], A_, S_)
            ts(blk, rank, 63.5, 1.0 / P, S_, M_)
            ts(blk, blk, ROUND, None, A_)
            ts(blk, blk, ROUND, None, S_)
            flat3 = "p t e -> p (t e)"
            stt(rank.rearrange(flat3), blk.rearrange(flat3), -float(P), rank.rearrange(flat3), M_, A_)
            ts(both, blk, 1.0, None, ALU.min)
            tt(both, both, novb.unsqueeze(1).to_broadcast([P, NT, NE]), M_)
            tt(blk, blk, both, A_)
            tt(blk, blk, eiota[:, :].unsqueeze(1).to_broadcast([P, NT, NE]), A_)
            stt(blk.rearrange(flat3), rank.rearrange(flat3), float(NBLK), blk.rearrange(flat3), M_, A_)
            for k in range(2):
                tt(both, pick[k], blk, M_)
                link(dve.reduce_sum(rt, both, AX))
                link(dve.tensor_copy(slot[:, :, k], rt))
            pay_f = pay.bitcast(F32)
            for k in range(2):
                link(dve.tensor_copy(pay_f[:, :, k, 1], gate[:, k, :]))
            dve.sem_inc(slots_ready, 1)
            tt(ovt, novend[0:1, :].unsqueeze(1).to_broadcast([1, OVF, NE]),
               iota_j[0:1, 0:OVF].unsqueeze(2).to_broadcast([1, OVF, NE]), ALU.is_le)
            link(dve.reduce_sum(ovf[:, 0:OVF], ovt, AX))
            ts(ovf[:, 0:OVF], ovf[:, 0:OVF], float(NE - 1), None, ALU.min)
            link(dve.tensor_copy(ovf[:, OVF:OVF + 1], novend[0:1, NE - 1:NE]))
            link(dve.tensor_copy(ovi[:, :], ovf))
            dve.sem_inc(ov_table, 4)

            def save_heT(e):
                dve.wait_ge(heT_filled, e + 1)
                dve.tensor_copy(heT.rearrange("p c n -> p (c n)"), psum[:, 2, :]).then_inc(heT_saved, 1)

            def hidden(e):
                dve.wait_ge(silu_e, e + 1)
                dve.wait_ge(b_filled, e + 1)
                dve.tensor_tensor(he, sil, psum[:, 1, :], M_).then_inc(he_ready, 1)

            def save_y(b, e):
                dve.wait_ge(idxs_copied, e + 1)
                dve.wait_ge(y_filled, e + 1)
                dve.tensor_scalar(ye[b][:, 512:D], psum[:, 6, :], idx[:, 2 + b, 1:2].bitcast(F32), None, M_).then_inc(y_saved_v, 1)

            dve.sem_inc(y_saved_v, 1)
            hidden(0)

            with dve.Fori(0, NE // 2 - 1) as it:
                for b in (1, 0):
                    e = 2 * it + (2 - b)
                    save_heT(e - 1)
                    hidden(e)
                    save_y(1 - b, e - 1)
            save_heT(NE - 2)
            hidden(NE - 1)
            save_y(0, NE - 2)
            save_heT(NE - 1)
            save_y(1, NE - 1)
            n_ov = dve.value_load(ovi[0:1, OVF:OVF + 1], min_val=0, max_val=OVF)
            with dve.Fori(0, OVF // 2) as it:
                for b in range(2):
                    with dve.If(n_ov > 2 * it + b):
                        e = 2 * it + (NE + b)
                        hidden(e)
                        save_heT(e)
                        save_y(b, e)

        @block.tensor
        def _(pe):
            def lo(n):
                if n >= 4:
                    pe.wait_ge(lo_drained, n - 3)
                return psum[:, n % 4, :]

            def hi(r):
                if r >= 1:
                    pe.wait_ge(hi_drained, r)

            pe.wait_ge(consts_made, 1)
            pe.wait_ge(ssm_par_in, 16 * 11)
            hi(R_C)
            for k in range(2):
                last = pe.transpose(psum[:, 4, k * P:(k + 1) * P], C2[:, k, :], ident[:, :])
            last.then_inc(hi_filled, 1)
            for i in range(NT):
                pe.wait_ge(x_normed, i + 1)
                for k in range(2):
                    bank = lo(F_XT(i, k))
                    for c in range(4):
                        last = pe.transpose(bank[:, c * P:(c + 1) * P], xin[i // 2][:, i % 2, (4 * k + c) * P:(4 * k + c + 1) * P], ident[:, :])
                    last.then_inc(lo_filled, 1)
            def project(n, half, c0):
                bank = lo(n)
                pe.wait_ge(lo_drained, F_XT(4 * half + 3, 1) + 1)
                for c in range(KC):
                    last = pe.matmul(bank, win[:, c, c0:c0 + P], hT[:, c, 4 * half:4 * half + 4, :].rearrange("p i j -> p (i j)"),
                                     start=(c == 0), stop=(c == KC - 1))
                last.then_inc(lo_filled, 1)

            pe.wait_ge(win_scaled, 1)
            for half in range(2):
                for m in range(2):
                    project(F_AG(half, 2 * m), half, G0 + m * P)
                    project(F_AG(half, 2 * m + 1), half, A0 + m * P)
            pe.wait_ge(ssm_w_ready, 1)
            hi(R_W)
            for k in range(2):
                for r in range(NPAIR):
                    last = pe.transpose(psum[:, 4 + 2 * k + r // 4, (r % 4) * P:(r % 4 + 1) * P],
                                        W[:, k, r].rearrange("p t c -> p (t c)"), ident[:, :])
            last.then_inc(hi_filled, 1)
            pe.wait_ge(win_scaled, 2)
            for i in range(NT):
                bank = lo(F_U(i))
                for c in range(KC):
                    last = pe.matmul(bank[:, 0:RD + SW], hT[:, c, i, :], win[:, c, KPE0:A0], start=(c == 0), stop=(c == KC - 1))
                last.then_inc(lo_filled, 1)
            pe.wait_ge(ssm_c_ready, 1)
            hi(R_H)
            for r in range(NPAIR):
                o = psum[0:2 * C, 4 + r // 4, (r % 4) * P:(r % 4 + 1) * P]
                for k in range(2):
                    last = pe.matmul(o, Bz[:, k, r].rearrange("p h c -> p (h c)"),
                                     CL[:, k, r, 0:STEP, :].rearrange("p t c -> p (t c)"), start=(k == 0), stop=(k == 1))
            last.then_inc(hi_filled, 1)
            hi(R_U)
            pe.wait_ge(lo_drained, F_U(NT - 1) + 1)
            for g in range(G):
                last = pe.transpose(psum[:, 4 + g // 4, (g % 4) * P:(g % 4 + 1) * P], utok[:, g].rearrange("p t c -> p (t c)"), ident[:, :])
            last.then_inc(hi_filled, 1)
            for half in range(2):
                for m, c0 in enumerate((CQ0, CQ0 + P, CKV0)):
                    project(F_LAT(half, m), half, c0)
            hi(R_V)
            for k in range(2):
                for r in range(NPAIR):
                    for h in range(2):
                        last = pe.matmul(psum[h * S:(h + 1) * S, 4 + 2 * k + r // 4, (r % 4) * P:(r % 4 + 1) * P],
                                         WT[:, k, r, h * S:(h + 1) * S], U[:, 2 * r + h, :], start=True, stop=True)
            last.then_inc(hi_filled, 1)
            pe.wait_ge(lat_squared, 1)
            bank = lo(F_SSQ)
            for i in range(NT):
                for m in range(2):
                    pe.matmul(bank[:, i:i + 1], sqc[:, m, i * P:(i + 1) * P], ones[:, 0:1], start=(m == 0), stop=(m == 1))
                last = pe.matmul(bank[:, NT + i:NT + i + 1], sqc[:, 2, i * P:(i + 1) * P], ones[:, 0:1], start=True, stop=True)
            last.then_inc(lo_filled, 1)
            pe.wait_ge(wproj_scaled, 1)

            def project_qkv(i):
                for k in range(2):
                    bank = lo(F_QKV(i, k))
                    for m in range(2):
                        last = pe.matmul(bank[:, 0:384], cqT[:, m, i * P:(i + 1) * P], wuq[:, m, k * 384:(k + 1) * 384],
                                         start=(m == 0), stop=(m == 1))
                    last.then_inc(lo_filled, 1)
                for k in range(2):
                    pe.matmul(lo(F_QKV(i, 2 + k)), ckvT[:, i * P:(i + 1) * P], wukv[:, k * 512:(k + 1) * 512],
                              start=True, stop=True).then_inc(lo_filled, 1)
            for i in range(4):
                project_qkv(i)
            pe.wait_ge(toep_in, 16 * 2 * STEP)
            pe.wait_ge(ssm_x_ready, 1)
            hi(R_Y)
            for h in range(2):
                for r in range(NPAIR):
                    o = psum[:, 4 + 2 * h + r // 4, (r % 4) * P:(r % 4 + 1) * P]
                    pe.matmul(o, U[:, 2 * r + h, :], toep[:, 2 * r + h, :], start=True, stop=False)
                    for k in range(2):
                        last = pe.matmul(o, Xp[h * S:(h + 1) * S, k, r, :],
                                         CL[h * S:(h + 1) * S, k, r, 1:STEP + 1, :].rearrange("p t c -> p (t c)"),
                                         start=False, stop=(k == 1))
            last.then_inc(hi_filled, 1)

            def turn(src, r):
                hi(r)
                for i in range(NT):
                    for c in range(2):
                        last = pe.transpose(psum[:, 4 + i // 2, (i % 2) * 256 + c * P:(i % 2) * 256 + (c + 1) * P], src(i, c), ident[:, :])
                last.then_inc(hi_filled, 1)

            for i in range(4, 6):
                project_qkv(i)
            pe.wait_ge(conv_done, 1)
            turn(lambda i, c: cperm[:, c, i, :], R_CONV)
            for i in range(6, NT):
                project_qkv(i)
            pe.wait_ge(z_ready, 1)
            turn(lambda i, c: yssm[:, i, c * P:(c + 1) * P], R_Z)
            hi(R_GLU)
            for i in range(NT):
                for c in range(2):
                    last = pe.matmul(psum[:, 4 + i // 2, (i % 2) * 256:(i % 2 + 1) * 256], zT[:, c, i * P:(i + 1) * P], wglu[:, c, :],
                                     start=(c == 0), stop=(c == 1))
            last.then_inc(hi_filled, 1)
            pe.wait_ge(mid_scaled, 1)
            turn(lambda i, c: ctok[:, i, c * P:(c + 1) * P], R_COUT)
            pe.wait_ge(mid_scaled, 2)
            turn(lambda i, c: sout[:, i, c * P:(c + 1) * P], R_SOUT)

            pe.wait_ge(mid_done, 1)
            with pe.Fori(0, H // 2) as it:
                it16, itF = pe.snap(STEPS * it), pe.snap(FILLS * it)
                ita, itv = pe.snap(saved_a[FILLS] * it), pe.snap(saved_v[FILLS] * it)
                for b in range(2):
                    pe.wait_ge(heads_made, 2 * it + (b + 1))
                    for a, buf in enumerate((qn[b], kn[b])):
                        for i in range(NT):
                            last = pe.transpose(psum[0:QH, 4 * b + 2 * a + i // 4, (i % 4) * P:(i % 4 + 1) * P], buf[:, i, :], ident[:, :])
                    last.then_inc(qkT_made, 1)

                def scores(n):
                    b, i = n // NT, tile_of[n]
                    if n % NT == 0:
                        pe.wait_ge(qT_saved, 2 * it + (b + 1))
                        pe.wait_ge(kT_saved, 2 * it + (b + 1))
                    if n >= 2:
                        pe.wait_ge(p_ready, it16 + (n - 1))
                    L = (i + 1) * P
                    for k in range((L + 511) // 512):
                        w = min(512, L - 512 * k)
                        last = pe.matmul(psum[:, 2 * (n % 2) + k, 0:w], qT[b][0:QH, i * P:(i + 1) * P], kT[b][0:QH, 512 * k:512 * k + w],
                                         start=True, stop=True)
                    last.then_inc(s_filled, 1)

                def saved(f, n):
                    pe.wait_ge(pT_saved_a, ita + saved_a[f + 1])
                    if saved_v[f + 1]:
                        pe.wait_ge(pT_saved_v, itv + saved_v[f + 1])

                def turn_probs(n):
                    pe.wait_ge(p_ready, it16 + (n + 1))
                    for f in range(first_fill[n], first_fill[n + 1]):
                        if f < 2:
                            pe.wait_ge(qT_saved, 2 * it + 2)
                        else:
                            saved(f - 2, n)
                        j0 = 4 * (f - first_fill[n])
                        for j in range(j0, min(j0 + 4, tile_of[n] + 1)):
                            last = pe.transpose(psum[:, 4 + f % 2, (j - j0) * P:(j - j0 + 1) * P], prob[n % 2][:, j * P:(j + 1) * P], ident[:, :])
                        last.then_inc(pT_filled, 1)

                def values(n):
                    i = tile_of[n]
                    if n < 2:
                        pe.wait_ge(kT_saved, 2 * it + 2)
                    else:
                        pe.wait_ge(o_saved, it16 + (n - 1))
                    for f in range(first_fill[n], first_fill[n + 1]):
                        saved(f, n)
                        j0 = 4 * (f - first_fill[n])
                        for j in range(j0, min(j0 + 4, i + 1)):
                            last = pe.matmul(psum[:, 6 + n % 2, 0:VD], probT[f % 4][:, j - j0, :],
                                             vtok[:, j, bass.ds((2 * it + n // NT) * VD, VD)], start=(j == 0), stop=(j == i))
                        last.then_inc(pv_done, 1)

                scores(0)
                scores(1)
                for n in range(STEPS):
                    turn_probs(n)
                    if n + 2 < STEPS:
                        scores(n + 2)
                    if n >= 1:
                        values(n - 1)
                values(STEPS - 1)
                pe.wait_ge(o_saved, it16 + STEPS)

            for i in range(NT):
                pe.wait_ge(o_scaled, i + 1)
                if i >= 4:
                    pe.wait_ge(oT_saved, i - 3)
                for c in range(4):
                    last = pe.transpose(psum[:, i % 4, c * P:(c + 1) * P], otok[:, i, c * P:(c + 1) * P], ident[:, :])
                last.then_inc(oT_filled, 1)
            pe.wait_ge(oT_saved, NT)
            pe.wait_ge(wout_scaled, 1)

            def logits(i):
                pe.wait_ge(h2T_saved, i + 1)
                if i >= 2:
                    pe.wait_ge(lg_saved, i - 1)
                for c in range(KC):
                    last = pe.matmul(psum[:, 6 + i % 2, 0:EG + NE], h2T[:, c, :], wr[:, c, :], start=(c == 0), stop=(c == KC - 1))
                last.then_inc(lg_filled, 1)

            for i in range(NT + 2):
                if i < NT:
                    if i >= 2:
                        pe.wait_ge(x2_ready, i - 1)
                    for k in range(2):
                        for c in range(KC):
                            y_ = oT[:, c, i, :] if c < 4 else yT[:, c - 4, i, :]
                            last = pe.matmul(psum[:, 2 * (i % 2) + k, :], y_, wout[:, c, 512 * k:512 * (k + 1)],
                                             start=(c == 0), stop=(c == KC - 1))
                    last.then_inc(out_filled, 1)
                if i >= 2:
                    logits(i - 2)
                if 1 <= i <= NT:
                    pe.wait_ge(h2_ready, i)
                    if i >= 2:
                        pe.wait_ge(h2T_saved, i - 1)
                    for c in range(KC):
                        last = pe.transpose(psum[:, 4 + c // 4, (c % 4) * P:(c % 4 + 1) * P], h2[(i - 1) % 2][:, c * P:(c + 1) * P], ident[:, :])
                    last.then_inc(h2T_filled, 1)
            pe.wait_ge(picks_ready, 1)
            o = psum[:, 0, 0:NT * NE]
            pe.matmul(o, before[:, :], both.rearrange("p t e -> p (t e)"), start=True, stop=False)
            pe.matmul(o, ones[:, :], prior[:, 0:NT, :].rearrange("p t e -> p (t e)"), start=False, stop=True)
            pe.matmul(psum[:, 1, 0:NE], ones[:, :], prior[:, NT, :], start=True, stop=True).then_inc(ranks_filled, 1)

            def turn_rows(b, e, gathers):
                pe.wait_ge(ROWS_IN[b], gathers)
                for c in range(KC):
                    last = pe.transpose(psum[:, 3 + c // 4, (c % 4) * P:(c % 4 + 1) * P], xg[b][:, c * P:(c + 1) * P], ident[:, :])
                last.then_inc(xgT_filled, 1)

            def up(k, b, e):
                for c in range(KC):
                    last = pe.matmul(psum[:, k, :], xgT[:, c, :], w13[b][k][:, c, :], start=(c == 0), stop=(c == KC - 1))
                last.then_inc((a_filled, b_filled)[k], 1)

            def turn_hidden(e):
                pe.wait_ge(he_ready, e + 1)
                for c in range(FC):
                    last = pe.transpose(psum[:, 2, c * P:(c + 1) * P], he[:, c * P:(c + 1) * P], ident[:, :])
                last.then_inc(heT_filled, 1)

            def down(b, e):
                pe.wait_ge(heT_saved, e + 1)
                pe.wait_ge(y_saved_a, e + 1)
                pe.wait_ge(y_saved_v, e + 1)
                for k in range(2):
                    for c in range(FC):
                        last = pe.matmul(psum[:, 5 + k, :], heT[:, c, :], w2s[b][:, c, 512 * k:512 * (k + 1)], start=(c == 0), stop=(c == FC - 1))
                last.then_inc(y_filled, 1)

            pe.wait_ge(slots_ready, 1)
            turn_rows(0, 0, 16)
            pe.wait_ge(xgT_saved, 1)
            pe.wait_ge(W13_IN[0], 32)
            up(0, 0, 0)
            up(1, 0, 0)
            turn_rows(1, 1, 16)
            with pe.Fori(0, NE // 2 - 1) as it:
                for b in (1, 0):
                    e = 2 * it + (2 - b)
                    pe.wait_ge(xgT_saved, e + 1)
                    pe.wait_ge(W13_IN[b], 32 * it + 32 * (2 - b))
                    pe.wait_ge(silu_e, e)
                    up(0, b, e)
                    turn_hidden(e - 1)
                    up(1, b, e)
                    turn_rows(1 - b, e + 1, 16 * it + 32)
                    pe.wait_ge(W2_IN[1 - b], 16 * it + 16)
                    down(1 - b, e - 1)
            pe.wait_ge(xgT_saved, NE)
            pe.wait_ge(W13_IN[1], 16 * NE)
            pe.wait_ge(silu_e, NE - 1)
            up(0, 1, NE - 1)
            turn_hidden(NE - 2)
            up(1, 1, NE - 1)
            pe.wait_ge(W2_IN[0], 8 * NE)
            down(0, NE - 2)
            turn_hidden(NE - 1)
            pe.wait_ge(W2_IN[1], 8 * NE)
            down(1, NE - 1)
            pe.wait_ge(ov_table, 1)
            n_ov = pe.value_load(ovi[0:1, OVF:OVF + 1], min_val=0, max_val=OVF)
            with pe.Fori(0, OVF // 2) as it:
                for b in range(2):
                    with pe.If(n_ov > 2 * it + b):
                        e = 2 * it + (NE + b)
                        turn_rows(b, e, 16 * it + 16 * (NE // 2 + 1))
                        pe.wait_ge(xgT_saved, e + 1)
                        pe.wait_ge(OV_W_IN[b], 48 * it + 48)
                        up(0, b, e)
                        up(1, b, e)
                        turn_hidden(e)
                        down(b, e)


_INS = ["x", "positions", "mix_norm", "w_in", "q_a_norm", "w_uq", "kv_a_norm", "w_ukv", "q_norm", "k_norm",
        "ssm_lam_re", "ssm_lam_im", "ssm_b_re", "ssm_b_im", "ssm_c_re", "ssm_c_im", "ssm_d", "ssm_log_dt", "ssm_w_glu",
        "conv_dw_w", "conv_dw_b", "conv_ln_w", "conv_ln_b", "out_norm", "w_out",
        "ffn_norm", "w_grp", "b_grp", "w_exp", "b_exp", "w1", "w3", "w2"]


def kernel(**inputs):
    import numpy as _np
    import concourse.bacc as _bacc
    from concourse import mybir as _mybir
    from concourse.bass_utils import run_bass_kernel_spmd as _run

    nc = _bacc.Bacc("TRN2", target_bir_lowering=False, num_devices=1)
    arrays, args = {}, []
    for name in _INS:
        a = _np.ascontiguousarray(inputs[name])
        arrays[f"in_{name}"] = a
        args.append(nc.dram_tensor(f"in_{name}", a.shape, _mybir.dt.from_np(a.dtype), kind="ExternalInput").ap())
    x = arrays["in_x"]
    out = nc.dram_tensor("out_0", x.shape, _mybir.dt.float32, kind="ExternalOutput").ap()
    build(nc, *args, out)
    r = _run(nc, [arrays], core_ids=[0])
    return r.results[0]["out_0"]
```

```python
from contextlib import ExitStack

import numpy as np

import concourse.bass as bass
from concourse import mybir

ALU = mybir.AluOpType
ACT = mybir.ActivationFunctionType
F32 = mybir.dt.float32
F32R = mybir.dt.float32r
I32 = mybir.dt.int32
U32 = mybir.dt.uint32
AX = mybir.AxisListType.X

P = 128
EPS = 1e-6
LN_EPS = 1e-5
LINKS = 13
PI = float(np.pi)
TWO_PI_SAFE = 6.2831850
TWO_PI_HI = 6.28125
TWO_PI_LO = 2.0 * PI - TWO_PI_HI
ROUND = 1.5 * 2.0 ** 23
ROUND16 = 1.5 * 2.0 ** 7
NEG = -3.0e38
SKIP_ROW = 1 << 20


def build(nc, x, positions, mix_norm, w_in, q_a_norm, w_uq, kv_a_norm, w_ukv, q_norm, k_norm,
          lam_re, lam_im, b_re, b_im, c_re, c_im, d_skip, log_dt, w_glu,
          dw_w, dw_b, ln_w, ln_b, out_norm, w_out,
          ffn_norm, w_grp, b_grp, w_exp, b_exp, w1, w3, w2, out):
    T, D = x.shape[1], x.shape[2]
    NT, KC = T // P, D // P
    QL, KL = q_a_norm.shape[1], kv_a_norm.shape[1]
    QH = q_norm.shape[1]
    H = w_uq.shape[2] // QH
    RD, ND = QH - QH // 3 * 2, QH // 3 * 2
    HR = RD // 2
    VD = w_ukv.shape[2] // H - ND
    G, S = lam_re.shape[1], lam_re.shape[2]
    C = b_re.shape[3]
    SW, CW, TAPS = G * C, dw_w.shape[2], dw_w.shape[1]
    NPAIR = G // 2
    STEP = P // C
    NJ = T // STEP
    EG, NE = w_grp.shape[2], w_exp.shape[2]
    EPG = NE // EG
    FF = w1.shape[3]
    FC = FF // P
    OVF = 2 * T // P
    MORE = T // P - 1
    NBLK = NE * (1 + MORE)
    ROUTE = ((0, NT - 2), (NT - 2, NT))
    assert (T, D, NT, KC, QH, RD, ND, VD) == (1024, 1024, 8, 8, 96, 32, 64, 64)
    assert STEP == NT and NJ == P and SW == CW == 256 and S == 64 and 2 * C == 32
    CQ0, CKV0, KPE0, U0, A0, G0 = 0, QL, QL + KL, QL + KL + RD, QL + KL + RD + SW, QL + KL + RD + SW + CW
    NIN = G0 + CW
    SCALE = float(QH) ** -0.5
    AW = H * VD

    with ExitStack() as ctx:
        def sb(name, shape, dt=F32):
            return ctx.enter_context(nc.sbuf_tensor(name, shape, dt))[tuple(slice(0, n) for n in shape)]

        def sem(name):
            return ctx.enter_context(nc.semaphore(name))

        WORDS = 50300
        base = -(-nc.sbuf_base // 32) * 32
        arena = sb("arena", [P, WORDS])
        assert nc.sbuf_base == base + 4 * WORDS

        def at(off, *dims, parts=P):
            n = int(np.prod(dims))
            assert off + n <= WORDS
            v = arena[0:parts, off:off + n]
            if len(dims) == 2:
                return v.rearrange("p (a b) -> p a b", b=dims[1])
            if len(dims) == 3:
                return v.rearrange("p (a b c) -> p a b c", b=dims[1], c=dims[2])
            if len(dims) == 4:
                return v.rearrange("p (a b c d) -> p a b c d", b=dims[1], c=dims[2], d=dims[3])
            return v

        def own(name, off, a, b, dt):
            t_ = nc.alloc_sbuf_tensor_at(name, [P, a * b], dt, offset=base + 4 * off)
            return t_[:, :].rearrange("p (a b) -> p a b", b=b)

        hT = at(0, KC, NT, P)
        win = at(8192, KC, NIN)
        PADW = T + TAPS - 1
        upad = at(17664, 2, PADW)
        cqT = at(19772, 2, T)
        ckvT = at(21820, T)
        kpe = at(22844, NT, RD)
        S0, YT0 = 23100, 44092
        xin = [at((S0, S0 + 2048, S0 + 4096, YT0 + 2048)[k], 2, D) for k in range(4)]
        wuq = at(S0 + 2048, 2, H * QH)
        wglu = at(S0 + 3584, 2, SW)
        utok = at(S0 + 4096, G, STEP, C)
        U = at(S0 + 6144, G, NJ)
        toep = at(S0 + 8192, G, P)
        WT = at(S0 + 10240, 2, NPAIR, P)
        CL = at(S0 + 12288, 2, NPAIR, STEP + 1, C)
        W = at(S0 + 14592, 2, NPAIR, STEP, C)
        cosj = at(S0 + 16640, NPAIR, NJ)
        sinj = at(S0 + 17664, NPAIR, NJ)
        decay = at(S0 + 18688, NPAIR, NJ)
        Bz = at(S0 + 19712, 2, NPAIR, 2, C)
        CTt = at(S0 + 20224, 2, NPAIR, C)
        C2 = at(S0 + 20480, 2, P)
        Bb = at(S0 + 20736, 2, NPAIR, C)
        Hk = at(YT0, NPAIR, STEP, C, parts=2 * C)
        Braw = at(YT0 + 1024, 2, NPAIR, C)
        kst = at(YT0 + 1280, NT, RD)
        sigT = at(19772, 2, T)
        sqc = at(14336, 3, T)
        cacc = at(YT0 + 2048, 2, T)
        wukv = at(48188, H * (ND + VD))
        tmp = at(49212, 1024)
        Vrot = at(S0 + 4096, 2, NPAIR, NJ)
        Zs = at(S0 + 10240, 2, NPAIR, NJ)
        Xp = at(S0 + 4096, 2, NPAIR, NJ)
        yssm = at(S0 + 16640, NT, SW)
        zT = at(S0 + 6144, 2, T)
        sout = at(S0 + 8192, NT, SW)
        cperm = at(S0 + 14592, 2, NT, P)
        ctok = at(S0, NT, CW)
        yT = at(YT0, 4, NT, P)
        qraw = at(0, NT, H * QH)
        kraw = at(6144, NT, H * ND)
        vtok = at(10240, NT, H * VD)
        qn = [at(14336 + 768 * b, NT, QH) for b in range(2)]
        kn = [at(14336 + 1536, NT, QH), at(S0 + 12032, NT, QH)]
        sqq = [at(14336 + 1280 * b, H, QH) for b in range(2)]
        sqk = [at(14336 + 1280 * b + 768, H, ND) for b in range(2)]
        rot = at(14336 + 2304, 2, NT, RD)
        rot_dve = at(14336 + 2816, 2, NT, RD)
        qT = [at(S0 + 1024 * b, T) for b in range(2)]
        kT = [at(S0 + 2048 + 1024 * b, T) for b in range(2)]
        prob = [at(S0 + 4096 + 1024 * b, T) for b in range(2)]
        probT = [at((S0 + 6144, S0 + 6656, S0 + 7168, 17664)[b], 4, P) for b in range(4)]
        otok = at(S0 + 7936, NT, AW)
        wout = at(35900, KC, D)
        oT = at(0, 4, NT, P)
        x2 = at(4096, NT, D)
        h2 = [at(32768, D), at(49212, D)]
        junk = at(48188, D)
        h2T = at(33792, KC, P)
        fnorm = at(34816, D)
        EW = KC * FF
        w13 = [[at(12288 + 12288 * b + EW * k, KC, FF) for k in range(2)] for b in range(2)]
        w2s = [own(f"w2_{b}", 12288 + 12288 * b + 2 * EW, FC, D, F32) for b in range(2)]
        M0 = 36864
        xg = [at(M0 + 1024 * b, D) for b in range(2)]
        xgT = at(M0 + 2048, KC, P)
        ye = [at(M0 + 4096 + 1024 * b, D) for b in range(2)]
        he = at(M0 + 6144, FF)
        heTh, heTl = own("heT_high", M0 + 7168, FC, P, F32R), own("heT_rest", M0 + 6656, FC, P, F32R)
        w2h = [own(f"w2_high_{b}", 4096 + FC * D * b, FC, D, F32R) for b in range(2)]
        w2l = [own(f"w2_rest_{b}", 12288 + 12288 * b + 2 * EW, FC, D, F32R) for b in range(2)]
        sil = at(M0 + 8192, FF)
        R0 = 12288 + 2 * EW
        ohg, expg = at(R0, NT, EG), at(R0 + 32, NT, EG)
        gm, rt, m1, m2, expe = (at(R0 + 64 + 8 * k, NT) for k in range(5))
        es, es2 = at(R0 + 128, NT, EPG), at(R0 + 192, NT, EPG)
        oh = [at(R0 + 256 + 64 * k, NT, EPG) for k in range(2)]
        sel = at(R0 + 384, NT, EG, EPG)
        rank, blk = at(R0 + 384, NT, NE), at(R0 + 640, NT, NE)
        pick = [at(R0 + 896 + 256 * k, NT, NE) for k in range(2)]
        both = at(R0 + 1408, NT, NE)
        prior = at(R0 + 1664, NT + 1, NE)
        nov, novend, one32 = (at(R0 + 1952 + NE * k, NE) for k in range(3))
        ovt = at(R0 + 2080, OVF + 1, NE, parts=1)
        tabi = arena[:, 48320:48320 + 2 * NBLK].bitcast(I32).rearrange("p (b k) -> p b k", k=2)
        ovf = at(48840, 2, OVF + 2, parts=1)
        tab0 = at(21820, NBLK, 2).bitcast(I32)

        ident = sb("ident", [P, P])
        ones = sb("ones", [P, P])
        minus_half = sb("minus_half", [P, NT * H])
        before = sb("before", [P, P])
        iota_j = sb("iota_j", [P, P])
        lnwb = sb("lnwb", [P, 2, CW])
        qkw = sb("qkw", [P, 2, QH])
        wrank = sb("wrank", [P, 8])
        eiota = sb("eiota", [P, NE])
        freq = sb("freq", [P, HR])
        rope = sb("rope", [P, 2, NT, RD])
        dwc = sb("dwc", [P, 2, TAPS + 1])
        normc = sb("normc", [P, 2 * KC + 4])
        wr = sb("wr", [P, KC, EG + NE])
        brow = sb("brow", [P, EG + NE])
        lg = rope.rearrange("p a i d -> p (a i d)")[:, 0:NT * (EG + NE)].rearrange("p (i e) -> p i e", i=NT)
        st = sb("st", [P, 128])
        qks = sb("qks", [P, 2, NT, H])
        halfpi = sb("halfpi", [P, 1])
        lamc, sc = at(YT0 + 1536, 3, NPAIR), at(YT0 + 1560, 20, NPAIR)
        Lp, Lv = at(YT0 + 1720, 2, STEP + 1, NPAIR), at(YT0 + 1864, 2, STEP, NPAIR)
        dch = sb("dch", [2 * C, NPAIR])
        posi = sb("posi", [P, NT], I32)
        posf = sb("posf", [P, NT])
        gate = sb("gate", [P, 2, NT])
        am = sb("am", [P, 4, 3])
        idx = sb("idx", [P, 4, 2], I32)
        pay = sb("pay", [P, NT, 2, 2], I32)
        slot = sb("slot", [P, NT, 2], I32)
        ovi = sb("ovi", [1, 2, OVF + 2], I32)
        obase = sb("obase", [P, NE])
        dmask = sb("dmask", [2 * C, C])
        bns = sb("bns", [P, NT, 8])
        psum = ctx.enter_context(nc.psum_tensor("psum", [P, 8, 512], F32))

        kpe_d = nc.dram_tensor("kpe_scratch", [T, RD], F32).ap()
        h2_d = nc.dram_tensor("h2_scratch", [T, D], F32).ap()
        tab_d = nc.dram_tensor("slot_table", [NBLK * P, 2], I32).ap()

        x_s = x.rearrange("a (p i) d -> (a p) i d", i=NT)
        out_s = out.rearrange("a (p i) d -> (a p) i d", i=NT)
        h2_s = h2_d.rearrange("(p i) d -> p i d", i=NT)
        out_d = out.rearrange("a t d -> (a t) d")
        w1_e = w1[0].rearrange("e (c p) f -> e p c f", p=P)
        w3_e = w3[0].rearrange("e (c p) f -> e p c f", p=P)
        w2_e = w2[0].rearrange("e (c p) d -> e p c d", p=P)

        def sems(text):
            return [sem(n) for n in text.split()]

        consts_made, ssm_par_in, small_par_in, row_par_in = sems("consts_made ssm_par_in small_par_in row_par_in")
        win_ag_in, win_rest_in, x01_in, x23_in, x45_in, x67_in = sems("win_ag_in win_rest_in x01_in x23_in x45_in x67_in")
        x_squared, x_rms, x_normed, win_scaled, win_ag_scaled, mix_norm_in, wproj_in = sems("x_squared x_rms x_normed win_scaled win_ag_scaled mix_norm_in wproj_in")
        wproj_scaled, lo_filled, lo_drained, hi_filled = sems("wproj_scaled lo_filled lo_drained hi_filled")
        hi_drained, trig_ready, trig_done, phase_ready = sems("hi_drained trig_ready trig_done phase_ready")
        tables_made, ssm_w_ready, ssm_c_ready, hk_saved = sems("tables_made ssm_w_ready ssm_c_ready hk_saved")
        toep_in, kst_out, kpe_in, upad_ready, ssm_x_ready = sems("toep_in kst_out kpe_in upad_ready ssm_x_ready")
        lat_squared, lat_rms, qk_saved, qk_squared = sems("lat_squared lat_rms qk_saved qk_squared")
        qk_summed, rope_ang, rope_made, ln_stats, ln_rstd = sems("qk_summed rope_ang rope_made ln_stats ln_rstd")
        ln_done, z_ready, sigm_done, glu_done, mid_squared = sems("ln_done z_ready sigm_done glu_done mid_squared")
        mid_rms, mid_scaled, mid_done, wout_in = sems("mid_rms mid_scaled mid_done wout_in")
        wout_scaled, qkT_made, qT_saved, kT_saved = sems("wout_scaled qkT_made qT_saved kT_saved")
        s_filled, s_masked, s_max, p_ready, pT_filled = sems("s_filled s_masked s_max p_ready pT_filled")
        pT_saved_a, pT_saved_v, pv_done, sum_inv, o_saved = sems("pT_saved_a pT_saved_v pv_done sum_inv o_saved")
        o_squared, o_rms, o_scaled, oT_filled, oT_saved = sems("o_squared o_rms o_scaled oT_filled oT_saved")
        x_again, out_filled, x2_ready, x2_squared, x2_rms = sems("x_again out_filled x2_ready x2_squared x2_rms")
        h2_ready, h2_a_stored, h2_b_stored, h2T_filled = sems("h2_ready h2_a_stored h2_b_stored h2T_filled")
        h2T_saved, lg_filled, lg_saved, expg_in, expg_done = sems("h2T_saved lg_filled lg_saved expg_in expg_done")
        expe_in, expe_done, picks_ready, ranks_filled = sems("expe_in expe_done picks_ready ranks_filled")
        slots_ready, tab_cleared, tab_rows_out, tab_in = sems("slots_ready tab_cleared tab_rows_out tab_in")
        ov_table, w13_a_in, w13_b_in, w2_a_in, w2_b_in = sems("ov_table w13_a_in w13_b_in w2_a_in w2_b_in")
        idxg_copied, idxs_copied, rows_a_in, rows_b_in = sems("idxg_copied idxs_copied rows_a_in rows_b_in")
        xgT_filled, xgT_saved, a_filled, silu_e, b_filled = sems("xgT_filled xgT_saved a_filled silu_e b_filled")
        he_ready, heT_filled, heT_saved, y_filled = sems("he_ready heT_filled heT_saved y_filled")
        y_saved_a, y_saved_v, y_a_out, y_b_out, ov_w_a_in, ov_w_b_in = sems("y_saved_a y_saved_v y_a_out y_b_out ov_w_a_in ov_w_b_in")
        out_stored = sem("out_stored")
        pool_seq, act_seq, dve_seq, pool_steps, head_seq = sems("pool_seq act_seq dve_seq pool_steps head_seq")
        w2h_ready, w2_split, heTh_saved = sems("w2h_ready w2_split heTh_saved")
        conv_done, qk_mean, qk_root, heads_made = sems("conv_done qk_mean qk_root heads_made")
        X_IN = (x01_in, x23_in, x45_in, x67_in)
        W13_IN, W2_IN = (w13_a_in, w13_b_in), (w2_a_in, w2_b_in)
        ROWS_IN, Y_OUT = (rows_a_in, rows_b_in), (y_a_out, y_b_out)
        ov_w2_a_in, ov_w2_b_in = sems("ov_w2_a_in ov_w2_b_in")
        OV_W_IN, OV_W2_IN = (ov_w_a_in, ov_w_b_in), (ov_w2_a_in, ov_w2_b_in)
        H2_OUT = (h2_a_stored, h2_b_stored)

        F_XT = lambda i, k: 2 * i + k + 4 * (2 * i // NT)
        F_AG = lambda half, m: (NT + 4) * half + NT + m
        F_U = lambda i: 2 * NT + 8 + i
        F_LAT = lambda half, m: 3 * NT + 8 + 3 * half + m
        F_SSQ = 3 * NT + 14
        F_QKV = lambda i, k: F_SSQ + 1 + 4 * i + k
        R_C, R_W, R_H, R_U, R_V, R_CONV, R_Y, R_Z, R_GLU, R_COUT, R_SOUT = range(11)
        STEPS = 2 * NT
        tile_of = [(NT - 1 - n % NT // 2) if n % 2 == 0 else n % NT // 2 for n in range(STEPS)]
        fills_of = [i // 4 + 1 for i in tile_of]
        first_fill = [sum(fills_of[:n]) for n in range(STEPS + 1)]
        FILLS = first_fill[STEPS]
        by_dve = [f % 3 == 2 for f in range(FILLS)]
        saved_a = [sum(not v for v in by_dve[:f]) for f in range(FILLS + 1)]
        saved_v = [sum(by_dve[:f]) for f in range(FILLS + 1)]

        block = ctx.enter_context(nc.Block())

        def natural(view, half):
            return view.rearrange("p (j i) -> p i j", i=NT)[:, half * 4:half * 4 + 4, :]

        def make_heads_part(eng, link, settle, hd, b, a, rot):
            mult, buf = ALU.mult, (qn, kn)[a][b]
            r = qks[:, a, :, bass.ds(hd, 1)]
            if settle:
                settle()
            if a == 0:
                link(eng.tensor_tensor(buf, qraw[:, :, bass.ds(hd * QH, QH)], r.to_broadcast([P, NT, QH]), mult))
            else:
                link(eng.tensor_tensor(buf[:, :, 0:ND], kraw[:, :, bass.ds(hd * ND, ND)], r.to_broadcast([P, NT, ND]), mult))
                if settle:
                    settle()
                link(eng.tensor_tensor(buf[:, :, ND:QH], kpe, r.to_broadcast([P, NT, RD]), mult))
            link(eng.tensor_tensor(buf, buf, qkw[:, a, :].unsqueeze(1).to_broadcast([P, NT, QH]), mult))
            link(eng.tensor_tensor(rot[:, 0], buf[:, :, ND:QH], rope[:, 0], mult))
            link(eng.tensor_tensor(rot[:, 1, :, 0:HR], buf[:, :, ND + HR:QH], rope[:, 1, :, 0:HR], mult))
            link(eng.tensor_tensor(rot[:, 1, :, HR:RD], buf[:, :, ND:ND + HR], rope[:, 1, :, HR:RD], mult))
            link(eng.tensor_tensor(buf[:, :, ND:QH], rot[:, 0], rot[:, 1], ALU.add))

        @block.sync
        def _(sp):
            def load_x(k):
                sp.dma_start(xin[k], x_s[:, 2 * k:2 * k + 2, :]).then_inc(X_IN[k], 16)

            load_x(0)
            with nc.allow_non_contiguous_dma(reason="parameters of a few KiB"):
                sp.dma_start(normc[:, 0:KC], mix_norm[0].rearrange("(c p) -> p c", p=P)).then_inc(mix_norm_in, 16)
            load_x(1)
            w_in_c = w_in[0].rearrange("(c p) n -> p c n", p=P)
            sp.dma_start(win[:, :, A0:NIN], w_in_c[:, :, A0:NIN]).then_inc(win_ag_in, 16)
            load_x(2)
            with nc.allow_non_contiguous_dma(reason="parameters of a few KiB"):
                for k, lam in enumerate((lam_re, lam_im)):
                    sp.dma_start(lamc[:, k, :], lam[0].rearrange("(r h) s -> (h s) r", h=2)).then_inc(ssm_par_in, 16)
                for h in range(2):
                    sp.dma_start(lamc[h * S:(h + 1) * S, 2, :],
                                   log_dt[0, h:G:2].partition_broadcast(S)).then_inc(ssm_par_in, 16)
                    for k, c_ in enumerate((c_re, c_im)):
                        sp.dma_start(C2[:, k, h * S:(h + 1) * S],
                                       c_[0].rearrange("(r h) c s -> r h c s", h=2)[:, h, :, :]).then_inc(ssm_par_in, 16)
                for k, b_ in enumerate((b_re, b_im)):
                    sp.dma_start(Braw[:, k, :, :], b_[0].rearrange("(r h) s c -> (h s) r c", h=2)).then_inc(ssm_par_in, 16)
                sp.dma_start(dch[:, :], d_skip[0].rearrange("(r h) c -> (h c) r", h=2)).then_inc(ssm_par_in, 16)
            load_x(3)
            with nc.allow_non_contiguous_dma(reason="parameters of a few KiB"):
                for k, (v, n) in enumerate(((out_norm, KC), (q_a_norm, 2), (kv_a_norm, 1))):
                    o = (KC, 2 * KC, 2 * KC + 2)[k]
                    sp.dma_start(normc[:, o:o + n], v[0].rearrange("(c p) -> p c", p=P)).then_inc(small_par_in, 16)
                for m in range(2):
                    sp.dma_start(dwc[:, m, 0:TAPS], dw_w[0].rearrange("k (m p) -> m p k", m=2)[m]).then_inc(small_par_in, 16)
                sp.dma_start(dwc[:, :, TAPS], dw_b[0].rearrange("(m p) -> p m", m=2)).then_inc(small_par_in, 16)
                sp.dma_start(posi[:, :], positions[0].rearrange("(i p) -> p i", p=P)).then_inc(small_par_in, 16)
            sp.dma_start(win[:, :, 0:A0], w_in_c[:, :, 0:A0]).then_inc(win_rest_in, 16)
            sp.wait_ge(lo_filled, F_XT(3, 1) + 1)
            sp.dma_start(wuq, w_uq[0].rearrange("(c p) n -> p c n", p=P)).then_inc(wproj_in, 16)
            sp.dma_start(wukv, w_ukv[0]).then_inc(wproj_in, 16)
            sp.dma_start(wglu, w_glu[0].rearrange("(c p) n -> p c n", p=P)).then_inc(wproj_in, 16)
            sp.wait_ge(hk_saved, 1)
            for t in range(STEP):
                for h in range(2):
                    sp.dma_start(toep.rearrange("p (r h) n -> p r h n", h=2)[t * C:(t + 1) * C, :, h, t * C:P],
                                 Hk[h * C:(h + 1) * C, :, 0:STEP - t, :].rearrange("p r t c -> p r (t c)")
                                 ).then_inc(toep_in, 16)
            sp.wait_ge(lo_drained, F_U(NT - 1) + 1)
            sp.dma_start(kpe_d.rearrange("(p i) d -> p i d", i=NT), kst).then_inc(kst_out, 16)
            sp.wait_ge(kst_out, 16)
            sp.dma_start(kpe, kpe_d.rearrange("(i p) d -> p i d", p=P)).then_inc(kpe_in, 16)
            sp.wait_ge(mid_done, 1)
            sp.dma_start(wout, w_out[0].rearrange("(c p) n -> p c n", p=P)).then_inc(wout_in, 16)
            sp.wait_ge(o_saved, H * NT)
            sp.dma_start(x2, x_s).then_inc(x_again, 16)
            sp.wait_ge(oT_filled, NT)
            sp.dma_start(fnorm, ffn_norm[0].partition_broadcast(P)).then_inc(x_again, 16)
            for b in range(2):
                sp.dma_start(w13[b][0], w1_e[b]).then_inc(W13_IN[b], 16)
                sp.dma_start(w13[b][1], w3_e[b]).then_inc(W13_IN[b], 16)
            for i in range(NT):
                sp.wait_ge(h2_ready, i + 1)
                sp.dma_start(h2_s[:, i, :], h2[i % 2]).then_inc(H2_OUT[i % 2], 16)
                sp.dma_start(out_s[:, i, :], x2[:, i, :]).then_inc(out_stored, 16)
            for b in range(2):
                sp.wait_ge(H2_OUT[b], 8 * NT)
            sp.wait_ge(lg_filled, NT)
            sp.wait_ge(tab_rows_out, 16 * 2 * NT)
            sp.wait_ge(x2_squared, NT)
            sp.dma_start(tabi, tab_d.rearrange("(p b) k -> p b k", p=P)).then_inc(tab_in, 16)

            sp.wait_ge(ov_table, 1)
            for b in range(2):
                sp.wait_ge(ROWS_IN[b], 16)
            sp.dma_start(w2s[0], w2_e[0]).then_inc(w2_a_in, 16)
            sp.dma_start(w2s[1], w2_e[1]).then_inc(w2_b_in, 16)

            with sp.Fori(0, NE // 2 - 1) as it:
                for b in range(2):
                    sp.wait_ge(a_filled, 2 * it + (b + 1))
                    sp.dma_start(w13[b][0], w1_e[2 * it + (b + 2)]).then_inc(W13_IN[b], 16)
                    sp.wait_ge(b_filled, 2 * it + (b + 1))
                    sp.dma_start(w13[b][1], w3_e[2 * it + (b + 2)]).then_inc(W13_IN[b], 16)
                    sp.wait_ge(y_filled, 2 * it + (b + 1))
                    sp.dma_start(w2s[b], w2_e[2 * it + (b + 2)]).then_inc(W2_IN[b], 16)

            sp.wait_ge(ov_table, 1)
            n_ov = sp.value_load(ovi[0:1, 0, OVF + 1:OVF + 2], min_val=0, max_val=OVF)
            with sp.Fori(0, OVF // 2) as it:
                for b in range(2):
                    with sp.If(n_ov > 2 * it + b):
                        e = sp.value_load(ovi[0:1, 0, bass.ds(2 * it + b, 1)], min_val=0, max_val=NE - 1)
                        sp.wait_ge(b_filled, 2 * it + (NE - 1 + b))
                        sp.dma_start(w13[b][0], w1_e[e]).then_inc(OV_W_IN[b], 16)
                        sp.dma_start(w13[b][1], w3_e[e]).then_inc(OV_W_IN[b], 16)
                        sp.wait_ge(y_filled, 2 * it + (NE - 1 + b))
                        sp.dma_start(w2s[b], w2_e[e]).then_inc(OV_W2_IN[b], 16)

        @block.gpsimd
        def _(pool):
            seq = [0]

            def link(ins):
                seq[0] += 1
                ins.then_inc(pool_seq, 1)
                pool.wait_ge(pool_seq, seq[0])

            def settle():
                pool.sem_inc(pool_steps, 1)

            def rms(col_in, col_out, n, width, eps, what):
                link(pool.tensor_scalar(st[:, col_out:col_out + width], st[:, col_in:col_in + width],
                                        1.0 / n, eps, ALU.mult, ALU.add))
                pool.tensor_tensor(st[:, col_out:col_out + width], st[:, col_out:col_out + width],
                                   minus_half[:, 0:width], ALU.pow).then_inc(what, 1)

            pool.memset(minus_half[:, :], -0.5)
            pool.memset(halfpi[:, :], PI / 2)
            for k in range(HR):
                pool.memset(freq[:, k:k + 1], float(np.float32(10000.0 ** (-2.0 * k / RD))))
            for k in range(8):
                pool.memset(wrank[:, k:k + 1], 8.0 - k)
            pool.memset(ones[:, :], 1.0)
            pool.memset(before[:, :], 1.0)
            pool.memset(upad[:, :, 0:TAPS - 1], 0.0)
            pool.iota(iota_j[:, :], [[1, P]], base=0, channel_multiplier=0, allow_small_or_imprecise_dtypes=True)
            pool.iota(eiota[:, :], [[1, NE]], base=0, channel_multiplier=0, allow_small_or_imprecise_dtypes=True)
            for k in range(2):
                pool.iota(pay[:, :, k, 0], [[1, NT]], base=0, channel_multiplier=NT)
            pool.memset(tab0, SKIP_ROW)
            link(pool.memset(ident[:, :], 0.0))
            pool.affine_select(out=ident[:, :], in_=ident[:, :], compare_op=ALU.not_equal, fill=1.0,
                               base=0, pattern=[[-1, P]], channel_multiplier=1)
            link(pool.affine_select(out=before[:, :], in_=before[:, :], compare_op=ALU.is_gt, fill=0.0,
                                    base=0, pattern=[[1, P]], channel_multiplier=-1))
            pool.tensor_tensor(dmask[:, :], ident[0:2 * C, 0:C], ident[0:2 * C, C:2 * C], ALU.add).then_inc(consts_made, 1)
            pool.memset(toep, 0.0).then_inc(consts_made, 1)
            pool.wait_ge(consts_made, 2)
            pool.dma_start(tab_d.rearrange("(p b) k -> p b k", p=P), tab0).then_inc(tab_cleared, 16)

            for i in range(NT):
                pool.wait_ge(x_squared, i + 1)
                rms(i, 8 + i, D, 1, EPS, x_rms)
            with nc.allow_non_contiguous_dma(reason="parameters of a few KiB"):
                for k, v in enumerate((ln_w, ln_b)):
                    pool.dma_start(lnwb[:, k, :], v[0].partition_broadcast(P)).then_inc(row_par_in, 16)
                for k, v in enumerate((q_norm, k_norm)):
                    pool.dma_start(qkw[:, k, :], v[0].partition_broadcast(P)).then_inc(row_par_in, 16)
                pool.dma_start(wr[:, :, 0:EG], w_grp[0].rearrange("(c p) n -> p c n", p=P)).then_inc(row_par_in, 16)
                pool.dma_start(wr[:, :, EG:EG + NE], w_exp[0].rearrange("(c p) n -> p c n", p=P)).then_inc(row_par_in, 16)
                pool.dma_start(brow[:, 0:EG], b_grp[0].partition_broadcast(P)).then_inc(row_par_in, 16)
                pool.dma_start(brow[:, EG:EG + NE], b_exp[0].partition_broadcast(P)).then_inc(row_par_in, 16)

            for half in range(2):
                for m in range(2):
                    pool.wait_ge(lo_drained, F_AG(half, 2 * m + 1) + 1)
                    v = natural(upad[:, m, TAPS - 1:PADW], half)
                    pool.tensor_tensor(v, v, natural(sigT[:, m, :], half), ALU.mult).then_inc(upad_ready, 1)
            pool.wait_ge(wproj_in, 16 * 3)
            for c in range(2):
                pool.tensor_scalar(wuq[:, c, :], wuq[:, c, :], normc[:, 2 * KC + c:2 * KC + c + 1], None, ALU.mult)
            pool.tensor_scalar(wukv, wukv, normc[:, 2 * KC + 2:2 * KC + 3], None, ALU.mult).then_inc(wproj_scaled, 1)
            pool.wait_ge(lo_drained, F_SSQ + 1)
            rms(16, 32, QL, NT, EPS, lat_rms)
            rms(24, 40, KL, NT, EPS, lat_rms)
            def square_qk(i):
                pool.wait_ge(qk_saved, i + 1)
                if i >= 2:
                    pool.wait_ge(qk_summed, i - 1)
                qv = qraw[:, i, :].rearrange("p (h d) -> p h d", d=QH)
                kv = kraw[:, i, :].rearrange("p (h d) -> p h d", d=ND)
                pool.tensor_tensor(sqq[i % 2], qv, qv, ALU.mult)
                pool.tensor_tensor(sqk[i % 2], kv, kv, ALU.mult).then_inc(qk_squared, 1)

            for i in range(2):
                square_qk(i)
            pool.wait_ge(ln_stats, 1)
            link(pool.tensor_scalar(st[:, 112:112 + NT], bns[:, :, 7], 1.0, LN_EPS, ALU.mult, ALU.add))
            pool.tensor_tensor(st[:, 112:112 + NT], st[:, 112:112 + NT], minus_half[:, 0:NT], ALU.pow).then_inc(ln_rstd, 1)
            for i in range(2, 6):
                square_qk(i)
            pool.wait_ge(mid_squared, 1)
            rms(64, 72, CW, NT, EPS, mid_rms)
            for i in range(6, NT):
                square_qk(i)
            pool.wait_ge(mid_squared, 2)
            rms(48, 56, SW, NT, EPS, mid_rms)
            pool.wait_ge(heads_made, 2)
            with pool.Fori(1, H // 2) as it:
                pool.wait_ge(qkT_made, 2 * it)
                for b in range(2):
                    n = [b * LINKS]

                    def hlink(ins):
                        n[0] += 1
                        ins.then_inc(head_seq, 1)
                        pool.wait_ge(head_seq, (it - 1) * (2 * LINKS) + n[0])

                    for a in range(2):
                        make_heads_part(pool, hlink, settle, 2 * it + b, b, a, rot)
                    assert n[0] == (b + 1) * LINKS
                    pool.sem_inc(heads_made, 1)

            pool.wait_ge(wout_in, 16)
            for c in range(KC):
                last = pool.tensor_scalar(wout[:, c, :], wout[:, c, :], normc[:, KC + c:KC + c + 1], None, ALU.mult)
            last.then_inc(wout_scaled, 1)
            pool.wait_ge(o_squared, NT)
            rms(80, 88, AW, NT, EPS, o_rms)
            for i in range(NT):
                pool.wait_ge(x2_squared, i + 1)
                rms(96 + i, 104 + i, D, 1, EPS, x2_rms)

            pool.wait_ge(out_filled, NT)
            for b in range(2):
                link(pool.memset(xg[b], 0.0))
            pool.wait_ge(tab_cleared, 16)
            for i in range(NT):
                for part in range(2):
                    if i == ROUTE[part][0]:
                        pool.wait_ge(slots_ready, part + 1)
                for k in range(2):
                    pool.indirect_dma_start(out=tab_d, out_offset=bass.IndirectOffsetOnAxis(ap=slot[:, i, k:k + 1], axis=0),
                                            in_=pay[:, i, k, :], in_offset=None).then_inc(tab_rows_out, 16)
            pool.wait_ge(tab_in, 16)
            for b in range(2):
                pool.wait_ge(H2_OUT[b], 8 * NT)

            def gather(b, e, row=None):
                pool.tensor_copy(idx[:, b, :], tabi[:, bass.ds(e if row is None else row, 1), :].rearrange("p a k -> p (a k)")).then_inc(idxg_copied, 1)
                pool.wait_ge(idxg_copied, e + 1)
                settle()
                pool.indirect_dma_start(out=xg[b], out_offset=None, in_=h2_d,
                                        in_offset=bass.IndirectOffsetOnAxis(ap=idx[:, b, 0:1], axis=0),
                                        bounds_check=T - 1, oob_is_err=False).then_inc(ROWS_IN[b], 16)

            def table_block(o):
                return pool.value_load(ovi[0:1, 1, bass.ds(o, 1)], min_val=0, max_val=NBLK - 1)

            def prepare(b, e, row=None):
                pool.tensor_copy(idx[:, 2 + b, :], tabi[:, bass.ds(e if row is None else row, 1), :].rearrange("p a k -> p (a k)")).then_inc(idxs_copied, 1)

            def scatter(b, e):
                pool.wait_ge(y_saved_a, e + 2)
                pool.wait_ge(y_saved_v, e + 2)
                settle()
                pool.indirect_dma_start(out=out_d, out_offset=bass.IndirectOffsetOnAxis(ap=idx[:, 2 + b, 0:1], axis=0),
                                        in_=ye[b], in_offset=None, bounds_check=T - 1, oob_is_err=False,
                                        compute_op=ALU.add).then_inc(Y_OUT[b], 16)

            prepare(0, 0)
            gather(0, 0)
            gather(1, 1)
            for e in range(2):
                pool.wait_ge(xgT_filled, e + 1)
                gather(e, e + 2)
            pool.wait_ge(out_stored, 16 * NT)

            def two_blocks(it):
                for b in range(2):
                    e = 2 * it + b
                    pool.wait_ge(xgT_filled, e + 1)
                    settle()
                    gather(b, e + 2)
                    if b == 1:
                        pool.wait_ge(Y_OUT[0], 16 * it)
                    elif not isinstance(it, int):
                        pool.wait_ge(Y_OUT[1], 16 * (it - 1))
                    settle()
                    prepare(1 - b, e - 1)
                    scatter(b, e - 2)

            two_blocks(1)
            with pool.Fori(2, NE // 2 - 1) as it:
                two_blocks(it)
            n_ov = pool.value_load(ovi[0:1, 0, OVF + 1:OVF + 2], min_val=0, max_val=OVF)
            for e in range(NE - 2, NE + 2):
                b = e % 2
                if e < NE:
                    with pool.If(n_ov > b):
                        pool.wait_ge(xgT_filled, e + 1)
                        gather(b, e + 2, table_block(b))
                pool.wait_ge(Y_OUT[1 - b], 16 * ((e - 2 - b) // 2 + b))
                prepare(1 - b, e - 1, table_block(0) if e - 1 == NE else None)
                scatter(b, e - 2)
            pool.wait_ge(Y_OUT[1], 8 * NE)
            with pool.Fori(0, OVF // 2) as it:
                for b in range(2):
                    with pool.If(n_ov > 2 * it + b):
                        with pool.If(n_ov > 2 * it + (b + 2)):
                            pool.wait_ge(xgT_filled, 2 * it + (NE + b + 1))
                            settle()
                            gather(b, 2 * it + (NE + b + 2), table_block(2 * it + (b + 2)))
                        prepare(1 - b, 2 * it + (NE + b + 1), table_block(2 * it + (b + 1)))
                        scatter(b, 2 * it + (NE + b))
                        pool.wait_ge(Y_OUT[b], 16 * it + 16 * (NE // 2 + 1))
                        settle()

        @block.scalar
        def _(act):
            seq = [0]

            def link(ins):
                seq[0] += 1
                ins.then_inc(act_seq, 1)
                act.wait_ge(act_seq, seq[0])

            def lo(n):
                return psum[:, n % 4, :]

            def save_xT(i):
                for k in range(2):
                    act.wait_ge(lo_filled, F_XT(i, k) + 1)
                    act.activation(hT[:, 4 * k:4 * k + 4, i, :], lo(F_XT(i, k)).rearrange("p (c j) -> p c j", c=4),
                                   ACT.Copy).then_inc(lo_drained, 1)

            def square_x(i):
                if i % 2 == 0:
                    act.wait_ge(X_IN[i // 2], 16)
                if i >= 1:
                    act.wait_ge(x_squared, i)
                act.activation(tmp, xin[i // 2][:, i % 2, :], ACT.Square, accum_out=st[:, i:i + 1]).then_inc(x_squared, 1)

            def scale_x(i):
                act.wait_ge(x_rms, i + 1)
                act.activation(xin[i // 2][:, i % 2, :], xin[i // 2][:, i % 2, :], ACT.Copy, scale=st[:, 8 + i:9 + i]).then_inc(x_normed, 1)

            def save_ag(half):
                for m in range(2):
                    n = F_AG(half, 2 * m)
                    act.wait_ge(lo_filled, n + 1)
                    act.activation(natural(sigT[:, m, :], half), lo(n).rearrange("p (i j) -> p i j", i=4),
                                   ACT.Sigmoid).then_inc(lo_drained, 1)
                    act.wait_ge(lo_filled, n + 2)
                    act.activation(natural(upad[:, m, TAPS - 1:PADW], half), lo(n + 1).rearrange("p (i j) -> p i j", i=4),
                                   ACT.Copy).then_inc(lo_drained, 1)

            square_x(0)
            for i in range(NT):
                if i + 1 < NT:
                    square_x(i + 1)
                scale_x(i)
                if 1 <= i <= 4:
                    save_xT(i - 1)
            act.wait_ge(trig_ready, 1)
            act.activation(sc[:, 7, :], sc[:, 5, :], ACT.Sin, scale=0.5)
            act.activation(sc[:, 8, :], sc[:, 5, :], ACT.Sin).then_inc(trig_done, 1)
            act.wait_ge(consts_made, 1)
            act.wait_ge(phase_ready, 1)
            act.activation(sinj, sinj, ACT.Sin, scale=TWO_PI_SAFE)
            act.activation(cosj, cosj, ACT.Sin, scale=-TWO_PI_SAFE, bias=halfpi[:, 0:1]).then_inc(tables_made, 1)
            act.wait_ge(rope_ang, 1)
            for k in range(2):
                act.activation(rope[:, k, :, HR:RD], rope[:, k, :, 0:HR], ACT.Sin,
                               **(dict(scale=-1.0, bias=halfpi[:, 0:1]) if k == 0 else {})).then_inc(rope_made, 1)
            save_ag(0)
            for i in range(4, NT):
                save_xT(i)
            save_ag(1)
            act.wait_ge(hi_filled, R_W + 1)
            for k in range(4):
                last = act.activation(WT[:, k // 2, 4 * (k % 2):4 * (k % 2) + 4, :],
                                      psum[:, 4 + k, :].rearrange("p (r n) -> p r n", r=4), ACT.Copy)
            last.then_inc(hi_drained, 1)
            act.wait_ge(ssm_w_ready, 1)
            for i in range(NT):
                n = F_U(i)
                act.wait_ge(lo_filled, n + 1)
                act.activation(kst[:, i, :], lo(n)[:, 0:RD], ACT.Copy)
                act.activation(utok[:, :, i, :], lo(n)[:, RD:RD + SW].rearrange("p (g c) -> p g c", c=C),
                               ACT.Copy).then_inc(lo_drained, 1)
            act.wait_ge(hi_filled, R_H + 1)
            for k in range(2):
                last = act.activation(Hk[:, 4 * k:4 * k + 4, :, :].rearrange("p r t c -> p r (t c)"),
                                      psum[0:2 * C, 4 + k, :].rearrange("p (r n) -> p r n", r=4), ACT.Copy)
            last.then_inc(hi_drained, 1)
            act.wait_ge(hi_filled, R_U + 1)
            for k in range(4):
                last = act.activation(U[:, 4 * k:4 * k + 4, :], psum[:, 4 + k, :].rearrange("p (g j) -> p g j", g=4), ACT.Copy)
            last.then_inc(hi_drained, 1)
            act.wait_ge(tab_cleared, 16)
            act.wait_ge(upad_ready, 4)
            for half in range(2):
                for m in range(3):
                    n = F_LAT(half, m)
                    act.wait_ge(lo_filled, n + 1)
                    dst = cqT[:, m, :] if m < 2 else ckvT
                    act.activation(natural(dst, half), lo(n).rearrange("p (i j) -> p i j", i=4), ACT.Copy).then_inc(lo_drained, 1)
            act.wait_ge(lo_drained, F_LAT(1, 2) + 1)
            for m in range(3):
                last = act.activation(sqc[:, m, :], cqT[:, m, :] if m < 2 else ckvT, ACT.Square)
            last.then_inc(lat_squared, 1)
            act.wait_ge(lo_filled, F_SSQ + 1)
            act.activation(st[:, 16:16 + 2 * NT], lo(F_SSQ)[:, 0:2 * NT], ACT.Copy).then_inc(lo_drained, 1)
            act.wait_ge(lat_rms, 2)

            def save_qkv(i):
                for k in range(2):
                    n = F_QKV(i, k)
                    act.wait_ge(lo_filled, n + 1)
                    act.activation(qraw[:, i, k * 384:k * 384 + 384], lo(n)[:, 0:384], ACT.Copy,
                                   scale=st[:, 32 + i:33 + i]).then_inc(lo_drained, 1)
                for k in range(2):
                    n = F_QKV(i, 2 + k)
                    act.wait_ge(lo_filled, n + 1)
                    v = lo(n).rearrange("p (h d) -> p h d", d=ND + VD)
                    for dst, d0 in ((kraw, 0), (vtok, ND)):
                        last = act.activation(dst[:, i, k * 256:k * 256 + 256].rearrange("p (h d) -> p h d", d=ND),
                                              v[:, :, d0:d0 + ND], ACT.Copy, scale=st[:, 40 + i:41 + i])
                    link(last)
                    act.sem_inc(lo_drained, 1)
                act.sem_inc(qk_saved, 1)

            for i in range(5):
                save_qkv(i)
            act.wait_ge(ln_done, 1)
            link(act.activation(ctok, ctok, ACT.Silu))
            for i in range(NT):
                link(act.activation(tmp[:, 0:CW], ctok[:, i, :], ACT.Square, accum_out=st[:, 64 + i:65 + i]))
            act.sem_inc(mid_squared, 1)
            act.wait_ge(ssm_x_ready, 1)
            act.wait_ge(hi_filled, R_Y + 1)
            z_v = yssm.rearrange("p t (r h c) -> p h r t c", h=2, c=C)
            for h in range(2):
                for k in range(2):
                    for t4 in range(4):
                        last = act.activation(z_v[:, h, 4 * k + t4, :, :],
                                              psum[:, 4 + 2 * h + k, t4 * P:(t4 + 1) * P].rearrange("p (t c) -> p t c", c=C),
                                              ACT.Gelu_apprx_tanh)
            link(last)
            act.sem_inc(z_ready, 1)
            act.sem_inc(hi_drained, 1)
            for i in range(5, NT):
                save_qkv(i)
            act.wait_ge(hi_filled, R_Z + 1)
            for k in range(4):
                last = act.activation(zT.rearrange("p c (k i j) -> p k i c j", k=4, i=2)[:, k],
                                      psum[:, 4 + k, :].rearrange("p (i c j) -> p i c j", i=2, c=2), ACT.Copy)
            last.then_inc(hi_drained, 1)
            act.wait_ge(qk_mean, 1)
            act.activation(at(14336 + 2816, 2 * NT * H), qks.rearrange("p a i h -> p (a i h)"), ACT.Sqrt).then_inc(qk_root, 1)
            act.wait_ge(hi_filled, R_GLU + 1)
            for k in range(4):
                last = act.activation(sout[:, 2 * k:2 * k + 2, :], psum[:, 4 + k, :].rearrange("p (i n) -> p i n", i=2), ACT.Sigmoid)
            link(last)
            act.sem_inc(hi_drained, 1)
            act.sem_inc(sigm_done, 1)
            act.wait_ge(mid_rms, 1)
            for i in range(NT):
                last = act.activation(ctok[:, i, :], ctok[:, i, :], ACT.Copy, scale=st[:, 72 + i:73 + i])
            link(last)
            act.sem_inc(mid_scaled, 1)
            act.wait_ge(glu_done, 1)
            for i in range(NT):
                link(act.activation(tmp[:, 0:SW], sout[:, i, :], ACT.Square, accum_out=st[:, 48 + i:49 + i]))
            act.sem_inc(mid_squared, 1)

            def save_yT(r, c0):
                act.wait_ge(hi_filled, r + 1)
                for k in range(4):
                    last = act.activation(yT[:, c0:c0 + 2].rearrange("p c (k i) j -> p k i c j", k=4)[:, k],
                                          psum[:, 4 + k, :].rearrange("p (i c j) -> p i c j", i=2, c=2), ACT.Copy)
                last.then_inc(hi_drained, 1)

            save_yT(R_COUT, 2)
            act.wait_ge(mid_rms, 2)
            for i in range(NT):
                last = act.activation(sout[:, i, :], sout[:, i, :], ACT.Copy, scale=st[:, 56 + i:57 + i])
            link(last)
            act.sem_inc(mid_scaled, 1)
            save_yT(R_SOUT, 0)
            act.wait_ge(hi_drained, R_SOUT + 1)
            act.sem_inc(mid_done, 1)

            with act.Fori(0, H // 2) as it:
                it16, itF = act.snap(STEPS * it), act.snap(FILLS * it)
                ita, itv = act.snap(saved_a[FILLS] * it), act.snap(saved_v[FILLS] * it)

                def save_kT(b):
                    act.wait_ge(qkT_made, 2 * it + (b + 1))
                    last = act.activation(kT[b][0:QH, :].rearrange("p (k n) -> p k n", k=2), psum[0:QH, 4 * b + 2:4 * b + 4, :], ACT.Copy)
                    last.then_inc(kT_saved, 1)

                def exponentials(n):
                    act.wait_ge(s_max, it16 + (n + 1))
                    if n >= 2:
                        act.wait_ge(pT_filled, itF + first_fill[n - 1])
                    i, a = tile_of[n], am[:, n % 4, :]
                    L = (i + 1) * P
                    act.activation(prob[n % 2][:, 0:L], psum[:, 2 * (n % 2):2 * (n % 2) + 2, :].rearrange("p a n -> p (a n)")[:, 0:L],
                                   ACT.Exp, bias=a[:, 0:1], accum_out=a[:, 1:2]).then_inc(p_ready, 1)

                for b in range(2):
                    save_kT(b)
                exponentials(0)
                exponentials(1)
                for n in range(STEPS):
                    for f in range(first_fill[n], first_fill[n + 1]):
                        if not by_dve[f]:
                            act.wait_ge(pT_filled, itF + (f + 1))
                            w = min(4, tile_of[n] + 1 - 4 * (f - first_fill[n]))
                            if f >= 4:
                                act.wait_ge(pv_done, itF + (f - 3))
                            act.activation(probT[f % 4][:, 0:w, :], psum[:, 4 + f % 2, 0:w * P].rearrange("p (a n) -> p a n", n=P),
                                           ACT.Copy).then_inc(pT_saved_a, 1)
                    if n + 2 < STEPS:
                        exponentials(n + 2)

            act.wait_ge(o_saved, H * NT)
            for i in range(NT):
                link(act.activation(prob[0][:, 0:AW], otok[:, i, :], ACT.Square, accum_out=st[:, 80 + i:81 + i]))
            act.sem_inc(o_squared, NT)
            act.wait_ge(o_rms, 1)
            for i in range(NT):
                act.activation(otok[:, i, :], otok[:, i, :], ACT.Copy, scale=st[:, 88 + i:89 + i]).then_inc(o_scaled, 1)
            for i in range(NT):
                act.wait_ge(oT_filled, i + 1)
                for c in range(4):
                    last = act.activation(oT[:, c, :, 16 * i:16 * i + 16].rearrange("p i j -> p j i"),
                                          psum[:, i % 4, c * P:(c + 1) * P].rearrange("p (j i) -> p j i", i=NT), ACT.Copy)
                last.then_inc(oT_saved, 1)
            def gate_exponentials(part):
                i0, i1 = ROUTE[part]
                act.wait_ge(expg_in, part + 1)
                act.activation(expg[:, i0:i1], expg[:, i0:i1], ACT.Exp).then_inc(expg_done, 1)
                act.wait_ge(expe_in, part + 1)
                act.activation(expe[:, i0:i1], expe[:, i0:i1], ACT.Exp).then_inc(expe_done, 1)

            for i in range(NT):
                act.wait_ge(x2_ready, i + 1)
                link(act.activation(junk, x2[:, i, :], ACT.Square, accum_out=st[:, 96 + i:97 + i]))
                act.sem_inc(x2_squared, 1)
                act.wait_ge(h2T_filled, i + 1)
                act.activation(h2T.rearrange("p (k c) n -> p k (c n)", k=2), psum[:, 4:6, :], ACT.Copy).then_inc(h2T_saved, 1)
                if i == NT - 2:
                    gate_exponentials(0)
            gate_exponentials(1)

            def save_xgT(e):
                act.wait_ge(xgT_filled, e + 1)
                act.activation(xgT.rearrange("p (k c) n -> p k (c n)", k=2), psum[:, 3:5, :], ACT.Copy).then_inc(xgT_saved, 1)

            def silu(e):
                if not isinstance(e, int) or e >= 1:
                    act.wait_ge(he_ready, e)
                act.wait_ge(a_filled, e + 1)
                act.activation(sil, psum[:, 0, :], ACT.Silu).then_inc(silu_e, 1)

            def save_y(b, e):
                act.wait_ge(idxs_copied, e + 1)
                act.wait_ge(y_filled, e + 1)
                act.activation(ye[b][:, 0:512], psum[:, 5, :], ACT.Copy, scale=idx[:, 2 + b, 1:2].bitcast(F32)).then_inc(y_saved_a, 1)

            def high_w2(b, e, arrived, n):
                act.wait_ge(arrived, n)
                act.activation(w2h[b], w2s[b], ACT.Copy).then_inc(w2h_ready, 1)

            act.wait_ge(out_stored, 16 * NT)
            act.sem_inc(y_saved_a, 1)
            save_xgT(0)
            silu(0)
            save_xgT(1)
            high_w2(0, 0, W2_IN[0], 16)

            with act.Fori(0, NE // 2 - 1) as it:
                for b in (1, 0):
                    e = 2 * it + (2 - b)
                    silu(e)
                    save_xgT(e + 1)
                    save_y(1 - b, e - 1)
                    high_w2(b, e, W2_IN[b], 16 * it + 16 * (2 - b))
            silu(NE - 1)
            high_w2(1, NE - 1, W2_IN[1], 8 * NE)
            save_y(0, NE - 2)
            save_y(1, NE - 1)
            n_ov = act.value_load(ovi[0:1, 0, OVF + 1:OVF + 2], min_val=0, max_val=OVF)
            with act.Fori(0, OVF // 2) as it:
                for b in range(2):
                    with act.If(n_ov > 2 * it + b):
                        e = 2 * it + (NE + b)
                        save_xgT(e)
                        high_w2(b, e, OV_W2_IN[b], 16 * it + 16)
                        silu(e)
                        save_y(b, e)

        @block.vector
        def _(dve):
            seq = [0]

            def link(ins):
                seq[0] += 1
                ins.then_inc(dve_seq, 1)
                dve.wait_ge(dve_seq, seq[0])

            def tt(out_, a, b_, op):
                link(dve.tensor_tensor(out_, a, b_, op))

            def ts(out_, a, s1, s2, op0, op1=None):
                link(dve.tensor_scalar(out_, a, s1, s2, op0, *(() if op1 is None else (op1,))))

            def stt(out_, a, s1, b_, op0, op1):
                link(dve.scalar_tensor_tensor(out_, a, s1, b_, op0, op1))

            def v(k):
                return sc[:, k, :]

            M_, A_, S_ = ALU.mult, ALU.add, ALU.subtract

            def scale_w_in(arrived, c0, c1, done):
                dve.wait_ge(arrived, 16)
                for c in range(KC):
                    last = dve.tensor_scalar(win[:, c, c0:c1], win[:, c, c0:c1], normc[:, c:c + 1], None, M_)
                last.then_inc(done, 1)

            dve.wait_ge(mix_norm_in, 16)
            scale_w_in(win_ag_in, A0, NIN, win_ag_scaled)
            dve.wait_ge(ssm_par_in, 16 * 11)
            lr, li = lamc[:, 0, :], lamc[:, 1, :]
            ts(v(0), lamc[:, 2, :], 1.0 / 16, None, M_)
            ts(v(1), v(0), 1.0 / 9, 1.0, M_, A_)
            for k in range(8, 0, -1):
                tt(v(1), v(1), v(0), M_)
                ts(v(1), v(1), 1.0 / k, 1.0, M_, A_)
            for _ in range(4):
                tt(v(1), v(1), v(1), M_)
            tt(v(2), lr, v(1), M_)
            ts(v(3), v(2), -20.0, 1.0 / 16, ALU.max, M_)
            ts(v(4), v(3), 1.0 / 7, 1.0, M_, A_)
            for k in range(6, 1, -1):
                tt(v(4), v(4), v(3), M_)
                ts(v(4), v(4), 1.0 / k, 1.0, M_, A_)
            tt(v(4), v(4), v(3), M_)
            for _ in range(4):
                stt(v(4), v(4), 2.0, v(4), A_, M_)

            def reduce_angle(x_, turns):
                ts(turns, x_, 1.0 / (2 * PI), ROUND, M_, A_)
                ts(turns, turns, ROUND, None, S_)
                stt(x_, turns, -TWO_PI_HI, x_, M_, A_)
                stt(x_, turns, -TWO_PI_LO, x_, M_, A_)
                ts(x_, x_, 3.1415925, -3.1415925, ALU.min, ALU.max)

            tt(v(5), li, v(1), M_)
            reduce_angle(v(5), v(6))
            dve.sem_inc(trig_ready, 1)
            ts(v(10), v(5), float(STEP), None, M_)
            reduce_angle(v(10), v(11))
            ts(v(10), v(10), 1.0 / (2 * PI), None, M_)
            ts(v(11), v(10), ROUND16, None, A_)
            ts(v(11), v(11), ROUND16, None, S_)
            tt(v(12), v(10), v(11), S_)
            dve.wait_ge(consts_made, 1)
            jb = iota_j[:, :].unsqueeze(1).to_broadcast([P, NPAIR, NJ])

            def wide(col):
                return col.unsqueeze(2).to_broadcast([P, NPAIR, NJ])

            tt(sinj, wide(v(11)), jb, M_)
            ts(cosj, sinj, ROUND, None, A_)
            ts(cosj, cosj, ROUND, None, S_)
            tt(sinj, sinj, cosj, S_)
            tt(cosj, wide(v(12)), jb, M_)
            tt(sinj, sinj, cosj, A_)
            ts(cosj, sinj, ROUND, None, A_)
            ts(cosj, cosj, ROUND, None, S_)
            tt(sinj, sinj, cosj, S_)
            ts(sinj, sinj, 0.5, -0.5, ALU.min, ALU.max)
            fl = "p r j -> p (r j)"
            stt(cosj.rearrange(fl), sinj.rearrange(fl), -1.0, sinj.rearrange(fl), M_, ALU.max)
            dve.sem_inc(phase_ready, 1)
            dve.wait_ge(small_par_in, 16 * 7)
            link(dve.tensor_copy(posf[:, :], posi[:, :]))
            ang, turns = rope[:, 1, :, 0:HR], rope[:, 0, :, 0:HR]
            tt(ang, posf[:, :].unsqueeze(2).to_broadcast([P, NT, HR]),
               freq[:, :].unsqueeze(1).to_broadcast([P, NT, HR]), M_)
            reduce_angle(ang, turns)
            stt(turns, ang, -1.0, ang, M_, ALU.max)
            dve.sem_inc(rope_ang, 1)
            scale_w_in(win_rest_in, 0, A0, win_scaled)
            dve.wait_ge(trig_done, 1)
            tt(v(7), v(7), v(7), M_)
            ts(v(7), v(7), -2.0, None, M_)
            stt(v(9), v(7), 1.0, v(4), A_, M_)
            tt(v(9), v(9), v(7), A_)
            link(dve.memset(Lp[:, 0, 0, :], 1.0))
            link(dve.memset(Lp[:, 1, 0, :], 0.0))
            ts(Lp[:, 0, 1, :], v(9), 1.0, None, A_)
            stt(Lp[:, 1, 1, :], v(4), 1.0, v(8), A_, M_)

            def lpow(k, n):
                a = [Lp[:, c, 1:1 + n, :] for c in range(2)]
                m = [Lp[:, c, k:k + 1, :].to_broadcast([P, n, NPAIR]) for c in range(2)]
                o = [Lp[:, c, k + 1:k + 1 + n, :] for c in range(2)]
                t_ = sc[:, 14:14 + n, :]
                tt(o[0], a[0], m[0], M_)
                tt(t_, a[1], m[1], M_)
                tt(o[0], o[0], t_, S_)
                tt(o[1], a[0], m[1], M_)
                tt(t_, a[1], m[0], M_)
                tt(o[1], o[1], t_, A_)

            lpow(1, 1)
            lpow(2, 2)
            lpow(4, 4)
            for t in range(STEP):
                link(dve.tensor_copy(Lv[:, :, t, :], Lp[:, :, STEP - 1 - t, :]))
            ts(v(13), v(4), 1.0, None, A_)
            for _ in range(3):
                tt(v(13), v(13), v(13), M_)
            link(dve.tensor_copy(decay, wide(v(13))))
            link(dve.memset(decay[:, :, 0:1], 0.0))
            tt(v(14), lr, lr, M_)
            tt(v(15), li, li, M_)
            tt(v(14), v(14), v(15), A_)
            link(dve.reciprocal(v(14), v(14)))
            tt(v(18), v(9), lr, M_)
            tt(v(15), Lp[:, 1, 1, :], li, M_)
            tt(v(18), v(18), v(15), A_)
            tt(v(18), v(18), v(14), M_)
            tt(v(19), Lp[:, 1, 1, :], lr, M_)
            tt(v(15), v(9), li, M_)
            tt(v(19), v(19), v(15), S_)
            tt(v(19), v(19), v(14), M_)

            def cmul(out_, a, b_, t_):
                tt(out_[0], a[0], b_[0], M_)
                tt(t_, a[1], b_[1], M_)
                tt(out_[0], out_[0], t_, S_)
                tt(out_[1], a[0], b_[1], M_)
                tt(t_, a[1], b_[0], M_)
                tt(out_[1], out_[1], t_, A_)

            T4 = at(S0 + 8192 - 2048, NPAIR, STEP, C)
            cmul([Bb[:, k] for k in range(2)], [v(k).unsqueeze(2).to_broadcast([P, NPAIR, C]) for k in (18, 19)],
                 [Braw[:, k] for k in range(2)], T4[:, :, 0, :])
            cmul([W[:, k] for k in range(2)],
                 [Lv[:, k].rearrange("p t r -> p r t").unsqueeze(3).to_broadcast([P, NPAIR, STEP, C]) for k in range(2)],
                 [Bb[:, k].unsqueeze(2).to_broadcast([P, NPAIR, STEP, C]) for k in range(2)], T4)
            link(dve.memset(Bz, 0.0))
            for h in range(2):
                link(dve.tensor_copy(Bz[h * S:(h + 1) * S, :, :, h, :], Bb[h * S:(h + 1) * S]))
            dve.sem_inc(ssm_w_ready, 1)
            dve.wait_ge(hi_filled, R_C + 1)
            link(dve.tensor_copy(CTt.rearrange("p a r c -> p a (r c)"), psum[:, 4, 0:2 * P].rearrange("p (a n) -> p a n", a=2)))
            dve.sem_inc(hi_drained, 1)
            T5 = at(S0 + 6144, NPAIR, STEP + 1, C)
            Cb = [CTt[:, k].unsqueeze(2).to_broadcast([P, NPAIR, STEP + 1, C]) for k in range(2)]
            Lb = [Lp[:, k].rearrange("p t r -> p r t").unsqueeze(3).to_broadcast([P, NPAIR, STEP + 1, C]) for k in range(2)]
            tt(CL[:, 0], Cb[0], Lb[0], M_)
            tt(T5, Cb[1], Lb[1], M_)
            tt(CL[:, 0], CL[:, 0], T5, S_)
            tt(CL[:, 1], Cb[0], Lb[1], M_)
            tt(T5, Cb[1], Lb[0], M_)
            flat = "p r t c -> p (r t c)"
            stt(CL[:, 1].rearrange(flat), CL[:, 1].rearrange(flat), -1.0, T5.rearrange(flat), M_, S_)
            dve.sem_inc(ssm_c_ready, 1)
            dve.wait_ge(rope_made, 2)
            link(dve.tensor_copy(rope[:, 0, :, 0:HR], rope[:, 0, :, HR:RD]))
            ts(rope[:, 1, :, 0:HR], rope[:, 1, :, HR:RD], -1.0, None, M_)
            dve.sem_inc(rope_made, 1)
            dve.wait_ge(upad_ready, 4)
            dve.wait_ge(lo_filled, F_XT(NT - 1, 1) + 1)
            dve.wait_ge(hi_filled, R_W + 1)
            base, n = seq[0], 0
            for k in range(TAPS):
                for m in range(2):
                    if n >= 2:
                        dve.wait_ge(dve_seq, base + n - 1)
                    src = upad[:, m, k:k + T]
                    if k == 0:
                        ins = dve.tensor_scalar(cacc[:, m, :], src, dwc[:, m, 0:1], dwc[:, m, TAPS:TAPS + 1], M_, A_)
                    elif k < TAPS - 1:
                        ins = dve.scalar_tensor_tensor(cacc[:, m, :], src, dwc[:, m, k:k + 1], cacc[:, m, :], M_, A_)
                    else:
                        ins = dve.scalar_tensor_tensor(cperm[:, m].rearrange("p i j -> p j i"), src.rearrange("p (j i) -> p j i", i=NT),
                                                       dwc[:, m, k:k + 1], cacc[:, m, :].rearrange("p (j i) -> p j i", i=NT), M_, A_)
                    ins.then_inc(dve_seq, 1)
                    n += 1
            seq[0] += n
            dve.wait_ge(dve_seq, seq[0])
            dve.sem_inc(conv_done, 1)

            dve.wait_ge(consts_made, 2)
            dd = at(YT0 + 1864, NPAIR, C, parts=2 * C)
            tt(dd, dmask[:, :].unsqueeze(1).to_broadcast([2 * C, NPAIR, C]),
               dch[:, :].unsqueeze(2).to_broadcast([2 * C, NPAIR, C]), M_)
            dve.wait_ge(hi_drained, R_H + 1)
            tt(Hk[:, :, 0, :], Hk[:, :, 0, :], dd, A_)
            dve.sem_inc(hk_saved, 1)

            dve.wait_ge(hi_filled, R_V + 1)
            dve.wait_ge(tables_made, 1)
            Vp = [psum[:, 4 + 2 * k:6 + 2 * k, :].rearrange("p a (r j) -> p (a r) j", j=NJ) for k in range(2)]
            tmp3 = tmp.rearrange("p (r j) -> p r j", j=NJ)
            tt(Vrot[:, 0], Vp[0], cosj, M_)
            tt(tmp3, Vp[1], sinj, M_)
            tt(Vrot[:, 0], Vrot[:, 0], tmp3, A_)
            tt(Vrot[:, 1], Vp[1], cosj, M_)
            tt(tmp3, Vp[0], sinj, M_)
            dve.sem_inc(hi_drained, 1)
            tt(Vrot[:, 1], Vrot[:, 1], tmp3, S_)
            for k in range(2):
                link(dve.tensor_tensor_scan(Zs[:, k].rearrange("p r j -> p (r j)"), decay.rearrange("p r j -> p (r j)"),
                                            Vrot[:, k].rearrange("p r j -> p (r j)"), 0.0, M_, A_))
            z_ = [Zs[:, k, :, 0:NJ - 1] for k in range(2)]
            cs_, sn_ = cosj[:, :, 0:NJ - 1], sinj[:, :, 0:NJ - 1]
            for k in range(2):
                link(dve.memset(Xp[:, k, :, 0:1], 0.0))
            tt(Xp[:, 0, :, 1:NJ], z_[0], cs_, M_)
            tt(tmp3[:, :, 1:NJ], z_[1], sn_, M_)
            tt(Xp[:, 0, :, 1:NJ], Xp[:, 0, :, 1:NJ], tmp3[:, :, 1:NJ], S_)
            tt(Xp[:, 1, :, 1:NJ], z_[0], sn_, M_)
            tt(tmp3[:, :, 1:NJ], z_[1], cs_, M_)
            tt(Xp[:, 1, :, 1:NJ], Xp[:, 1, :, 1:NJ], tmp3[:, :, 1:NJ], A_)
            dve.sem_inc(ssm_x_ready, 1)

            def sum_qk(i):
                dve.wait_ge(qk_squared, i + 1)
                link(dve.reduce_sum(qks[:, 0, i, :], sqq[i % 2], AX))
                link(dve.reduce_sum(qks[:, 1, i, :], sqk[i % 2], AX))
                dve.sem_inc(qk_summed, 1)
            sum_qk(0)
            dve.wait_ge(hi_filled, R_CONV + 1)
            pc = [psum[:, 4 + i // 2, (i % 2) * CW:(i % 2 + 1) * CW] for i in range(NT)]
            for i in range(NT):
                last = dve.bn_stats(bns[:, i, 0:6], pc[i])
            link(last)
            for i in range(NT):
                last = dve.bn_aggr(bns[:, i, 6:8], bns[:, i, 0:6])
            link(last)
            dve.sem_inc(ln_stats, 1)
            dve.wait_ge(ln_rstd, 1)
            for i in range(NT):
                last = dve.tensor_scalar(ctok[:, i, :], pc[i], bns[:, i, 6:7], st[:, 112 + i:113 + i], S_, M_)
            link(last)
            dve.sem_inc(hi_drained, 1)
            dve.wait_ge(row_par_in, 16 * 8)
            tt(ctok, ctok, lnwb[:, 0, :].unsqueeze(1).to_broadcast([P, NT, CW]), M_)
            tt(ctok, ctok, lnwb[:, 1, :].unsqueeze(1).to_broadcast([P, NT, CW]), A_)
            dve.sem_inc(ln_done, 1)
            for i in range(1, NT):
                sum_qk(i)
            dve.wait_ge(kpe_in, 16)
            kp2 = at(14336 + 2560, NT, RD)
            tt(kp2, kpe, kpe, M_)
            link(dve.reduce_sum(st[:, 120:120 + NT], kp2, AX))
            tt(qks[:, 1], qks[:, 1], st[:, 120:120 + NT].unsqueeze(2).to_broadcast([P, NT, H]), A_)
            dve.sem_inc(qk_summed, 1)

            qk_f, qkr = qks.rearrange("p a i h -> p (a i h)"), at(14336 + 2816, 2 * NT * H)
            ts(qk_f, qk_f, 1.0 / QH, EPS, M_, A_)
            dve.sem_inc(qk_mean, 1)
            dve.wait_ge(qk_root, 1)
            link(dve.reciprocal(qkr, qkr))
            tt(qk_f, qk_f, qkr, M_)
            tt(qk_f, qk_f, qkr, M_)
            ts(qk_f, qk_f, -0.5, 1.5, M_, A_)
            tt(qk_f, qk_f, qkr, M_)
            ts(qkw[:, 0, :], qkw[:, 0, :], SCALE, None, M_)
            for b in range(2):
                for a in range(2):
                    make_heads_part(dve, link, None, b, b, a, rot_dve)
                    if (b, a) == (0, 0):
                        dve.wait_ge(sigm_done, 1)
                        tt(sout, sout, yssm, M_)
                        dve.sem_inc(glu_done, 1)
                dve.sem_inc(heads_made, 1)

            dve.wait_ge(mid_done, 1)
            with dve.Fori(0, H // 2) as it:
                it16, itF = dve.snap(STEPS * it), dve.snap(FILLS * it)

                def save_qT(b):
                    dve.wait_ge(qkT_made, 2 * it + (b + 1))
                    dve.tensor_copy(qT[b][0:QH, :].rearrange("p (k n) -> p k n", k=2),
                                    psum[0:QH, 4 * b:4 * b + 2, :]).then_inc(qT_saved, 1)

                def row_max(n):
                    i = tile_of[n]
                    sv = psum[:, 2 * (n % 2):2 * (n % 2) + 2, :].rearrange("p a n -> p (a n)")
                    dve.wait_ge(s_filled, it16 + (n + 1))
                    dve.memset(sv[0:P // 2, (i + 1) * P - P // 2:(i + 1) * P], NEG).then_inc(s_masked, 1)
                    dve.wait_ge(s_masked, it16 + (n + 1))
                    dve.reduce_max(am[:, n % 4, 0:1], sv[:, 0:(i + 1) * P], AX, negate=True).then_inc(s_max, 1)

                def save_o(n):
                    a = am[:, n % 4, :]
                    dve.wait_ge(p_ready, it16 + (n + 1))
                    dve.reciprocal(a[:, 2:3], a[:, 1:2]).then_inc(sum_inv, 1)
                    dve.wait_ge(sum_inv, it16 + (n + 1))
                    dve.wait_ge(pv_done, itF + first_fill[n + 1])
                    dve.tensor_scalar(otok[:, tile_of[n], bass.ds((2 * it + n // NT) * VD, VD)],
                                      psum[:, 6 + n % 2, 0:VD], a[:, 2:3], None, M_).then_inc(o_saved, 1)

                for b in range(2):
                    save_qT(b)
                row_max(0)
                row_max(1)
                for n in range(STEPS):
                    for f in range(first_fill[n], first_fill[n + 1]):
                        if by_dve[f]:
                            dve.wait_ge(pT_filled, itF + (f + 1))
                            w = min(4, tile_of[n] + 1 - 4 * (f - first_fill[n]))
                            if f >= 4:
                                dve.wait_ge(pv_done, itF + (f - 3))
                            dve.tensor_copy(probT[f % 4][:, 0:w, :], psum[:, 4 + f % 2, 0:w * P].rearrange("p (a n) -> p a n", n=P)
                                            ).then_inc(pT_saved_v, 1)
                    if n + 2 < STEPS:
                        row_max(n + 2)
                    if n >= 1:
                        save_o(n - 1)
                save_o(STEPS - 1)

            dve.wait_ge(x_again, 16 * 2)
            def save_logits(i):
                dve.wait_ge(lg_filled, i + 1)
                dve.tensor_tensor(lg[:, i, :], psum[:, 6 + i % 2, 0:EG + NE], brow[:, :], A_).then_inc(lg_saved, 1)

            def choose(part):
                i0, i1 = ROUTE[part]
                n_t = i1 - i0
                gl, el = lg[:, i0:i1, 0:EG], lg[:, i0:i1, EG:EG + NE].rearrange("p t (g k) -> p t g k", g=EG)
                og, eg, gmx, t_, a1, a2 = (v_[:, i0:i1] for v_ in (ohg, expg, gm, rt, m1, m2))
                e1, e2, h1, h2_, dif, sl = (v_[:, i0:i1] for v_ in (es, es2, oh[0], oh[1], expe, sel))

                def over(a, n_):
                    return a.unsqueeze(2).to_broadcast([P, n_t, n_])

                def first_max(hot, top, x_, n_):
                    link(dve.reduce_max(top, x_, AX))
                    tt(hot, x_, over(top, n_), ALU.is_equal)
                    tt(hot, hot, wrank[:, 8 - n_:8].unsqueeze(1).to_broadcast([P, n_t, n_]), M_)
                    link(dve.reduce_max(t_, hot, AX))
                    tt(hot, hot, over(t_, n_), ALU.is_equal)

                dve.wait_ge(lg_saved, i1)
                first_max(og, gmx, gl, EG)
                tt(eg, gl, over(gmx, EG), S_)
                dve.sem_inc(expg_in, 1)
                tt(sl, el, og.unsqueeze(3).to_broadcast([P, n_t, EG, EPG]), M_)
                link(dve.reduce_sum(e1, sl.rearrange("p t g k -> p t k g"), AX))
                first_max(h1, a1, e1, EPG)
                flat2 = "p t k -> p (t k)"
                stt(e2.rearrange(flat2), h1.rearrange(flat2), -1e30, e1.rearrange(flat2), M_, A_)
                first_max(h2_, a2, e2, EPG)
                tt(dif, a2, a1, S_)
                dve.sem_inc(expe_in, 1)
                for k in range(2):
                    tt(pick[k][:, i0:i1].rearrange("p t (g k) -> p t g k", g=EG), og.unsqueeze(3).to_broadcast([P, n_t, EG, EPG]),
                       (h1, h2_)[k].unsqueeze(2).to_broadcast([P, n_t, EG, EPG]), M_)
                tt(both[:, i0:i1], pick[0][:, i0:i1], pick[1][:, i0:i1], A_)
                if part == 0:
                    link(dve.memset(prior[:, 0, :], 0.0))
                for i in range(i0, i1):
                    tt(prior[:, i + 1, :], prior[:, i, :], both[:, i, :], A_)
                dve.sem_inc(picks_ready, 1)
                dve.wait_ge(expg_done, part + 1)
                link(dve.reduce_sum(t_, eg, AX))
                dve.wait_ge(expe_done, part + 1)
                ts(a1, dif, 1.0, None, A_)
                tt(t_, t_, a1, M_)
                link(dve.reciprocal(gate[:, 0, i0:i1], t_))
                tt(gate[:, 1, i0:i1], gate[:, 0, i0:i1], dif, M_)
                pay_f = pay.bitcast(F32)
                for k in range(2):
                    link(dve.tensor_copy(pay_f[:, i0:i1, k, 1], gate[:, k, i0:i1]))

            def place(part):
                i0, i1 = ROUTE[part]
                n_t = i1 - i0
                flat3 = "p t e -> p (t e)"
                rk, bk, more = rank[:, i0:i1], blk[:, i0:i1], both[:, i0:i1]
                dve.wait_ge(ranks_filled, part + 1)
                link(dve.tensor_copy(rk, psum[:, 2 * part, 0:n_t * NE].rearrange("p (t e) -> p t e", e=NE)))
                ts(bk, rk, 63.5, 1.0 / P, S_, M_)
                ts(bk, bk, ROUND, None, A_)
                ts(bk, bk, ROUND, None, S_)
                stt(rk.rearrange(flat3), bk.rearrange(flat3), -float(P), rk.rearrange(flat3), M_, A_)
                ts(more, bk, 1.0, None, ALU.min)
                tt(more, more, obase[:, :].unsqueeze(1).to_broadcast([P, n_t, NE]), M_)
                tt(bk, bk, more, A_)
                tt(bk, bk, eiota[:, :].unsqueeze(1).to_broadcast([P, n_t, NE]), A_)
                stt(bk.rearrange(flat3), rk.rearrange(flat3), float(NBLK), bk.rearrange(flat3), M_, A_)
                for k in range(2):
                    tt(more, pick[k][:, i0:i1], bk, M_)
                    link(dve.reduce_sum(rt[:, i0:i1], more, AX))
                    link(dve.tensor_copy(slot[:, i0:i1, k], rt[:, i0:i1]))
                dve.sem_inc(slots_ready, 1)

            ts(obase[:, :], eiota[:, :], float(MORE - 1), float(NE - 1), M_, A_)
            for i in range(NT):
                dve.wait_ge(out_filled, i + 1)
                xi = x2[:, i, :].rearrange("p (a n) -> p a n", a=2)
                dve.tensor_tensor(xi, xi, psum[:, 2 * (i % 2):2 * (i % 2) + 2, :], A_).then_inc(x2_ready, 1)
                if i >= 1:
                    save_logits(i - 1)
                dve.wait_ge(x2_rms, i + 1)
                if i >= 2:
                    dve.wait_ge(H2_OUT[i % 2], 16 * (i // 2))
                    dve.wait_ge(h2T_filled, i - 1)
                dve.scalar_tensor_tensor(h2[i % 2], x2[:, i, :], st[:, 104 + i:105 + i], fnorm, M_, M_).then_inc(h2_ready, 1)
                if i == NT - 2:
                    choose(0)
            place(0)
            save_logits(NT - 1)
            choose(1)
            place(1)
            ts(nov, psum[:, 3, 0:NE], 63.5, 1.0 / P, A_, M_)
            ts(nov, nov, ROUND, None, A_)
            ts(nov, nov, ROUND + 1.0, 0.0, S_, ALU.max)
            link(dve.memset(one32, 1.0))
            link(dve.tensor_tensor_scan(novend, one32, nov, 0.0, M_, A_))
            number = iota_j[0:1, 0:OVF + 1]
            whose, where = ovf[:, 0, 0:OVF + 1], ovf[:, 1, 0:OVF + 1]
            tt(ovt, novend[0:1, :].unsqueeze(1).to_broadcast([1, OVF + 1, NE]),
               number.unsqueeze(2).to_broadcast([1, OVF + 1, NE]), ALU.is_le)
            link(dve.reduce_sum(whose, ovt, AX))
            tt(ovt, ovt, nov[0:1, :].unsqueeze(1).to_broadcast([1, OVF + 1, NE]), M_)
            link(dve.reduce_sum(where, ovt, AX))
            ts(whose, whose, float(NE - 1), None, ALU.min)
            tt(where, number, where, S_)
            stt(where, whose, float(MORE), where, M_, A_)
            ts(where, where, float(NE), float(NBLK - 1), A_, ALU.min)
            link(dve.tensor_copy(ovf[:, 0, OVF + 1:OVF + 2], novend[0:1, NE - 1:NE]))
            link(dve.tensor_copy(ovf[:, 1, OVF + 1:OVF + 2], novend[0:1, NE - 1:NE]))
            link(dve.tensor_copy(ovi[:, :, :], ovf))
            dve.sem_inc(ov_table, 1)

            def save_heT(e):
                dve.wait_ge(heT_filled, e + 1)
                dve.tensor_copy(heTh.rearrange("p c n -> p (c n)"), psum[:, 2, :]).then_inc(heTh_saved, 1)
                dve.wait_ge(heTh_saved, e + 1)
                dve.tensor_tensor(heTl.rearrange("p c n -> p (c n)"), psum[:, 2, :],
                                  heTh.rearrange("p c n -> p (c n)").bitcast(F32), S_).then_inc(heT_saved, 1)

            def rest_w2(b, e):
                dve.wait_ge(w2h_ready, e + 1)
                dve.tensor_tensor(w2l[b], w2s[b], w2h[b].bitcast(F32), S_).then_inc(w2_split, 1)

            def hidden(e):
                dve.wait_ge(silu_e, e + 1)
                dve.wait_ge(b_filled, e + 1)
                dve.tensor_tensor(he, sil, psum[:, 1, :], M_).then_inc(he_ready, 1)

            def save_y(b, e):
                dve.wait_ge(idxs_copied, e + 1)
                dve.wait_ge(y_filled, e + 1)
                dve.tensor_scalar(ye[b][:, 512:D], psum[:, 6, :], idx[:, 2 + b, 1:2].bitcast(F32), None, M_).then_inc(y_saved_v, 1)

            dve.sem_inc(y_saved_v, 1)
            hidden(0)
            rest_w2(0, 0)
            with dve.Fori(0, NE // 2 - 1) as it:
                for b in (1, 0):
                    e = 2 * it + (2 - b)
                    save_heT(e - 1)
                    hidden(e)
                    save_y(1 - b, e - 1)
                    rest_w2(b, e)
            save_heT(NE - 2)
            hidden(NE - 1)
            rest_w2(1, NE - 1)
            save_y(0, NE - 2)
            save_heT(NE - 1)
            save_y(1, NE - 1)
            n_ov = dve.value_load(ovi[0:1, 0, OVF + 1:OVF + 2], min_val=0, max_val=OVF)
            with dve.Fori(0, OVF // 2) as it:
                for b in range(2):
                    with dve.If(n_ov > 2 * it + b):
                        e = 2 * it + (NE + b)
                        rest_w2(b, e)
                        hidden(e)
                        save_heT(e)
                        save_y(b, e)

        @block.tensor
        def _(pe):
            def lo(n):
                if n >= 4:
                    pe.wait_ge(lo_drained, n - 3)
                return psum[:, n % 4, :]

            def hi(r):
                if r >= 1:
                    pe.wait_ge(hi_drained, r)

            pe.wait_ge(consts_made, 1)
            def project(n, half, c0):
                bank = lo(n)
                pe.wait_ge(lo_drained, F_XT(4 * half + 3, 1) + 1)
                for c in range(KC):
                    last = pe.matmul(bank, win[:, c, c0:c0 + P], hT[:, c, 4 * half:4 * half + 4, :].rearrange("p i j -> p (i j)"),
                                     start=(c == 0), stop=(c == KC - 1))
                last.then_inc(lo_filled, 1)

            def turn_x(half):
                for i in range(4 * half, 4 * half + 4):
                    pe.wait_ge(x_normed, i + 1)
                    for k in range(2):
                        bank = lo(F_XT(i, k))
                        for c in range(4):
                            last = pe.transpose(bank[:, c * P:(c + 1) * P], xin[i // 2][:, i % 2, (4 * k + c) * P:(4 * k + c + 1) * P], ident[:, :])
                        last.then_inc(lo_filled, 1)
            for half in range(2):
                turn_x(half)
                pe.wait_ge(win_ag_scaled, 1)
                for m in range(2):
                    project(F_AG(half, 2 * m), half, G0 + m * P)
                    project(F_AG(half, 2 * m + 1), half, A0 + m * P)
            pe.wait_ge(ssm_par_in, 16 * 11)
            hi(R_C)
            for k in range(2):
                last = pe.transpose(psum[:, 4, k * P:(k + 1) * P], C2[:, k, :], ident[:, :])
            last.then_inc(hi_filled, 1)
            pe.wait_ge(ssm_w_ready, 1)
            hi(R_W)
            for k in range(2):
                for r in range(NPAIR):
                    last = pe.transpose(psum[:, 4 + 2 * k + r // 4, (r % 4) * P:(r % 4 + 1) * P],
                                        W[:, k, r].rearrange("p t c -> p (t c)"), ident[:, :])
            last.then_inc(hi_filled, 1)
            pe.wait_ge(win_scaled, 1)
            for i in range(NT):
                bank = lo(F_U(i))
                for c in range(KC):
                    last = pe.matmul(bank[:, 0:RD + SW], hT[:, c, i, :], win[:, c, KPE0:A0], start=(c == 0), stop=(c == KC - 1))
                last.then_inc(lo_filled, 1)
            pe.wait_ge(ssm_c_ready, 1)
            hi(R_H)
            for r in range(NPAIR):
                o = psum[0:2 * C, 4 + r // 4, (r % 4) * P:(r % 4 + 1) * P]
                for k in range(2):
                    last = pe.matmul(o, Bz[:, k, r].rearrange("p h c -> p (h c)"),
                                     CL[:, k, r, 0:STEP, :].rearrange("p t c -> p (t c)"), start=(k == 0), stop=(k == 1))
            last.then_inc(hi_filled, 1)
            hi(R_U)
            pe.wait_ge(lo_drained, F_U(NT - 1) + 1)
            for g in range(G):
                last = pe.transpose(psum[:, 4 + g // 4, (g % 4) * P:(g % 4 + 1) * P], utok[:, g].rearrange("p t c -> p (t c)"), ident[:, :])
            last.then_inc(hi_filled, 1)
            for half in range(2):
                for m, c0 in enumerate((CQ0, CQ0 + P, CKV0)):
                    project(F_LAT(half, m), half, c0)
            hi(R_V)
            for k in range(2):
                for r in range(NPAIR):
                    for h in range(2):
                        last = pe.matmul(psum[h * S:(h + 1) * S, 4 + 2 * k + r // 4, (r % 4) * P:(r % 4 + 1) * P],
                                         WT[:, k, r, h * S:(h + 1) * S], U[:, 2 * r + h, :], start=True, stop=True)
            last.then_inc(hi_filled, 1)
            pe.wait_ge(lat_squared, 1)
            bank = lo(F_SSQ)
            for i in range(NT):
                for m in range(2):
                    pe.matmul(bank[:, i:i + 1], sqc[:, m, i * P:(i + 1) * P], ones[:, 0:1], start=(m == 0), stop=(m == 1))
                last = pe.matmul(bank[:, NT + i:NT + i + 1], sqc[:, 2, i * P:(i + 1) * P], ones[:, 0:1], start=True, stop=True)
            last.then_inc(lo_filled, 1)
            pe.wait_ge(wproj_scaled, 1)

            def project_qkv(i):
                for k in range(2):
                    bank = lo(F_QKV(i, k))
                    for m in range(2):
                        last = pe.matmul(bank[:, 0:384], cqT[:, m, i * P:(i + 1) * P], wuq[:, m, k * 384:(k + 1) * 384],
                                         start=(m == 0), stop=(m == 1))
                    last.then_inc(lo_filled, 1)
                for k in range(2):
                    pe.matmul(lo(F_QKV(i, 2 + k)), ckvT[:, i * P:(i + 1) * P], wukv[:, k * 512:(k + 1) * 512],
                              start=True, stop=True).then_inc(lo_filled, 1)
            def turn(src, r):
                hi(r)
                for i in range(NT):
                    for c in range(2):
                        last = pe.transpose(psum[:, 4 + i // 2, (i % 2) * 256 + c * P:(i % 2) * 256 + (c + 1) * P], src(i, c), ident[:, :])
                last.then_inc(hi_filled, 1)

            pe.wait_ge(conv_done, 1)
            turn(lambda i, c: cperm[:, c, i, :], R_CONV)
            for i in range(5):
                project_qkv(i)
            pe.wait_ge(toep_in, 16 * 2 * STEP)
            pe.wait_ge(ssm_x_ready, 1)
            hi(R_Y)
            for h in range(2):
                for r in range(NPAIR):
                    o = psum[:, 4 + 2 * h + r // 4, (r % 4) * P:(r % 4 + 1) * P]
                    pe.matmul(o, U[:, 2 * r + h, :], toep[:, 2 * r + h, :], start=True, stop=False)
                    for k in range(2):
                        last = pe.matmul(o, Xp[h * S:(h + 1) * S, k, r, :],
                                         CL[h * S:(h + 1) * S, k, r, 1:STEP + 1, :].rearrange("p t c -> p (t c)"),
                                         start=False, stop=(k == 1))
            last.then_inc(hi_filled, 1)

            for i in range(5, NT):
                project_qkv(i)
            pe.wait_ge(z_ready, 1)
            turn(lambda i, c: yssm[:, i, c * P:(c + 1) * P], R_Z)
            hi(R_GLU)
            for i in range(NT):
                for c in range(2):
                    last = pe.matmul(psum[:, 4 + i // 2, (i % 2) * 256:(i % 2 + 1) * 256], zT[:, c, i * P:(i + 1) * P], wglu[:, c, :],
                                     start=(c == 0), stop=(c == 1))
            last.then_inc(hi_filled, 1)
            pe.wait_ge(mid_scaled, 1)
            turn(lambda i, c: ctok[:, i, c * P:(c + 1) * P], R_COUT)
            pe.wait_ge(mid_scaled, 2)
            turn(lambda i, c: sout[:, i, c * P:(c + 1) * P], R_SOUT)

            pe.wait_ge(mid_done, 1)
            with pe.Fori(0, H // 2) as it:
                it16, itF = pe.snap(STEPS * it), pe.snap(FILLS * it)
                ita, itv = pe.snap(saved_a[FILLS] * it), pe.snap(saved_v[FILLS] * it)
                for b in range(2):
                    pe.wait_ge(heads_made, 2 * it + (b + 1))
                    for a, buf in enumerate((qn[b], kn[b])):
                        for i in range(NT):
                            last = pe.transpose(psum[0:QH, 4 * b + 2 * a + i // 4, (i % 4) * P:(i % 4 + 1) * P], buf[:, i, :], ident[:, :])
                    last.then_inc(qkT_made, 1)

                def scores(n):
                    b, i = n // NT, tile_of[n]
                    if n % NT == 0:
                        pe.wait_ge(qT_saved, 2 * it + (b + 1))
                        pe.wait_ge(kT_saved, 2 * it + (b + 1))
                    if n >= 2:
                        pe.wait_ge(p_ready, it16 + (n - 1))
                    L = (i + 1) * P
                    for k in range((L + 511) // 512):
                        w = min(512, L - 512 * k)
                        last = pe.matmul(psum[:, 2 * (n % 2) + k, 0:w], qT[b][0:QH, i * P:(i + 1) * P], kT[b][0:QH, 512 * k:512 * k + w],
                                         start=True, stop=True)
                    last.then_inc(s_filled, 1)

                def saved(f, n):
                    pe.wait_ge(pT_saved_a, ita + saved_a[f + 1])
                    if saved_v[f + 1]:
                        pe.wait_ge(pT_saved_v, itv + saved_v[f + 1])

                def turn_probs(n):
                    pe.wait_ge(p_ready, it16 + (n + 1))
                    for f in range(first_fill[n], first_fill[n + 1]):
                        if f < 2:
                            pe.wait_ge(qT_saved, 2 * it + 2)
                        else:
                            saved(f - 2, n)
                        j0 = 4 * (f - first_fill[n])
                        for j in range(j0, min(j0 + 4, tile_of[n] + 1)):
                            last = pe.transpose(psum[:, 4 + f % 2, (j - j0) * P:(j - j0 + 1) * P], prob[n % 2][:, j * P:(j + 1) * P], ident[:, :])
                        last.then_inc(pT_filled, 1)

                def values(n):
                    i = tile_of[n]
                    if n < 2:
                        pe.wait_ge(kT_saved, 2 * it + 2)
                    else:
                        pe.wait_ge(o_saved, it16 + (n - 1))
                    for f in range(first_fill[n], first_fill[n + 1]):
                        saved(f, n)
                        j0 = 4 * (f - first_fill[n])
                        for j in range(j0, min(j0 + 4, i + 1)):
                            last = pe.matmul(psum[:, 6 + n % 2, 0:VD], probT[f % 4][:, j - j0, :],
                                             vtok[:, j, bass.ds((2 * it + n // NT) * VD, VD)], start=(j == 0), stop=(j == i))
                        last.then_inc(pv_done, 1)

                scores(0)
                scores(1)
                for n in range(STEPS):
                    turn_probs(n)
                    if n + 2 < STEPS:
                        scores(n + 2)
                    if n >= 1:
                        values(n - 1)
                values(STEPS - 1)
                pe.wait_ge(o_saved, it16 + STEPS)

            for i in range(NT):
                pe.wait_ge(o_scaled, i + 1)
                if i >= 4:
                    pe.wait_ge(oT_saved, i - 3)
                for c in range(4):
                    last = pe.transpose(psum[:, i % 4, c * P:(c + 1) * P], otok[:, i, c * P:(c + 1) * P], ident[:, :])
                last.then_inc(oT_filled, 1)
            pe.wait_ge(oT_saved, NT)
            pe.wait_ge(wout_scaled, 1)

            def logits(i):
                pe.wait_ge(h2T_saved, i + 1)
                if i >= 2:
                    pe.wait_ge(lg_saved, i - 1)
                for c in range(KC):
                    last = pe.matmul(psum[:, 6 + i % 2, 0:EG + NE], h2T[:, c, :], wr[:, c, :], start=(c == 0), stop=(c == KC - 1))
                last.then_inc(lg_filled, 1)

            def ranks(part):
                i0, i1 = ROUTE[part]
                pe.wait_ge(picks_ready, part + 1)
                o = psum[:, 2 * part, 0:(i1 - i0) * NE]
                pe.matmul(o, before[:, :], both[:, i0:i1].rearrange("p t e -> p (t e)"), start=True, stop=False)
                last = pe.matmul(o, ones[:, :], prior[:, i0:i1].rearrange("p t e -> p (t e)"), start=False, stop=True)
                if part == 1:
                    last = pe.matmul(psum[:, 3, 0:NE], ones[:, :], prior[:, NT, :], start=True, stop=True)
                last.then_inc(ranks_filled, 1)

            def turn_h2(i):
                pe.wait_ge(h2_ready, i + 1)
                if i >= 1:
                    pe.wait_ge(h2T_saved, i)
                for c in range(KC):
                    last = pe.transpose(psum[:, 4 + c // 4, (c % 4) * P:(c % 4 + 1) * P], h2[i % 2][:, c * P:(c + 1) * P], ident[:, :])
                last.then_inc(h2T_filled, 1)

            for i in range(NT):
                if i >= 2:
                    pe.wait_ge(x2_ready, i - 1)
                for k in range(2):
                    for c in range(KC):
                        y_ = oT[:, c, i, :] if c < 4 else yT[:, c - 4, i, :]
                        last = pe.matmul(psum[:, 2 * (i % 2) + k, :], y_, wout[:, c, 512 * k:512 * (k + 1)],
                                         start=(c == 0), stop=(c == KC - 1))
                    if i >= 1 and k == 0:
                        turn_h2(i - 1)
                last.then_inc(out_filled, 1)
                if i == NT - 1:
                    pe.wait_ge(x2_ready, NT - 1)
                    ranks(0)
                if i >= 1:
                    logits(i - 1)
            turn_h2(NT - 1)
            logits(NT - 1)
            ranks(1)

            def turn_rows(b, e, gathers):
                pe.wait_ge(ROWS_IN[b], gathers)
                for c in range(KC):
                    last = pe.transpose(psum[:, 3 + c // 4, (c % 4) * P:(c % 4 + 1) * P], xg[b][:, c * P:(c + 1) * P], ident[:, :])
                last.then_inc(xgT_filled, 1)

            def up(k, b, e):
                for c in range(KC):
                    last = pe.matmul(psum[:, k, :], xgT[:, c, :], w13[b][k][:, c, :], start=(c == 0), stop=(c == KC - 1))
                last.then_inc((a_filled, b_filled)[k], 1)

            def turn_hidden(e):
                pe.wait_ge(he_ready, e + 1)
                for c in range(FC):
                    last = pe.transpose(psum[:, 2, c * P:(c + 1) * P], he[:, c * P:(c + 1) * P], ident[:, :])
                last.then_inc(heT_filled, 1)

            def down(b, e):
                pe.wait_ge(heT_saved, e + 1)
                pe.wait_ge(w2_split, e + 1)
                pe.wait_ge(y_saved_a, e + 1)
                pe.wait_ge(y_saved_v, e + 1)
                parts = ((heTh, w2h[b]), (heTl, w2h[b]), (heTh, w2l[b]))
                for k in range(2):
                    for c in range(FC):
                        for n, (h_, w_) in enumerate(parts):
                            last = pe.matmul(psum[:, 5 + k, :], h_[:, c, :], w_[:, c, 512 * k:512 * (k + 1)],
                                             start=(c == 0 and n == 0), stop=(c == FC - 1 and n == 2))
                last.then_inc(y_filled, 1)

            pe.wait_ge(ov_table, 1)
            turn_rows(0, 0, 16)
            pe.wait_ge(xgT_saved, 1)
            pe.wait_ge(W13_IN[0], 32)
            up(0, 0, 0)
            up(1, 0, 0)
            turn_rows(1, 1, 16)
            with pe.Fori(0, NE // 2 - 1) as it:
                for b in (1, 0):
                    e = 2 * it + (2 - b)
                    pe.wait_ge(xgT_saved, e + 1)
                    pe.wait_ge(W13_IN[b], 32 * it + 32 * (2 - b))
                    pe.wait_ge(silu_e, e)
                    up(0, b, e)
                    turn_hidden(e - 1)
                    up(1, b, e)
                    turn_rows(1 - b, e + 1, 16 * it + 32)
                    down(1 - b, e - 1)
            pe.wait_ge(xgT_saved, NE)
            pe.wait_ge(W13_IN[1], 16 * NE)
            pe.wait_ge(silu_e, NE - 1)
            up(0, 1, NE - 1)
            turn_hidden(NE - 2)
            up(1, 1, NE - 1)
            down(0, NE - 2)
            turn_hidden(NE - 1)
            down(1, NE - 1)
            n_ov = pe.value_load(ovi[0:1, 0, OVF + 1:OVF + 2], min_val=0, max_val=OVF)
            with pe.Fori(0, OVF // 2) as it:
                for b in range(2):
                    with pe.If(n_ov > 2 * it + b):
                        e = 2 * it + (NE + b)
                        turn_rows(b, e, 16 * it + 16 * (NE // 2 + 1))
                        pe.wait_ge(xgT_saved, e + 1)
                        pe.wait_ge(OV_W_IN[b], 32 * it + 32)
                        up(0, b, e)
                        up(1, b, e)
                        turn_hidden(e)
                        down(b, e)


_INS = ["x", "positions", "mix_norm", "w_in", "q_a_norm", "w_uq", "kv_a_norm", "w_ukv", "q_norm", "k_norm",
        "ssm_lam_re", "ssm_lam_im", "ssm_b_re", "ssm_b_im", "ssm_c_re", "ssm_c_im", "ssm_d", "ssm_log_dt", "ssm_w_glu",
        "conv_dw_w", "conv_dw_b", "conv_ln_w", "conv_ln_b", "out_norm", "w_out",
        "ffn_norm", "w_grp", "b_grp", "w_exp", "b_exp", "w1", "w3", "w2"]


def kernel(**inputs):
    import numpy as _np
    import concourse.bacc as _bacc
    from concourse import mybir as _mybir
    from concourse.bass_utils import run_bass_kernel_spmd as _run

    nc = _bacc.Bacc("TRN2", target_bir_lowering=False, num_devices=1)
    arrays, args = {}, []
    for name in _INS:
        a = _np.ascontiguousarray(inputs[name])
        arrays[f"in_{name}"] = a
        args.append(nc.dram_tensor(f"in_{name}", a.shape, _mybir.dt.from_np(a.dtype), kind="ExternalInput").ap())
    x = arrays["in_x"]
    out = nc.dram_tensor("out_0", x.shape, _mybir.dt.float32, kind="ExternalOutput").ap()
    build(nc, *args, out)
    r = _run(nc, [arrays], core_ids=[0])
    return r.results[0]["out_0"]
```
